# Optimizing a Trainium2 kernel written in Bass

```python
import math
import jax
import jax.numpy as jnp
from jax import lax
import numpy as np

D_MODEL = 1024
BATCH = 1
SEQ = 1024
DEPTH = 1

HEAD_DIM = 64
N_MIXERS = 4
HEADS = D_MODEL // (N_MIXERS * HEAD_DIM)
GROUP_WIDTH = HEADS * HEAD_DIM
Q_BLOCK = 128
NEG_INF = -1e30

DIFF_DK = HEAD_DIM // 2
SWA_WINDOW = 128
SWA_KV_HEADS = 2
CMP_BLOCK = 32
CMP_STRIDE = 16
CMP_HIDDEN = 2 * HEAD_DIM
SEL_BLOCK = 64
SEL_TOPK = 16
NSA_WINDOW = 512
FORCE_SCORE = 1e4

N_EXPERTS = 64
N_EXPERT_GROUPS = 8
EXPERTS_PER_GROUP = N_EXPERTS // N_EXPERT_GROUPS
TOP_K = 2
D_EXPERT = D_MODEL // 2
ROW_BLOCK = 128

KV_WIDTH = SWA_KV_HEADS * HEAD_DIM
IN_SPLITS = (
    GROUP_WIDTH, GROUP_WIDTH, GROUP_WIDTH,
    GROUP_WIDTH, KV_WIDTH, KV_WIDTH,
    GROUP_WIDTH, GROUP_WIDTH, GROUP_WIDTH, HEADS,
    GROUP_WIDTH, HEAD_DIM, HEAD_DIM, HEAD_DIM, HEAD_DIM,
    HEAD_DIM, HEAD_DIM, 3 * HEADS,
)
IN_COLS = sum(IN_SPLITS)

kernel_name = 'hybrid_parallel_heads_moe_block'

def rms_norm(x, g, eps=1e-6):
    xf = x.astype(jnp.float32)
    y = xf * lax.rsqrt(jnp.mean(xf * xf, axis=-1, keepdims=True) + eps)
    return (y * g.astype(jnp.float32)).astype(x.dtype)

def split_heads(t, n_heads):
    b, s, _ = t.shape
    return t.reshape(b, s, n_heads, -1).transpose(0, 2, 1, 3)

def split_cols(p, widths):
    offs = np.cumsum((0,) + tuple(widths))
    return [p[..., int(offs[i]):int(offs[i + 1])] for i in range(len(widths))]

def alibi_slopes():
    n = 3 * HEADS
    m = 2.0 ** (-8.0 * np.arange(1, n + 1) / n)
    return jnp.asarray(m.reshape(HEADS, 3).T, dtype=jnp.float32)

def banded_blocks(t, n_prev):
    b, h, s, d = t.shape
    nb = s // Q_BLOCK
    tb = jnp.pad(t.reshape(b, h, nb, Q_BLOCK, d), ((0, 0), (0, 0), (n_prev, 0), (0, 0), (0, 0)))
    return jnp.concatenate([tb[:, :, j:j + nb] for j in range(n_prev + 1)], axis=3)

def band_geometry(nb, n_prev):
    blk = jnp.arange(nb)[:, None]
    qpos = blk * Q_BLOCK + jnp.arange(Q_BLOCK)[None, :]
    kpos = (blk - n_prev) * Q_BLOCK + jnp.arange((n_prev + 1) * Q_BLOCK)[None, :]
    dist = qpos[:, :, None] - kpos[:, None, :]
    return dist, (kpos >= 0)[:, None, :]

def diff_attention(q, k, v, lam_q1, lam_k1, lam_q2, lam_k2, subln_g, slopes, layer_idx):
    f32 = jnp.float32
    b, s, _ = q.shape
    nb = s // Q_BLOCK
    lam_init = 0.8 - 0.6 * math.exp(-0.3 * layer_idx)
    lam = (jnp.exp(jnp.sum(lam_q1.astype(f32) * lam_k1.astype(f32)))
           - jnp.exp(jnp.sum(lam_q2.astype(f32) * lam_k2.astype(f32))) + lam_init)
    q = q.astype(f32).reshape(b, nb, Q_BLOCK, HEADS, 2, DIFF_DK) * DIFF_DK ** -0.5
    qb = q.transpose(1, 0, 3, 4, 2, 5)
    kt = k.astype(f32).reshape(b, s, HEADS, 2, DIFF_DK).transpose(0, 2, 3, 1, 4)
    vt = split_heads(v.astype(f32), HEADS)
    kpos = jnp.arange(s)
    m = slopes[None, :, None, None, None]

    def block(args):
        qi, i = args
        tpos = i * Q_BLOCK + jnp.arange(Q_BLOCK)
        dist = (tpos[:, None] - kpos[None, :]).astype(f32)
        sc = jnp.einsum('bhmqd,bhmkd->bhmqk', qi, kt) - m * dist
        a = jax.nn.softmax(jnp.where(dist >= 0, sc, NEG_INF), axis=-1)
        w = a[:, :, 0] - lam * a[:, :, 1]
        return jnp.einsum('bhqk,bhkd->bhqd', w, vt)

    o = lax.map(block, (qb, jnp.arange(nb)))
    o = rms_norm(o, subln_g) * (1.0 - lam_init)
    return o.transpose(1, 0, 3, 2, 4).reshape(b, s, GROUP_WIDTH)

def swa_sink_attention(q, k, v, sinks, slopes):
    f32 = jnp.float32
    b, s, _ = q.shape
    nb = s // Q_BLOCK
    g = HEADS // SWA_KV_HEADS
    n_prev = SWA_WINDOW // Q_BLOCK
    q = q.astype(f32).reshape(b, nb, Q_BLOCK, SWA_KV_HEADS, g, HEAD_DIM).transpose(0, 3, 4, 1, 2, 5)
    q = q * HEAD_DIM ** -0.5
    kb = banded_blocks(split_heads(k.astype(f32), SWA_KV_HEADS), n_prev)
    vb = banded_blocks(split_heads(v.astype(f32), SWA_KV_HEADS), n_prev)
    dist, kvalid = band_geometry(nb, n_prev)
    valid = kvalid & (dist >= 0) & (dist < SWA_WINDOW)
    m = slopes.reshape(SWA_KV_HEADS, g)[None, :, :, None, None, None]
    sc = jnp.einsum('bcgnqd,bcnkd->bcgnqk', q, kb) - m * dist.astype(f32)
    sc = jnp.where(valid, sc, NEG_INF)
    sink = jnp.broadcast_to(sinks.astype(f32).reshape(SWA_KV_HEADS, g)[None, :, :, None, None, None],
                            sc.shape[:-1] + (1,))
    p = jax.nn.softmax(jnp.concatenate([sc, sink], axis=-1), axis=-1)[..., :-1]
    o = jnp.einsum('bcgnqk,bcnkd->bcgnqd', p, vb)
    return o.transpose(0, 3, 4, 1, 2, 5).reshape(b, s, GROUP_WIDTH)

def forgetting_attention(q, k, v, f_logit, b_f):
    f32 = jnp.float32
    b, s, _ = q.shape
    nb = s // Q_BLOCK
    q = split_heads(q.astype(f32), HEADS) * HEAD_DIM ** -0.5
    k = split_heads(k.astype(f32), HEADS)
    v = split_heads(v.astype(f32), HEADS)
    cum = jnp.cumsum(jax.nn.log_sigmoid(f_logit.astype(f32) + b_f.astype(f32)), axis=1)
    cum = cum.transpose(0, 2, 1)
    qb = q.reshape(b, HEADS, nb, Q_BLOCK, HEAD_DIM).transpose(2, 0, 1, 3, 4)
    cb = cum.reshape(b, HEADS, nb, Q_BLOCK).transpose(2, 0, 1, 3)
    kpos = jnp.arange(s)

    def block(args):
        qi, ci, i = args
        tpos = i * Q_BLOCK + jnp.arange(Q_BLOCK)
        sc = jnp.einsum('bhqd,bhkd->bhqk', qi, k) + ci[..., None] - cum[:, :, None, :]
        sc = jnp.where(tpos[:, None] >= kpos[None, :], sc, NEG_INF)
        return jnp.einsum('bhqk,bhkd->bhqd', jax.nn.softmax(sc, axis=-1), v)

    o = lax.map(block, (qb, cb, jnp.arange(nb)))
    return o.transpose(1, 0, 3, 2, 4).reshape(b, s, GROUP_WIDTH)

def compress(t, pos, w1, b1, w2):
    f32 = jnp.float32
    b, s, d = t.shape
    n_cmp = (s - CMP_BLOCK) // CMP_STRIDE + 1
    idx = np.arange(n_cmp)[:, None] * CMP_STRIDE + np.arange(CMP_BLOCK)[None, :]
    blocks = (t[:, idx] + pos.astype(f32)).reshape(b, n_cmp, CMP_BLOCK * d)
    hid = jax.nn.gelu(blocks @ w1.astype(f32) + b1.astype(f32))
    return hid @ w2.astype(f32)

def nsa_attention(q, k_cmp, v_cmp, k_sel, v_sel, k_win, v_win, gate_logit,
                  cmp_pos, cmp_w1, cmp_b1, cmp_w2, slopes):
    f32 = jnp.float32
    b, s, _ = q.shape
    nb = s // Q_BLOCK
    q = split_heads(q.astype(f32), HEADS) * HEAD_DIM ** -0.5
    qb = q.reshape(b, HEADS, nb, Q_BLOCK, HEAD_DIM).transpose(2, 0, 1, 3, 4)
    kc = compress(k_cmp.astype(f32), cmp_pos[0], cmp_w1[0], cmp_b1[0], cmp_w2[0])
    vc = compress(v_cmp.astype(f32), cmp_pos[1], cmp_w1[1], cmp_b1[1], cmp_w2[1])
    n_cmp = kc.shape[1]
    cmp_start = jnp.arange(n_cmp) * CMP_STRIDE
    cmp_end = cmp_start + CMP_BLOCK - 1
    n_sel = s // SEL_BLOCK
    n_top = min(SEL_TOPK, n_sel)
    sel_start = jnp.arange(n_sel) * SEL_BLOCK
    cover = jnp.clip(jnp.minimum(cmp_start[:, None] + CMP_BLOCK, sel_start[None, :] + SEL_BLOCK)
                     - jnp.maximum(cmp_start[:, None], sel_start[None, :]), 0).astype(f32) / CMP_BLOCK
    ks_blocks = k_sel.astype(f32).reshape(b, n_sel, SEL_BLOCK, HEAD_DIM)
    vs_blocks = v_sel.astype(f32).reshape(b, n_sel, SEL_BLOCK, HEAD_DIM)
    kw_pad = jnp.pad(k_win.astype(f32), ((0, 0), (NSA_WINDOW, 0), (0, 0)))
    vw_pad = jnp.pad(v_win.astype(f32), ((0, 0), (NSA_WINDOW, 0), (0, 0)))
    n_win_keys = NSA_WINDOW + Q_BLOCK
    m = slopes[None, :, None, None]
    gather_blocks = jax.vmap(lambda kb, ib: kb[ib])

    def block(args):
        qi, i = args
        t0 = i * Q_BLOCK
        tpos = t0 + jnp.arange(Q_BLOCK)
        dc = (tpos[:, None] - cmp_end[None, :]).astype(f32)
        cvalid = dc >= 0
        sc = jnp.einsum('bhqd,bnd->bhqn', qi, kc) - m * dc
        pc = jax.nn.softmax(jnp.where(cvalid, sc, NEG_INF), axis=-1) * cvalid
        o_cmp = jnp.einsum('bhqn,bnd->bhqd', pc, vc)
        imp = jnp.einsum('bhqn,nj->bqj', pc, cover)
        cur = (tpos // SEL_BLOCK)[:, None]
        blk = jnp.arange(n_sel)[None, :]
        forced = (blk == 0) | (blk == cur) | (blk == cur - 1)
        score = jnp.where(forced, FORCE_SCORE, jnp.where(blk <= cur, imp, -1.0))
        _, idx = lax.top_k(score, n_top)
        kg = gather_blocks(ks_blocks, idx).reshape(b, Q_BLOCK, n_top * SEL_BLOCK, HEAD_DIM)
        vg = gather_blocks(vs_blocks, idx).reshape(b, Q_BLOCK, n_top * SEL_BLOCK, HEAD_DIM)
        kp = (idx[..., None] * SEL_BLOCK + jnp.arange(SEL_BLOCK)).reshape(b, Q_BLOCK, -1)
        ds = (tpos[None, :, None] - kp).astype(f32)[:, None]
        ss = jnp.einsum('bhqd,bqkd->bhqk', qi, kg) - m * ds
        o_sel = jnp.einsum('bhqk,bqkd->bhqd',
                           jax.nn.softmax(jnp.where(ds >= 0, ss, NEG_INF), axis=-1), vg)
        kw = lax.dynamic_slice_in_dim(kw_pad, t0, n_win_keys, axis=1)
        vw = lax.dynamic_slice_in_dim(vw_pad, t0, n_win_keys, axis=1)
        wpos = t0 - NSA_WINDOW + jnp.arange(n_win_keys)
        dw = tpos[:, None] - wpos[None, :]
        wvalid = (wpos[None, :] >= 0) & (dw >= 0) & (dw < NSA_WINDOW)
        sw = jnp.einsum('bhqd,bkd->bhqk', qi, kw) - m * dw.astype(f32)
        o_win = jnp.einsum('bhqk,bkd->bhqd',
                           jax.nn.softmax(jnp.where(wvalid, sw, NEG_INF), axis=-1), vw)
        return jnp.stack([o_cmp, o_sel, o_win], axis=-1)

    o = lax.map(block, (qb, jnp.arange(nb)))
    g = jax.nn.sigmoid(gate_logit.astype(f32)).reshape(b, nb, Q_BLOCK, HEADS, 3)
    o = jnp.einsum('nbhqdr,bnqhr->bnqhd', o, g)
    return o.reshape(b, s, GROUP_WIDTH)

def moe_ffn(h, router_w, router_b, w_gate, w_up, w_down):
    f32 = jnp.float32
    b, s, d = h.shape
    t = b * s
    hf = h.reshape(t, d)
    aff = jax.nn.sigmoid(hf.astype(f32) @ router_w.astype(f32))
    sel = aff + router_b.astype(f32)
    grp_top = lax.top_k(sel.reshape(t, N_EXPERT_GROUPS, EXPERTS_PER_GROUP), TOP_K)[0]
    grp = jnp.argmax(jnp.sum(grp_top, axis=-1), axis=-1)
    in_grp = (jnp.arange(N_EXPERTS) // EXPERTS_PER_GROUP)[None, :] == grp[:, None]
    _, e_idx = lax.top_k(jnp.where(in_grp, sel, NEG_INF), TOP_K)
    gate = jnp.take_along_axis(aff, e_idx, axis=-1)
    gate = gate / jnp.sum(gate, axis=-1, keepdims=True)
    n_assign = t * TOP_K
    e_flat = e_idx.reshape(n_assign)
    tok = jnp.repeat(jnp.arange(t), TOP_K)
    order = jnp.argsort(e_flat)
    e_sorted = e_flat[order]
    counts = jnp.bincount(e_flat, length=N_EXPERTS)
    padded = (counts + ROW_BLOCK - 1) // ROW_BLOCK * ROW_BLOCK
    pend = jnp.cumsum(padded)
    rank = jnp.arange(n_assign) - (jnp.cumsum(counts) - counts)[e_sorted]
    dest = (pend - padded)[e_sorted] + rank
    n_blocks = (n_assign + N_EXPERTS * (ROW_BLOCK - 1) + ROW_BLOCK - 1) // ROW_BLOCK
    n_rows = n_blocks * ROW_BLOCK
    row_tok = jnp.full((n_rows,), t, jnp.int32).at[dest].set(tok[order])
    row_gate = jnp.zeros((n_rows,), f32).at[dest].set(gate.reshape(n_assign)[order])
    blk_expert = jnp.minimum(jnp.searchsorted(pend, jnp.arange(n_blocks) * ROW_BLOCK, side='right'),
                             N_EXPERTS - 1)
    rows = jnp.concatenate([hf, jnp.zeros((1, d), hf.dtype)], axis=0)[row_tok]
    rows = rows.reshape(n_blocks, ROW_BLOCK, d)

    def expert_rows(args):
        xb, e = args
        return (jax.nn.silu(xb @ w_gate[e]) * (xb @ w_up[e])) @ w_down[e]

    out = lax.map(expert_rows, (rows, blk_expert)).reshape(n_rows, d)
    y = jnp.zeros((t + 1, d), f32).at[row_tok].add(out.astype(f32) * row_gate[:, None])
    return y[:t].reshape(b, s, d).astype(h.dtype)

def setup_inputs(seed: int = 0) -> dict:
    key = jax.random.key(seed)
    ks = jax.random.split(key, 25)
    f32 = jnp.float32

    def nrm(k, shape, scale):
        return scale * jax.random.normal(k, shape, f32)

    d = D_MODEL
    d_mix = N_MIXERS * GROUP_WIDTH
    return {
        'x': nrm(ks[0], (BATCH, SEQ, d), 1.0),
        'c': nrm(ks[1], (BATCH, d), 1.0),
        'ada_w': nrm(ks[2], (DEPTH, d, 6 * d), 0.5 * d ** -0.5),
        'ada_b': nrm(ks[3], (DEPTH, 6 * d), 0.02),
        'norm_attn_g': 1.0 + nrm(ks[4], (DEPTH, d), 0.05),
        'norm_moe_g': 1.0 + nrm(ks[5], (DEPTH, d), 0.05),
        'norm_final_g': 1.0 + nrm(ks[6], (d,), 0.05),
        'w_in': nrm(ks[7], (DEPTH, d, IN_COLS), d ** -0.5),
        'w_out': nrm(ks[8], (DEPTH, d_mix, d), d_mix ** -0.5),
        'diff_lam_q1': nrm(ks[9], (DEPTH, DIFF_DK), 0.1),
        'diff_lam_k1': nrm(ks[10], (DEPTH, DIFF_DK), 0.1),
        'diff_lam_q2': nrm(ks[11], (DEPTH, DIFF_DK), 0.1),
        'diff_lam_k2': nrm(ks[12], (DEPTH, DIFF_DK), 0.1),
        'diff_subln_g': 1.0 + nrm(ks[13], (DEPTH, HEAD_DIM), 0.05),
        'swa_sinks': nrm(ks[14], (DEPTH, HEADS), 0.5),
        'fox_forget_b': 2.0 + nrm(ks[15], (DEPTH, HEADS), 0.1),
        'nsa_cmp_pos': nrm(ks[16], (DEPTH, 2, CMP_BLOCK, HEAD_DIM), 0.5),
        'nsa_cmp_w1': nrm(ks[17], (DEPTH, 2, CMP_BLOCK * HEAD_DIM, CMP_HIDDEN), (CMP_BLOCK * HEAD_DIM) ** -0.5),
        'nsa_cmp_b1': nrm(ks[18], (DEPTH, 2, CMP_HIDDEN), 0.02),
        'nsa_cmp_w2': nrm(ks[19], (DEPTH, 2, CMP_HIDDEN, HEAD_DIM), CMP_HIDDEN ** -0.5),
        'router_w': nrm(ks[20], (d, N_EXPERTS), d ** -0.5),
        'router_b': nrm(ks[21], (N_EXPERTS,), 0.01),
        'exp_w_gate': nrm(ks[22], (DEPTH, N_EXPERTS, d, D_EXPERT), d ** -0.5),
        'exp_w_up': nrm(ks[23], (DEPTH, N_EXPERTS, d, D_EXPERT), d ** -0.5),
        'exp_w_down': nrm(ks[24], (DEPTH, N_EXPERTS, D_EXPERT, d), D_EXPERT ** -0.5),
    }

def reference(x, c, ada_w, ada_b, norm_attn_g, norm_moe_g, norm_final_g, w_in, w_out,
              diff_lam_q1, diff_lam_k1, diff_lam_q2, diff_lam_k2, diff_subln_g,
              swa_sinks, fox_forget_b, nsa_cmp_pos, nsa_cmp_w1, nsa_cmp_b1, nsa_cmp_w2,
              router_w, router_b, exp_w_gate, exp_w_up, exp_w_down):
    slopes = alibi_slopes()
    cond = jax.nn.silu(c)
    for l in range(DEPTH):
        mod = (cond @ ada_w[l] + ada_b[l])[:, None, :]
        sh_a, sc_a, g_a, sh_m, sc_m, g_m = jnp.split(mod, 6, axis=-1)
        h = rms_norm(x, norm_attn_g[l]) * (1 + sc_a) + sh_a
        p = split_cols(h @ w_in[l], IN_SPLITS)
        ya = diff_attention(p[0], p[1], p[2], diff_lam_q1[l], diff_lam_k1[l], diff_lam_q2[l],
                            diff_lam_k2[l], diff_subln_g[l], slopes[0], l)
        yb = swa_sink_attention(p[3], p[4], p[5], swa_sinks[l], slopes[1])
        yc = forgetting_attention(p[6], p[7], p[8], p[9], fox_forget_b[l])
        yd = nsa_attention(p[10], p[11], p[12], p[13], p[14], p[15], p[16], p[17],
                           nsa_cmp_pos[l], nsa_cmp_w1[l], nsa_cmp_b1[l], nsa_cmp_w2[l], slopes[2])
        y = jnp.concatenate([ya, yb, yc, yd], axis=-1).astype(x.dtype) @ w_out[l]
        x = x + g_a * y
        h = rms_norm(x, norm_moe_g[l]) * (1 + sc_m) + sh_m
        x = x + g_m * moe_ffn(h, router_w, router_b, exp_w_gate[l], exp_w_up[l], exp_w_down[l])
    return rms_norm(x, norm_final_g)


_drawn_inputs = setup_inputs


def setup_inputs(seed=0):
    import zlib

    import numpy as np

    out = dict(_drawn_inputs(seed))
    spreads = {}
    factors = {'diff_lam_q1': 2.838,
     'diff_lam_k1': 3.571,
     'diff_lam_q2': 6.39,
     'diff_subln_g': 3.236,
     'swa_sinks': 21.65,
     'fox_forget_b': 64.0,
     'nsa_cmp_b1': 26.71}
    for name, (base, spread) in spreads.items():
        noise = np.random.default_rng([zlib.crc32(name.encode()), seed]).standard_normal(out[name].shape)
        drawn = base * np.exp(spread * noise) if base else spread * noise
        out[name] = jnp.asarray(drawn.astype(out[name].dtype))
    for name, factor in factors.items():
        out[name] = (out[name] * factor).astype(out[name].dtype)
    return out
```

```python
from contextlib import ExitStack

import concourse.bass as bass
from concourse import mybir

F32 = mybir.dt.float32
I32 = mybir.dt.int32
U32 = mybir.dt.uint32
ALU = mybir.AluOpType
ACT = mybir.ActivationFunctionType
AX_X = mybir.AxisListType.X
ds = bass.ds

P = 128
T = 1024
NT = T // P
D = 1024
DC = D // P
HD = 64
NH = 4
EPS = 1e-6
BIG = 1e32
HUGE = 3e38

C_DQ, C_DK, C_DV = 0, 256, 512
C_SQ, C_SK, C_SV = 768, 1024, 1152
C_FQ, C_FK, C_FV, C_FF = 1280, 1536, 1792, 2048
C_NQ, C_KC, C_KS, C_KW, C_VS, C_VW, C_G = 2052, 2308, 2436, 2500, 2564, 2628, 2692
IN_COLS = 2704
ROW_TILES = (
    [(c, 32 ** -0.5) for c in (0, 128)] + [(c, 1.0) for c in (256, 384)]
    + [(c, 0.125) for c in (768, 896)] + [(1024, 1.0)]
    + [(c, 0.125) for c in (1280, 1408)] + [(c, 1.0) for c in (1536, 1664)]
    + [(c, 0.125) for c in (2052, 2180)] + [(C_KC, 1.0), (C_KS, 1.0)]
)
TOKEN_RUNS = [[(C_DV, 256), (C_SV, 128)], [(C_FV, 260), (C_VS, 64), (C_VW, 76)]]
VA = 384
VW = 784
V_D, V_S, V_F, V_FF, V_KS, V_KW, V_G = 0, 256, 384, 640, 644, 708, 772

SL = 256
N_SL = 6 * D // SL
ADA_RING = 2
NC = 63
NE = 64
EB = 64
NOV = 31
ROWS = 6144
DF = 512
FC = DF // P
LAM_INIT = 0.2


def slope(mixer, head):
    return 2.0 ** (-8.0 * (3 * head + mixer + 1) / (3 * NH))


GROUPS = [
    dict(name="diff", rounds=4, k=32, prev=7, q=(C_DQ, 64, 32), kk=(C_DK, 64, 32), v=(V_D, 64, 0), y=(0, 64, 0), job=0),
    dict(name="swa", rounds=2, k=64, prev=1, q=(C_SQ, 128, 64), kk=(C_SK, 64, 0), v=(V_S, 64, 0), y=(256, 128, 64), job=8),
    dict(name="fox", rounds=2, k=66, prev=7, q=(C_FQ, 128, 64), kk=(C_FK, 128, 64), v=(V_F, 128, 64), y=(512, 128, 64), job=12),
    dict(name="cmp", rounds=2, k=64, prev=0, q=(C_NQ, 128, 64), kk=None, v=None, y=(768, 128, 64), job=16, gate=0),
    dict(name="sel", rounds=2, k=64, prev=7, q=(C_NQ, 128, 64), kk=(C_KS, 0, 0), v=(V_KS, 0, 0), y=(768, 128, 64), job=20, gate=1),
    dict(name="win", rounds=2, k=64, prev=4, q=(C_NQ, 128, 64), kk=(C_KW, 0, 0), v=(V_KW, 0, 0), y=(768, 128, 64), job=24, gate=2),
]
NJOBS = 28
NEG_SLOPES = [-slope(0, j // 2) for j in range(8)] + [-slope(1, j) for j in range(4)] + [0.0] * 4 + [
    -slope(2, j % 4) for j in range(12)]


class Chain:

    def __init__(self, engine, semaphore):
        self.engine, self.semaphore, self.count = engine, semaphore, 0

    def __call__(self, ins):
        self.count += 1
        ins.then_inc(self.semaphore, 1)
        self.engine.wait_ge(self.semaphore, self.count)


def build(nc, x, c, ada_w, ada_b, norm_attn_g, norm_moe_g, norm_final_g, w_in, w_out,
          diff_lam_q1, diff_lam_k1, diff_lam_q2, diff_lam_k2, diff_subln_g,
          swa_sinks, fox_forget_b, nsa_cmp_pos, nsa_cmp_w1, nsa_cmp_b1, nsa_cmp_w2,
          router_w, router_b, exp_w_gate, exp_w_up, exp_w_down, neg_slopes, out):
    ctx = ExitStack()

    def dram(name, shape):
        return nc.dram_tensor(name, shape, F32).ap()

    qk_rows = dram("qk_rows", [IN_COLS, T])
    cum_rows = dram("cum_rows", [2, NH, T])
    slots_in = dram("slots_in", [ROWS, D])
    slots_out = dram("slots_out", [ROWS, D])

    with ctx:
        def sb(name, shape, dt=F32, to=None):
            return (to or ctx).enter_context(nc.sbuf_tensor(name, shape, dt))

        def sem(name):
            return ctx.enter_context(nc.semaphore(name))

        link = Chain(nc.vector, sem("s_chain"))
        then = Chain(nc.gpsimd, sem("s_pool"))
        bank = ctx.enter_context(nc.psum_tensor("bank", [P, 8, 512], F32))

        ident = sb("ident", [P, P])
        ones = sb("ones", [P, P])
        earlier = sb("earlier", [P, P])
        mod_cols = sb("mod_cols", [P, 48])
        gain_attn = sb("gain_attn", [P, 8])
        gain_moe = sb("gain_moe", [P, 8])
        param_cols = sb("param_cols", [P, 72])
        gate_attn = sb("gate_attn", [P, D])
        gate_moe = sb("gate_moe", [P, D])
        eps_col = sb("eps_col", [P, 1])
        row_gate = sb("row_gate", [P, NT, 2])
        row_slot = sb("row_slot", [P, NT, 2], I32)

        proj = ExitStack()
        heads = ExitStack()
        kcvc = heads.enter_context(nc.sbuf_tensor("kcvc", [P, T], F32))
        v_tok = heads.enter_context(nc.sbuf_tensor("v_tok", [P, NT, VW], F32))

        pj = lambda name, shape, dt=F32: proj.enter_context(nc.sbuf_tensor(name, shape, dt))
        params = pj("params", [72, P])
        cond = pj("cond", [P, 8])
        cond_e = pj("cond_e", [P, 8])
        cond_wide = pj("cond_wide", [P, 8, P])
        xt = pj("xt", [P, 4, D])
        squares = pj("squares", [P, D])
        ss = pj("ss", [P, 3, NT])
        ht = pj("ht", [P, DC, T])
        win = pj("win", [P, DC, IN_COLS])
        ada = pj("ada", [P, ADA_RING, DC, SL])
        stage = pj("stage", [P, 4, 512])
        zeros = squares

        s_param = sem("s_param")
        s_param_t = sem("s_param_t")
        s_const = sem("s_const")
        s_eps = sem("s_eps")
        s_cond = sem("s_cond")
        s_cexp = sem("s_cexp")
        s_x = [sem(f"s_x{i}") for i in range(4)]
        s_ada = [sem(f"s_ada{i}") for i in range(ADA_RING)]
        s_ada_used = sem("s_ada_used")
        s_win = sem("s_win")
        s_sq = sem("s_sq")
        s_sd = sem("s_sd")
        s_xn = sem("s_xn")
        s_tr = sem("s_tr")
        s_ht_a = sem("s_ht_a")
        s_ht_v = sem("s_ht_v")
        s_mod = sem("s_mod")
        s_row_ev = sem("s_row_ev")
        s_rt = sem("s_rt")
        s_rt_a = sem("s_rt_a")
        s_rt_v = sem("s_rt_v")
        s_store = [sem(f"s_store{i}") for i in range(4)]
        s_tk = sem("s_tk")
        s_tk_v = sem("s_tk_v")
        s_bias = sem("s_bias")
        s_zero = sem("s_zero")
        s_zfill = sem("s_zfill")

        ada_v = ada_w[0].rearrange("(k p) n -> p k n", p=P)
        win_v = w_in[0].rearrange("(k p) n -> p k n", p=P)
        x_v = x[0].rearrange("(t p) d -> p t d", p=P)
        N_RT = 2 * len(ROW_TILES)
        CMP_TILE = 13

        def slice_section(s):
            return s * SL // D

        with nc.Block() as block:
            @block.sync
            def _(sp):
                sp.dma_start(params[0:48, :], ada_b[0].rearrange("(m p) -> m p", p=P)).then_inc(s_param, 16)
                sp.dma_start(params[48:56, :], norm_attn_g[0].rearrange("(m p) -> m p", p=P)).then_inc(s_param, 16)
                sp.dma_start(params[56:64, :], norm_moe_g[0].rearrange("(m p) -> m p", p=P)).then_inc(s_param, 16)
                sp.dma_start(params[64:72, :], c[0].rearrange("(m p) -> m p", p=P)).then_inc(s_param, 16)
                for s in range(N_SL):
                    if s < 4:
                        sp.dma_start(xt[:, s, :], x_v[:, s, :]).then_inc(s_x[s], 16)
                    if s >= ADA_RING:
                        sp.wait_ge(s_ada_used, s - ADA_RING + 1)
                    sp.dma_start(ada[:, s % ADA_RING, :, :], ada_v[:, :, s * SL:(s + 1) * SL]).then_inc(
                        s_ada[s % ADA_RING], 16)
                    if s == 8 + ADA_RING - 1:
                        for t in range(4, NT):
                            if t == 4:
                                sp.wait_ge(s_tr, 8)
                            sp.dma_start(xt[:, t - 4, :], x_v[:, t, :]).then_inc(s_x[t - 4], 16)

            @block.gpsimd
            def _(pool):
                for k in range(DC):
                    pool.dma_start(win[:, k, 0:C_KW], win_v[:, k, 0:C_KW]).then_inc(s_win, 16)
                for dst, src, w in ((C_KW, C_VS, 64), (C_VS, C_KW, 64), (C_VW, C_VW, IN_COLS - C_VW)):
                    pool.dma_start(win[:, :, dst:dst + w], win_v[:, :, src:src + w]).then_inc(s_win, 16)
                pool.dma_start(gate_attn[:, :], ada_b[0:1, 2 * D:3 * D].to_broadcast([P, D])).then_inc(s_bias, 16)
                pool.dma_start(gate_moe[:, :], ada_b[0:1, 5 * D:6 * D].to_broadcast([P, D])).then_inc(s_bias, 16)
                then(pool.memset(ident[:, :], 0.0))
                then(pool.affine_select(out=ident[:, :], in_=ident[:, :], compare_op=ALU.not_equal, fill=1.0,
                                        base=0, pattern=[[-1, P]], channel_multiplier=1))
                then(pool.memset(ones[:, :], 1.0))
                pool.sem_inc(s_const, 1)
                then(pool.affine_select(out=earlier[:, :], in_=ones[:, :], compare_op=ALU.is_gt, fill=0.0,
                                        base=0, pattern=[[1, P]], channel_multiplier=-1))
                for i in range(N_RT):
                    if i // 2 == CMP_TILE:
                        continue
                    pool.wait_ge((s_rt_a, s_rt_v)[i % 2], i // 2 + 1)
                    m, half = i // 2, i % 2
                    c0 = ROW_TILES[m][0]
                    src = stage[:, i % 4, :]
                    cols = slice(half * 512, half * 512 + 512)
                    pool.dma_start(qk_rows[c0:c0 + P, cols], src).then_inc(s_store[i % 4], 16)
                pool.wait_ge(s_zero, 1)
                pool.dma_start(slots_in.rearrange("(p r) d -> p r d", p=P),
                               zeros[:, :].rearrange("p (a d) -> p a d", a=1).to_broadcast([P, ROWS // P, D])).then_inc(s_zfill, 16)
                over_rows = ROWS - NE * EB
                pool.dma_start(slots_out[NE * EB:, :].rearrange("(p r) d -> p r d", p=P),
                               zeros[:, :].rearrange("p (a d) -> p a d", a=1).to_broadcast([P, over_rows // P, D])).then_inc(s_zfill, 16)

            @block.tensor
            def _(pe):
                pe.wait_ge(s_param, 64)
                pe.wait_ge(s_const, 1)
                pe.transpose(bank[:, 0, 0:72], params[:, :], ident[0:72, 0:72]).then_inc(s_param_t, 1)
                rows_done = 0

                def ada_slice(s):
                    nonlocal rows_done
                    sec = slice_section(s)
                    pe.wait_ge(s_ada[s % ADA_RING], 16 * (s // ADA_RING + 1))
                    if sec in (2, 5):
                        if rows_done >= 2:
                            pe.wait_ge(s_row_ev, rows_done - 1)
                        o = bank[:, 2 + rows_done % 2, 0:SL]
                        for k in range(DC):
                            mm = pe.matmul(o, cond_wide[:, k, :], ada[:, s % ADA_RING, k, :],
                                           start=(k == 0), stop=(k == DC - 1))
                        rows_done += 1
                    else:
                        for m in range(SL // P):
                            col = sec * 8 + (s * SL % D) // P + m
                            o = bank[:, 1 if sec < 2 else 0, 128 + col:129 + col]
                            for k in range(DC):
                                mm = pe.matmul(o, ada[:, s % ADA_RING, k, m * P:(m + 1) * P], cond[:, k:k + 1],
                                               start=(k == 0), stop=(k == DC - 1))
                    return mm

                pe.wait_ge(s_cond, 2)
                for s in range(8):
                    ada_slice(s).then_inc(s_ada_used, 1)
                n = 0
                for g in range(2):
                    for k in range(DC):
                        for i in range(4):
                            t = 4 * g + i
                            if k == 0:
                                pe.wait_ge(s_xn, t + 1)
                            if i == 0 and n >= 2:
                                pe.wait_ge((s_ht_a, s_ht_v)[n % 2], n // 2)
                            mm = pe.transpose(bank[:, 2 + n % 2, i * P:(i + 1) * P], xt[:, i, k * P:(k + 1) * P], ident[:, :])
                        mm.then_inc(s_tr, 1)
                        n += 1
                pe.wait_ge(s_win, 16 * (DC + 3))
                pe.wait_ge(s_ht_a, 8)
                pe.wait_ge(s_ht_v, 8)
                for i in range(N_RT):
                    m, half = i // 2, i % 2
                    c0 = ROW_TILES[m][0]
                    if i >= 2:
                        pe.wait_ge((s_rt_a, s_rt_v)[i % 2], i // 2)
                    for k in range(DC):
                        mm = pe.matmul(bank[:, 4 + i % 2, :], win[:, k, c0:c0 + P], ht[:, k, half * 512:half * 512 + 512],
                                       start=(k == 0), stop=(k == DC - 1))
                    mm.then_inc(s_rt, 1)
                for i in range(2 * NT):
                    t, b = i // 2, i % 2
                    if i >= 2:
                        pe.wait_ge(s_tk_v, i - 1)
                    at = 0
                    for c0, w in TOKEN_RUNS[b]:
                        for k in range(DC):
                            mm = pe.matmul(bank[:, 6 + b, at:at + w], ht[:, k, t * P:(t + 1) * P], win[:, k, c0:c0 + w],
                                           start=(k == 0), stop=(k == DC - 1))
                        at += w
                    mm.then_inc(s_tk, 1)
                for s in range(8, N_SL):
                    ada_slice(s).then_inc(s_ada_used, 1)

            @block.scalar
            def _(act):
                act.wait_ge(s_cond, 1)
                act.activation(cond_e[:, :], param_cols[:, 64:72], ACT.Exp, scale=-1.0).then_inc(s_cexp, 1)
                act.wait_ge(s_eps, 1)
                n = 0
                for t in range(NT):
                    act.wait_ge(s_x[t % 4], 16 * (t // 4 + 1))
                    act.activation(squares[:, :], xt[:, t % 4, :], ACT.Square, accum_out=ss[:, 0, t:t + 1]).then_inc(s_sq, 1)
                    act.wait_ge(s_sq, t + 1)
                    act.activation(ss[:, 1, t:t + 1], ss[:, 0, t:t + 1], ACT.Sqrt, bias=eps_col[:, :], scale=1.0 / D).then_inc(s_sd, 1)
                    if t == 3:
                        act.wait_ge(s_mod, 1)
                        for k in range(0, DC, 2):
                            act.wait_ge(s_tr, k + 1)
                            act.activation(ht[:, k, 0:512], bank[:, 2, :], ACT.Identity, bias=mod_cols[:, k:k + 1],
                                           scale=gain_attn[:, k:k + 1]).then_inc(s_ht_a, 1)
                act.sem_inc(s_zero, 1)
                for k in range(0, DC, 2):
                    act.wait_ge(s_tr, 8 + k + 1)
                    act.activation(ht[:, k, 512:1024], bank[:, 2, :], ACT.Identity, bias=mod_cols[:, k:k + 1],
                                   scale=gain_attn[:, k:k + 1]).then_inc(s_ht_a, 1)
                for i in range(0, N_RT, 2):
                    m = i // 2
                    act.wait_ge(s_rt, i + 1)
                    if m == CMP_TILE:
                        act.copy(kcvc[:, 0:512], bank[:, 4, :]).then_inc(s_rt_a, 1)
                        continue
                    if i >= 4:
                        uses = sum(1 for j in range(i % 4, i, 4) if j // 2 != CMP_TILE)
                        act.wait_ge(s_store[i % 4], 16 * uses)
                    act.mul(stage[:, i % 4, :], bank[:, 4, :], ROW_TILES[m][1]).then_inc(s_rt_a, 1)

            @block.vector
            def _(dve):
                dve.memset(eps_col[:, :], EPS).then_inc(s_eps, 1)
                dve.wait_ge(s_param_t, 1)
                link(dve.tensor_copy(param_cols[:, :], bank[:, 0, 0:72]))
                dve.sem_inc(s_cond, 1)
                dve.wait_ge(s_cexp, 1)
                link(dve.tensor_scalar(cond_e[:, :], cond_e[:, :], 1.0, None, ALU.add))
                link(dve.reciprocal(cond_e[:, :], cond_e[:, :]))
                link(dve.tensor_tensor(cond[:, :], param_cols[:, 64:72], cond_e[:, :], ALU.mult))
                dve.wait_ge(s_const, 1)
                for k in range(DC):
                    last = dve.tensor_scalar(cond_wide[:, k, :], ones[:, :], cond[:, k:k + 1], None, ALU.mult)
                last.then_inc(s_cond, 1)

                def normalise(t):
                    dve.wait_ge(s_sd, t + 1)
                    link(dve.reciprocal(ss[:, 2, t:t + 1], ss[:, 1, t:t + 1]))
                    dve.tensor_scalar(xt[:, t % 4, :], xt[:, t % 4, :], ss[:, 2, t:t + 1], None, ALU.mult).then_inc(s_xn, 1)

                for t in range(4):
                    normalise(t)
                dve.wait_ge(s_ada_used, 8)
                link(dve.tensor_tensor(mod_cols[:, 0:16], bank[:, 1, 128:144], param_cols[:, 0:16], ALU.add))
                link(dve.tensor_scalar(gain_attn[:, :], mod_cols[:, 8:16], 1.0, None, ALU.add))
                link(dve.tensor_tensor(gain_attn[:, :], gain_attn[:, :], param_cols[:, 48:56], ALU.mult))
                dve.sem_inc(s_mod, 1)
                for g in range(2):
                    for k in range(1, DC, 2):
                        dve.wait_ge(s_tr, 8 * g + k + 1)
                        dve.tensor_scalar(ht[:, k, g * 512:g * 512 + 512], bank[:, 3, :], gain_attn[:, k:k + 1],
                                          mod_cols[:, k:k + 1], ALU.mult, ALU.add).then_inc(s_ht_v, 1)
                    if g == 0:
                        for t in range(4, NT):
                            normalise(t)
                dve.wait_ge(s_zero, 1)
                dve.memset(zeros[:, :], 0.0).then_inc(s_zero, 1)
                for i in range(1, N_RT, 2):
                    m = i // 2
                    dve.wait_ge(s_rt, i + 1)
                    if m == CMP_TILE:
                        dve.tensor_copy(kcvc[:, 512:1024], bank[:, 5, :]).then_inc(s_rt_v, 1)
                        continue
                    if i >= 4:
                        uses = sum(1 for j in range(i % 4, i, 4) if j // 2 != CMP_TILE)
                        dve.wait_ge(s_store[i % 4], 16 * uses)
                    dve.tensor_scalar(stage[:, i % 4, :], bank[:, 5, :], ROW_TILES[m][1], None, ALU.mult).then_inc(s_rt_v, 1)
                for i in range(2 * NT):
                    t, b = i // 2, i % 2
                    w = (VA, VW - VA)[b]
                    dve.wait_ge(s_tk, i + 1)
                    dve.tensor_copy(v_tok[:, t, b * VA:b * VA + w], bank[:, 6 + b, 0:w]).then_inc(s_tk_v, 1)
                rows = 0
                dve.wait_ge(s_bias, 32)
                for s in range(8, N_SL):
                    if slice_section(s) in (2, 5):
                        o = (gate_attn if slice_section(s) == 2 else gate_moe)[:, s * SL % D:s * SL % D + SL]
                        dve.wait_ge(s_ada_used, s + 1)
                        dve.tensor_tensor(o, bank[:, 2 + rows % 2, 0:SL], o, ALU.add).then_inc(s_row_ev, 1)
                        rows += 1
                dve.wait_ge(s_ada_used, N_SL)
                link(dve.tensor_tensor(mod_cols[:, 24:40], bank[:, 0, 152:168], param_cols[:, 24:40], ALU.add))
                link(dve.tensor_scalar(gain_moe[:, :], mod_cols[:, 32:40], 1.0, None, ALU.add))
                link(dve.tensor_tensor(gain_moe[:, :], gain_moe[:, :], param_cols[:, 56:64], ALU.mult))
        proj.close()

        y = heads.enter_context(nc.sbuf_tensor("y", [P, NT, D], F32))
        kc_t = heads.enter_context(nc.sbuf_tensor("kc_t", [HD, NC], F32))
        vc = heads.enter_context(nc.sbuf_tensor("vc", [NC, HD], F32))
        nsa_gate = heads.enter_context(nc.sbuf_tensor("nsa_gate", [P, NT, 3 * NH], F32))
        neg_lam = heads.enter_context(nc.sbuf_tensor("neg_lam", [P, 1], F32))
        dist_full = heads.enter_context(nc.sbuf_tensor("dist_full", [P, T], F32))
        dist_win = heads.enter_context(nc.sbuf_tensor("dist_win", [P, 640], F32))
        dist_swa = heads.enter_context(nc.sbuf_tensor("dist_swa", [P, 256], F32))
        dist_cmp = heads.enter_context(nc.sbuf_tensor("dist_cmp", [P, 119], F32))
        causal = heads.enter_context(nc.sbuf_tensor("causal", [P, T], F32))
        row_seen = heads.enter_context(nc.sbuf_tensor("row_seen", [P, 1], F32))
        comp = ExitStack()
        cp = lambda name, shape, dt=F32: comp.enter_context(nc.sbuf_tensor(name, shape, dt))
        w1 = cp("w1", [P, 32, P])
        pos_rows = cp("pos_rows", [64, HD])
        pos = cp("pos", [P, 32])
        b1 = cp("b1", [P, 2])
        w2 = cp("w2", [P, 2, HD])
        blocks_t = cp("blocks_t", [P, 32, NC])
        hid = cp("hid", [P, 2 * NC])
        hid_a = cp("hid_a", [P, 2 * NC])
        bf = cp("bf", [P, NH])
        fz = cp("fz", [P, 8, NT, NH])
        f_t = cp("f_t", [NH, 2, T])
        cum = cp("cum", [NH, T])
        lam_in = cp("lam_in", [P, 4, 32])
        lam = cp("lam", [P, 4])
        ge = cp("ge", [P, NT, 12])

        s_ld2 = sem("s_ld2")
        s_post = sem("s_post")
        s_pos = sem("s_pos")
        s_blk = sem("s_blk")
        s_hid = sem("s_hid")
        s_a2 = sem("s_a2")
        s_v2 = sem("s_v2")
        s_hid2 = sem("s_hid2")
        s_kc = sem("s_kc")
        s_ft = sem("s_ft")
        s_f = sem("s_f")
        s_cum = sem("s_cum")
        s_cumst = sem("s_cumst")

        with nc.Block() as block:
            @block.sync
            def _(sp):
                for h in range(2):
                    sp.dma_start(w1[64 * h:64 * h + 64, :, :], nsa_cmp_w1[0, h].rearrange("(j d) o -> d j o", d=HD)).then_inc(s_ld2, 16)
                sp.dma_start(pos_rows[:, :], nsa_cmp_pos[0].rearrange("h j d -> (h j) d")).then_inc(s_ld2, 16)
                sp.dma_start(b1[:, :], nsa_cmp_b1[0].rearrange("h o -> o h"), allow_slow_non_contiguous=True).then_inc(s_ld2, 16)
                sp.dma_start(w2[:, :, :], nsa_cmp_w2[0].rearrange("h o d -> o h d")).then_inc(s_ld2, 16)
                sp.dma_start(bf[:, :], fox_forget_b[0:1, :].to_broadcast([P, NH])).then_inc(s_ld2, 16)
                for i, v in enumerate((diff_lam_q1, diff_lam_k1, diff_lam_q2, diff_lam_k2)):
                    sp.dma_start(lam_in[:, i, :], v[0:1, :].to_broadcast([P, 32])).then_inc(s_ld2, 16)
                for i in range(2):
                    sp.wait_ge(s_cum, 1)
                    sp.dma_start(cum_rows[i], (f_t[:, 1, :], cum[:, :])[i]).then_inc(s_cumst, 16)
                sp.wait_ge(s_cumst, 32)
                for i in range(4):
                    uses = sum(1 for j in range(i, N_RT, 4) if j // 2 != CMP_TILE)
                    sp.wait_ge(s_store[i], 16 * uses)
                sp.wait_ge(s_zfill, 32)

            @block.gpsimd
            def _(pool):
                then(pool.iota(dist_full[:, :], pattern=[[-1, T]], base=T - P, channel_multiplier=1,
                               allow_small_or_imprecise_dtypes=True))
                then(pool.affine_select(out=dist_full[:, :], in_=dist_full[:, :], compare_op=ALU.is_ge, fill=BIG,
                                        base=T - P, pattern=[[-1, T]], channel_multiplier=1))
                then(pool.affine_select(out=dist_win[:, :], in_=dist_full[:, T - 640:], compare_op=ALU.is_gt, fill=BIG,
                                        base=0, pattern=[[1, 640]], channel_multiplier=-1))
                then(pool.affine_select(out=dist_swa[:, :], in_=dist_full[:, T - 256:], compare_op=ALU.is_gt, fill=BIG,
                                        base=0, pattern=[[1, 256]], channel_multiplier=-1))
                then(pool.iota(dist_cmp[:, :], pattern=[[-16, 119]], base=16 * 56 - 31, channel_multiplier=1,
                               allow_small_or_imprecise_dtypes=True))
                then(pool.affine_select(out=dist_cmp[:, :], in_=dist_cmp[:, :], compare_op=ALU.is_ge, fill=BIG,
                                        base=16 * 56 - 31, pattern=[[-16, 119]], channel_multiplier=1))
                then(pool.memset(causal[:, :], 0.0))
                then(pool.affine_select(out=causal[:, :], in_=causal[:, :], compare_op=ALU.is_ge, fill=-1e30,
                                        base=T - P, pattern=[[-1, T]], channel_multiplier=1))
                then(pool.memset(row_seen[:, :], 1.0))
                then(pool.affine_select(out=row_seen[:, :], in_=row_seen[:, :], compare_op=ALU.is_ge, fill=0.0,
                                        base=-31, pattern=[[0, 1]], channel_multiplier=1))

            @block.tensor
            def _(pe):
                pe.wait_ge(s_ld2, 160)
                pe.transpose(bank[0:64, 0, 0:64], pos_rows[:, :], ident[0:64, 0:64]).then_inc(s_post, 1)
                pe.wait_ge(s_blk, 1)
                for h in range(2):
                    for j in range(32):
                        mm = pe.matmul(bank[:, 2 + h, 0:NC], w1[64 * h:64 * h + 64, j, :],
                                       blocks_t[64 * h:64 * h + 64, j, :], start=(j == 0), stop=(j == 31))
                mm.then_inc(s_hid, 1)
                pe.wait_ge(s_f, 1)
                for t in range(NT):
                    mm = pe.transpose(bank[0:NH, 4 + t // 4, t % 4 * P:t % 4 * P + P], fz[:, 7, t, :], ident[:, :])
                mm.then_inc(s_ft, 1)
                pe.wait_ge(s_hid2, 1)
                pe.matmul(bank[0:HD, 6, 0:NC], w2[:, 0, :], hid[:, 0:NC], start=True, stop=True)
                pe.matmul(bank[0:NC, 7, 0:HD], hid[:, NC:2 * NC], w2[:, 1, :], start=True, stop=True).then_inc(s_kc, 1)

            @block.scalar
            def _(act):
                act.activation(ge[:, :, :], v_tok[:, :, V_G:V_G + 12], ACT.Exp, scale=-1.0).then_inc(s_a2, 1)
                act.wait_ge(s_v2, 1)
                act.activation(fz[:, 2, :, :], fz[:, 1, :, :], ACT.Exp).then_inc(s_a2, 1)
                act.wait_ge(s_v2, 2)
                act.activation(lam[:, 0:2], lam[:, 0:2], ACT.Exp).then_inc(s_a2, 1)
                act.wait_ge(s_v2, 3)
                act.activation(hid_a[:, :], hid_a[:, :], ACT.Exp, scale=-2.0 * (2.0 / 3.141592653589793) ** 0.5).then_inc(s_a2, 1)
                act.wait_ge(s_v2, 4)
                act.activation(fz[:, 4, :, :], fz[:, 3, :, :], ACT.Ln).then_inc(s_a2, 1)

            @block.vector
            def _(dve):
                dve.wait_ge(s_ld2, 160)
                z = fz[:, 0, :, :]
                link(dve.tensor_tensor(z, v_tok[:, :, V_FF:V_FF + NH],
                                       bf[:, :].rearrange("p (a h) -> p a h", a=1).to_broadcast([P, NT, NH]), ALU.add))
                link(dve.tensor_scalar(fz[:, 1, :, :], z, -1.0, None, ALU.mult))
                link(dve.tensor_tensor(fz[:, 1, :, :], fz[:, 1, :, :], z, ALU.min))
                dve.sem_inc(s_v2, 1)
                link(dve.tensor_tensor(lam_in[:, 0, :], lam_in[:, 0, :], lam_in[:, 1, :], ALU.mult))
                link(dve.tensor_tensor(lam_in[:, 2, :], lam_in[:, 2, :], lam_in[:, 3, :], ALU.mult))
                link(dve.reduce_sum(lam[:, 0:1], lam_in[:, 0, :], AX_X))
                link(dve.reduce_sum(lam[:, 1:2], lam_in[:, 2, :], AX_X))
                dve.sem_inc(s_v2, 1)
                dve.wait_ge(s_post, 1)
                link(dve.tensor_copy(pos[0:64, :], bank[0:64, 0, 0:32]))
                link(dve.tensor_copy(pos[64:P, :], bank[0:64, 0, 32:64]))
                kv3 = kcvc[:, :].rearrange("p (n b) -> p b n", b=16)
                for a in range(2):
                    link(dve.tensor_tensor(blocks_t[:, 16 * a:16 * a + 16, :], kv3[:, :, a:a + NC],
                                           pos[:, 16 * a:16 * a + 16].rearrange("p (j a) -> p j a", a=1).to_broadcast([P, 16, NC]),
                                           ALU.add))
                dve.sem_inc(s_blk, 1)
                dve.wait_ge(s_a2, 2)
                link(dve.tensor_scalar(fz[:, 3, :, :], fz[:, 2, :, :], 1.0, None, ALU.add))
                dve.wait_ge(s_a2, 1)
                link(dve.tensor_scalar(ge[:, :, :], ge[:, :, :], 1.0, None, ALU.add))
                link(dve.reciprocal(nsa_gate[:, :, :], ge[:, :, :]))
                dve.wait_ge(s_a2, 3)
                link(dve.tensor_tensor(lam[:, 2:3], lam[:, 1:2], lam[:, 0:1], ALU.subtract))
                link(dve.tensor_scalar(neg_lam[:, :], lam[:, 2:3], -LAM_INIT, None, ALU.add))
                dve.wait_ge(s_hid, 1)
                for h in range(2):
                    link(dve.tensor_scalar(hid[:, h * NC:h * NC + NC], bank[:, 2 + h, 0:NC], b1[:, h:h + 1], None, ALU.add))
                link(dve.tensor_tensor(hid_a[:, :], hid[:, :], hid[:, :], ALU.mult))
                link(dve.tensor_scalar(hid_a[:, :], hid_a[:, :], 0.044715, 1.0, ALU.mult, ALU.add))
                link(dve.tensor_tensor(hid_a[:, :], hid_a[:, :], hid[:, :], ALU.mult))
                dve.sem_inc(s_v2, 1)
                dve.wait_ge(s_a2, 4)
                link(dve.tensor_scalar(hid_a[:, :], hid_a[:, :], 1.0, None, ALU.add))
                link(dve.reciprocal(hid_a[:, :], hid_a[:, :]))
                link(dve.tensor_tensor(hid[:, :], hid[:, :], hid_a[:, :], ALU.mult))
                dve.sem_inc(s_hid2, 1)
                dve.sem_inc(s_v2, 1)
                e, w, lw = fz[:, 2, :, :], fz[:, 3, :, :], fz[:, 4, :, :]
                is_one, den = fz[:, 5, :, :], fz[:, 6, :, :]
                dve.wait_ge(s_a2, 5)
                link(dve.tensor_scalar(den, w, -1.0, None, ALU.add))
                link(dve.tensor_scalar(is_one, den, 0.0, None, ALU.is_equal))
                link(dve.tensor_tensor(den, den, is_one, ALU.add))
                link(dve.tensor_tensor(lw, lw, is_one, ALU.add))
                link(dve.reciprocal(den, den))
                link(dve.tensor_tensor(lw, lw, e, ALU.mult))
                link(dve.tensor_tensor(lw, lw, den, ALU.mult))
                link(dve.tensor_scalar(z, z, 0.0, None, ALU.min))
                link(dve.tensor_tensor(fz[:, 7, :, :], z, lw, ALU.subtract))
                dve.sem_inc(s_f, 1)
                link(dve.memset(f_t[:, 1, :], 1.0))
                dve.wait_ge(s_ft, 1)
                link(dve.tensor_copy(f_t[:, 0, :], bank[0:NH, 4:6, :].rearrange("p a b -> p (a b)")))
                link(dve.tensor_tensor_scan(cum[:, :], f_t[:, 1, :], f_t[:, 0, :], 0.0, ALU.mult, ALU.add))
                link(dve.tensor_scalar(f_t[:, 1, :], cum[:, :], -1.0, None, ALU.mult))
                dve.sem_inc(s_cum, 1)
                dve.wait_ge(s_kc, 1)
                link(dve.tensor_copy(kc_t[:, :], bank[0:HD, 6, 0:NC]))
                link(dve.tensor_copy(vc[:, :], bank[0:NC, 7, 0:HD]))
        comp.close()

        att = ExitStack()
        at_ = lambda name, shape, dt=F32: att.enter_context(nc.sbuf_tensor(name, shape, dt))
        qb = [at_(f"qb{i}", [P, T]) for i in range(2)]
        kb = [at_(f"kb{i}", [P, T]) for i in range(2)]
        neg_slope = at_("neg_slope", [P, 2])
        sink = at_("sink", [P, 2])
        neg_sink = at_("neg_sink", [P, 2])
        sink_exp = at_("sink_exp", [P, 8])
        bias = at_("bias", [P, 2, T])
        probs = at_("probs", [P, 2, T])
        probs_t = at_("probs_t", [P, 2, 8, P])
        low = at_("low", [P, 8])
        total = at_("total", [P, 8])
        factor = at_("factor", [P, 8])
        spare = at_("spare", [P, 2])
        nil = at_("nil", [P, 1])
        first_map = at_("first_map", [P, NT, HD])

        attend(nc, sem, dict(
            bank=bank, ident=ident, qb=qb, kb=kb, neg_slope=neg_slope, sink=sink, neg_sink=neg_sink,
            sink_exp=sink_exp, bias=bias, probs=probs, probs_t=probs_t, low=low, total=total, factor=factor,
            first_map=first_map, spare=spare, nil=nil, y=y, v_tok=v_tok, kc_t=kc_t, vc=vc, nsa_gate=nsa_gate, neg_lam=neg_lam,
            row_seen=row_seen, causal=causal, dist_full=dist_full, dist_win=dist_win, dist_swa=dist_swa,
            dist_cmp=dist_cmp, qk_rows=qk_rows, cum_rows=cum_rows, neg_slopes=neg_slopes, swa_sinks=swa_sinks))
        att.close()

        po = ExitStack()
        tail = ExitStack()
        o_ = lambda name, shape, dt=F32: po.enter_context(nc.sbuf_tensor(name, shape, dt))
        wo = o_("wo", [P, DC, D])
        y_t = o_("y_t", [P, DC, T])
        sub = o_("sub", [P, NT, NH, HD])
        sub_s = o_("sub_s", [P, 3, NT * NH])
        sub_g = o_("sub_g", [P, HD])
        xr = o_("xr", [P, 4, D])
        x1_d = dram("x1_rows", [T, D])
        x1_v = x1_d.rearrange("(t p) d -> p t d", p=P)
        s_wo = sem("s_wo")
        s_sub = sem("s_sub")
        s_sqr = sem("s_sqr")
        s_yn = sem("s_yn")
        s_yt = sem("s_yt")
        s_yt_a = sem("s_yt_a")
        s_yt_v = sem("s_yt_v")
        s_wout = sem("s_wout")
        s_x1_done = sem("s_x1_done")
        s_xr = [sem(f"s_xr{i}") for i in range(4)]
        s_x1st = [sem(f"s_x1st{i}") for i in range(4)]
        with nc.Block() as block:
            @block.sync
            def _(sp):
                sp.dma_start(sub_g[:, :], diff_subln_g[0:1, :].to_broadcast([P, HD])).then_inc(s_sub, 16)
                for k in range(DC):
                    sp.dma_start(wo[:, k, :], w_out[0, k * P:(k + 1) * P, :]).then_inc(s_wo, 16)
                for t in range(NT):
                    if t >= 4:
                        sp.wait_ge(s_x1st[t % 4], 16 * (t // 4))
                    sp.dma_start(xr[:, t % 4, :], x_v[:, t, :]).then_inc(s_xr[t % 4], 16)

            @block.gpsimd
            def _(pool):
                for t in range(NT):
                    pool.wait_ge(s_x1_done, t + 1)
                    pool.dma_start(x1_v[:, t, :], xr[:, t % 4, :]).then_inc(s_x1st[t % 4], 16)
                for i in range(4):
                    pool.wait_ge(s_x1st[i], 32)

            @block.tensor
            def _(pe):
                n = 0
                for k in (2, 3, 4, 5, 6, 7, 0, 1):
                    if k == 0:
                        pe.wait_ge(s_yn, 1)
                    for g in range(2):
                        if n >= 2:
                            pe.wait_ge((s_yt_a, s_yt_v)[n % 2], n // 2)
                        for i in range(4):
                            mm = pe.transpose(bank[:, n % 2, i * P:(i + 1) * P], y[:, 4 * g + i, k * P:(k + 1) * P], ident[:, :])
                        mm.then_inc(s_yt, 1)
                        n += 1
                pe.wait_ge(s_yt_a, 8)
                pe.wait_ge(s_yt_v, 8)
                pe.wait_ge(s_wo, 16 * DC)
                for t in range(NT):
                    if t >= 2:
                        pe.wait_ge(s_x1_done, t - 1)
                    for half in range(2):
                        for k in range(DC):
                            mm = pe.matmul(bank[:, 2 + 2 * (t % 2) + half, :], y_t[:, k, t * P:(t + 1) * P],
                                           wo[:, k, half * 512:half * 512 + 512], start=(k == 0), stop=(k == DC - 1))
                    mm.then_inc(s_wout, 1)

            @block.scalar
            def _(act):
                act.wait_ge(s_sqr, 1)
                act.activation(sub_s[:, 1, :], sub_s[:, 0, :], ACT.Sqrt, bias=eps_col[:, :], scale=1.0 / HD).then_inc(s_sqr, 1)
                order = [(k, g) for k in (2, 3, 4, 5, 6, 7, 0, 1) for g in range(2)]
                for n in range(0, 16, 2):
                    k, g = order[n]
                    act.wait_ge(s_yt, n + 1)
                    act.copy(y_t[:, k, g * 512:g * 512 + 512], bank[:, 0, :]).then_inc(s_yt_a, 1)

            @block.vector
            def _(dve):
                yd = y[:, :, 0:NH * HD].rearrange("p t (h d) -> p t h d", h=NH)
                for t in range(NT):
                    link(dve.tensor_tensor(sub[:, t, :, :], yd[:, t, :, :], yd[:, t, :, :], ALU.mult))
                link(dve.reduce_sum(sub_s[:, 0, :], sub[:, :, :, :].rearrange("p t h d -> p (t h) d"), AX_X))
                dve.sem_inc(s_sqr, 1)
                dve.wait_ge(s_sub, 16)
                link(dve.tensor_scalar(sub_g[:, :], sub_g[:, :], 1.0 - LAM_INIT, None, ALU.mult))
                dve.wait_ge(s_sqr, 2)
                link(dve.reciprocal(sub_s[:, 2, :], sub_s[:, 1, :]))
                for t in range(NT):
                    r = sub_s[:, 2, t * NH:(t + 1) * NH].rearrange("p (h a) -> p h a", a=1).to_broadcast([P, NH, HD])
                    link(dve.tensor_tensor(yd[:, t, :, :], yd[:, t, :, :], r, ALU.mult))
                    link(dve.tensor_tensor(yd[:, t, :, :], yd[:, t, :, :],
                                           sub_g[:, :].rearrange("p (a d) -> p a d", a=1).to_broadcast([P, NH, HD]), ALU.mult))
                dve.sem_inc(s_yn, 1)
                order = [(k, g) for k in (2, 3, 4, 5, 6, 7, 0, 1) for g in range(2)]
                for m in range(1, 16, 2):
                    k, g = order[m]
                    dve.wait_ge(s_yt, m + 1)
                    dve.tensor_copy(y_t[:, k, g * 512:g * 512 + 512], bank[:, 1, :]).then_inc(s_yt_v, 1)
                for t in range(NT):
                    dve.wait_ge(s_wout, t + 1)
                    dve.wait_ge(s_xr[t % 4], 16 * (t // 4 + 1))
                    acc = bank[:, 2 + 2 * (t % 2):4 + 2 * (t % 2), :].rearrange("p a b -> p (a b)")
                    o = sub[:, 4 * (t % 2):4 * (t % 2) + 4, :, :].rearrange("p a b c -> p (a b c)")
                    link(dve.tensor_tensor(o, acc, gate_attn[:, :], ALU.mult))
                    dve.tensor_tensor(xr[:, t % 4, :], xr[:, t % 4, :], o, ALU.add).then_inc(s_x1_done, 1)
        po.close()
        heads.close()

        rt = ExitStack()
        over = ctx.enter_context(nc.sbuf_tensor("over", [1, 64], I32))
        r_ = lambda name, shape, dt=F32: rt.enter_context(nc.sbuf_tensor(name, shape, dt))
        xn = r_("xn", [P, NT, D])
        h2_t = r_("h2_t", [P, DC, T])
        sq2 = r_("sq2", [P, D])
        rs2 = r_("rs2", [P, 3, NT])
        rw = r_("rw", [P, DC, NE])
        rb = r_("rb", [P, NE])
        aff = r_("aff", [P, NT, NE])
        sel = r_("sel", [P, NT, NE])
        top = r_("top", [P, NT, 8, 8])
        gsum = r_("gsum", [P, NT, 8])
        gmax = r_("gmax", [P, NT, 8])
        gidx = r_("gidx", [P, NT, 8], U32)
        gidx_f = r_("gidx_f", [P, NT, 8])
        keep = r_("keep", [P, NT, NE])
        hot = r_("hot", [P, 2, NT, NE])
        both = r_("both", [P, NT, NE])
        before = r_("before", [P, NT, NE])
        tmp = r_("tmp", [P, NT, NE])
        iota_e = r_("iota_e", [P, NE])
        iota_g = r_("iota_g", [P, NE])
        steps = r_("steps", [P, 16])
        counts = r_("counts", [P, NE])
        cmp16 = r_("cmp16", [P, NE, 16])
        ovn = r_("ovn", [P, NE])
        ov_end = r_("ov_end", [P, NE])
        ov_base = r_("ov_base", [P, NE])
        ones_row = r_("ones_row", [P, NE])
        iota_b = r_("iota_b", [1, 32])
        cmpb = r_("cmpb", [1, 32, NE])
        over_f = r_("over_f", [1, 33])
        rank = r_("rank", [P, NT, 8])
        slot_f = r_("slot_f", [P, NT, 2])
        s_ld4 = sem("s_ld4")
        s_x1r = [sem(f"s_x1r{i}") for i in range(NT)]
        s_iota = sem("s_iota")
        s_sq4 = sem("s_sq4")
        s_sd4 = sem("s_sd4")
        s_xn4 = sem("s_xn4")
        s_tr4 = sem("s_tr4")
        s_h_a = sem("s_h_a")
        s_h_v = sem("s_h_v")
        s_log = sem("s_log")
        s_sig = sem("s_sig")
        s_both = sem("s_both")
        s_pre = sem("s_pre")
        s_slot = sem("s_slot")
        s_scat = sem("s_scat")
        with nc.Block() as block:
            @block.sync
            def _(sp):
                for t in range(NT):
                    sp.dma_start(xn[:, t, :], x1_v[:, t, :]).then_inc(s_x1r[t], 16)
                sp.dma_start(rw[:, :, :], router_w.rearrange("(k p) e -> p k e", p=P)).then_inc(s_ld4, 16)
                sp.dma_start(rb[:, :], router_b.rearrange("(a e) -> a e", a=1).to_broadcast([P, NE])).then_inc(s_ld4, 16)

            @block.gpsimd
            def _(pool):
                imp = dict(allow_small_or_imprecise_dtypes=True)
                pool.iota(iota_e[:, :], pattern=[[1, NE]], base=0, channel_multiplier=0, **imp).then_inc(s_iota, 1)
                pool.iota(iota_g[:, :], pattern=[[1, 8], [0, 8]], base=0, channel_multiplier=0, **imp).then_inc(s_iota, 1)
                pool.iota(steps[:, :], pattern=[[EB, 16]], base=EB, channel_multiplier=0, **imp).then_inc(s_iota, 1)
                pool.iota(iota_b[:, :], pattern=[[1, 32]], base=0, channel_multiplier=0, **imp).then_inc(s_iota, 1)
                pool.memset(ones_row[:, :], 1.0).then_inc(s_iota, 1)
                pool.wait_ge(s_slot, 1)
                for t in range(NT):
                    for j in range(2):
                        pool.indirect_dma_start(
                            out=slots_in, out_offset=bass.IndirectOffsetOnAxis(ap=row_slot[:, t, j:j + 1].bitcast(U32), axis=0),
                            in_=xn[:, t, :], in_offset=None).then_inc(s_scat, 16)
                pool.wait_ge(s_scat, 16 * 2 * NT)

            @block.tensor
            def _(pe):
                n = 0
                for g in range(2):
                    for k in range(DC):
                        for i in range(4):
                            t = 4 * g + i
                            if k == 0:
                                pe.wait_ge(s_xn4, t + 1)
                            if i == 0 and n >= 2:
                                pe.wait_ge((s_h_a, s_h_v)[n % 2], n // 2)
                            mm = pe.transpose(bank[:, n % 2, i * P:(i + 1) * P], xn[:, t, k * P:(k + 1) * P], ident[:, :])
                        mm.then_inc(s_tr4, 1)
                        n += 1
                    pe.wait_ge(s_h_a, 4 * g + 4)
                    pe.wait_ge(s_h_v, 4 * g + 4)
                    pe.wait_ge(s_ld4, 32)
                    for i in range(4):
                        t = 4 * g + i
                        for k in range(DC):
                            mm = pe.matmul(bank[:, 2, t * NE:(t + 1) * NE], h2_t[:, k, t * P:(t + 1) * P], rw[:, k, :],
                                           start=(k == 0), stop=(k == DC - 1))
                mm.then_inc(s_log, 1)
                pe.wait_ge(s_both, 1)
                for t in range(NT):
                    for u in range(t):
                        pe.matmul(bank[:, 3, t * NE:(t + 1) * NE], ones[:, :], both[:, u, :], start=(u == 0), stop=False)
                    pe.matmul(bank[:, 3, t * NE:(t + 1) * NE], earlier[:, :], both[:, t, :], start=(t == 0), stop=True)
                for u in range(NT):
                    mm = pe.matmul(bank[:, 4, 0:NE], ones[:, :], both[:, u, :], start=(u == 0), stop=(u == NT - 1))
                mm.then_inc(s_pre, 1)

            @block.scalar
            def _(act):
                for t in range(NT):
                    act.wait_ge(s_x1r[t], 16)
                    act.activation(sq2[:, :], xn[:, t, :], ACT.Square, accum_out=rs2[:, 0, t:t + 1]).then_inc(s_sq4, 1)
                    act.wait_ge(s_sq4, t + 1)
                    act.activation(rs2[:, 1, t:t + 1], rs2[:, 0, t:t + 1], ACT.Sqrt, bias=eps_col[:, :], scale=1.0 / D).then_inc(s_sd4, 1)
                for n in range(0, 16, 2):
                    k, g = n % 8, n // 8
                    act.wait_ge(s_tr4, n + 1)
                    act.activation(h2_t[:, k, g * 512:g * 512 + 512], bank[:, 0, :], ACT.Identity, bias=mod_cols[:, 24 + k:25 + k],
                                   scale=gain_moe[:, k:k + 1]).then_inc(s_h_a, 1)
                act.wait_ge(s_log, 1)
                act.activation(aff[:, :, :].rearrange("p t e -> p (t e)"), bank[:, 2, :], ACT.Exp, scale=-1.0).then_inc(s_sig, 1)

            @block.vector
            def _(dve):
                def wide(ap, shape, spec, **kw):
                    return ap.rearrange(spec, **kw).to_broadcast(shape)

                def norm(t):
                    dve.wait_ge(s_sd4, t + 1)
                    link(dve.reciprocal(rs2[:, 2, t:t + 1], rs2[:, 1, t:t + 1]))
                    dve.tensor_scalar(xn[:, t, :], xn[:, t, :], rs2[:, 2, t:t + 1], None, ALU.mult).then_inc(s_xn4, 1)

                for t in range(NT):
                    norm(t)
                for m in range(1, 16, 2):
                    k, g = m % 8, m // 8
                    dve.wait_ge(s_tr4, m + 1)
                    dve.tensor_scalar(h2_t[:, k, g * 512:g * 512 + 512], bank[:, 1, :], gain_moe[:, k:k + 1],
                                      mod_cols[:, 24 + k:25 + k], ALU.mult, ALU.add).then_inc(s_h_v, 1)
                dve.wait_ge(s_sig, 1)
                dve.wait_ge(s_ld4, 32)
                link(dve.tensor_scalar(aff[:, :, :], aff[:, :, :], 1.0, None, ALU.add))
                link(dve.reciprocal(aff[:, :, :], aff[:, :, :]))
                link(dve.tensor_tensor(sel[:, :, :], aff[:, :, :], wide(rb[:, :], [P, NT, NE], "p (a e) -> p a e", a=1), ALU.add))
                for t in range(NT):
                    for g in range(8):
                        last = dve.max(out=top[:, t, g, :], in_=sel[:, t, 8 * g:8 * g + 8])
                link(last)
                link(dve.tensor_tensor(gsum[:, :, :], top[:, :, :, 0], top[:, :, :, 1], ALU.add))
                for t in range(NT):
                    last = dve.max(out=gmax[:, t, :], in_=gsum[:, t, :])
                link(last)
                for t in range(NT):
                    last = dve.max_index(out=gidx[:, t, :], in_max=gmax[:, t, :], in_values=gsum[:, t, :])
                link(last)
                link(dve.tensor_copy(gidx_f[:, :, :], gidx[:, :, :]))
                dve.wait_ge(s_iota, 5)
                link(dve.tensor_tensor(keep[:, :, :], wide(iota_g[:, :], [P, NT, NE], "p (a e) -> p a e", a=1),
                                       gidx_f[:, :, 0:1].to_broadcast([P, NT, NE]), ALU.is_equal))
                link(dve.tensor_tensor(sel[:, :, :], sel[:, :, :], keep[:, :, :], ALU.mult))
                link(dve.tensor_scalar(keep[:, :, :], keep[:, :, :], -1.0, 1e30, ALU.add, ALU.mult))
                link(dve.tensor_tensor(sel[:, :, :], sel[:, :, :], keep[:, :, :], ALU.add))
                for t in range(NT):
                    last = dve.max(out=gmax[:, t, :], in_=sel[:, t, :])
                link(last)
                for t in range(NT):
                    last = dve.max_index(out=gidx[:, t, :], in_max=gmax[:, t, :], in_values=sel[:, t, :])
                link(last)
                link(dve.tensor_copy(gidx_f[:, :, :], gidx[:, :, :]))
                for j in range(2):
                    link(dve.tensor_tensor(hot[:, j, :, :], wide(iota_e[:, :], [P, NT, NE], "p (a e) -> p a e", a=1),
                                           gidx_f[:, :, j:j + 1].to_broadcast([P, NT, NE]), ALU.is_equal))
                link(dve.tensor_tensor(both[:, :, :], hot[:, 0, :, :], hot[:, 1, :, :], ALU.add))
                dve.sem_inc(s_both, 1)

                def pick(o, table, j):
                    link(dve.tensor_tensor(tmp[:, :, :], hot[:, j, :, :], table, ALU.mult))
                    link(dve.reduce_sum(o, tmp[:, :, :], AX_X))

                for j in range(2):
                    pick(rank[:, :, j], aff[:, :, :], j)
                link(dve.tensor_tensor(rank[:, :, 2], rank[:, :, 0], rank[:, :, 1], ALU.add))
                link(dve.reciprocal(rank[:, :, 2], rank[:, :, 2]))
                for j in range(2):
                    link(dve.tensor_tensor(row_gate[:, :, j], rank[:, :, j], rank[:, :, 2], ALU.mult))
                dve.wait_ge(s_pre, 1)
                link(dve.tensor_copy(before[:, :, :].rearrange("p t e -> p (t e)"), bank[:, 3, :]))
                link(dve.tensor_copy(counts[:, :], bank[:, 4, 0:NE]))
                link(dve.tensor_tensor(cmp16[:, :, :], wide(counts[:, :], [P, NE, 16], "p (e a) -> p e a", a=1),
                                       wide(steps[:, :], [P, NE, 16], "p (a s) -> p a s", a=1), ALU.is_gt))
                link(dve.reduce_sum(ovn[:, :], cmp16[:, :, :], AX_X))
                link(dve.tensor_tensor_scan(ov_end[:, :], ones_row[:, :], ovn[:, :], 0.0, ALU.mult, ALU.add))
                link(dve.tensor_tensor(ov_base[:, :], ov_end[:, :], ovn[:, :], ALU.subtract))
                link(dve.tensor_tensor(cmpb[:, :, :], wide(ov_end[0:1, :], [1, 32, NE], "p (a e) -> p a e", a=1),
                                       wide(iota_b[:, :], [1, 32, NE], "p (b a) -> p b a", a=1), ALU.is_le))
                link(dve.reduce_sum(over_f[:, 0:32], cmpb[:, :, :], AX_X))
                link(dve.tensor_scalar(over_f[:, 0:32], over_f[:, 0:32], float(NE - 1), None, ALU.min))
                link(dve.tensor_copy(over_f[:, 32:33], ov_end[0:1, NE - 1:NE]))
                link(dve.tensor_copy(over[:, 0:33], over_f[:, :]))
                link(dve.tensor_scalar(ov_base[:, :], ov_base[:, :], float(EB), float(NE * EB - EB), ALU.mult, ALU.add))
                for j in range(2):
                    pick(rank[:, :, 3], before[:, :, :], j)
                    pick(rank[:, :, 4], wide(ov_base[:, :], [P, NT, NE], "p (a e) -> p a e", a=1), j)
                    link(dve.tensor_scalar(rank[:, :, 5], rank[:, :, 3], float(EB), None, ALU.is_ge))
                    link(dve.tensor_scalar(rank[:, :, 6], gidx_f[:, :, j], float(EB), None, ALU.mult))
                    link(dve.tensor_tensor(rank[:, :, 4], rank[:, :, 4], rank[:, :, 6], ALU.subtract))
                    link(dve.tensor_tensor(rank[:, :, 4], rank[:, :, 4], rank[:, :, 5], ALU.mult))
                    link(dve.tensor_tensor(rank[:, :, 3], rank[:, :, 3], rank[:, :, 6], ALU.add))
                    link(dve.tensor_tensor(slot_f[:, :, j], rank[:, :, 3], rank[:, :, 4], ALU.add))
                link(dve.tensor_copy(row_slot[:, :, :], slot_f[:, :, :]))
                dve.sem_inc(s_slot, 1)
        rt.close()

        ex = ExitStack()
        e_ = lambda name, shape, dt=F32: ex.enter_context(nc.sbuf_tensor(name, shape, dt))
        wg = [e_(f"wg{i}", [P, DC, DF]) for i in range(2)]
        wu = [e_(f"wu{i}", [P, DC, DF]) for i in range(2)]
        wd = [e_(f"wd{i}", [P, FC, D]) for i in range(2)]
        xe = [e_(f"xe{i}", [EB, D]) for i in range(2)]
        xe_t = [e_(f"xe_t{i}", [P, DC, EB]) for i in range(2)]
        act_e = [e_(f"act_e{i}", [P, FC, EB]) for i in range(2)]
        act_h = [e_(f"act_h{i}", [P, FC, EB]) for i in range(2)]
        xe_mid = e_("xe_mid", [P, DC, EB])
        oe = [e_(f"oe{i}", [EB, D]) for i in range(2)]
        gate_v = exp_w_gate[0].rearrange("e (k p) f -> e p k f", p=P)
        up_v = exp_w_up[0].rearrange("e (k p) f -> e p k f", p=P)
        down_v = exp_w_down[0].rearrange("e (k p) d -> e p k d", p=P)
        wide_gain = lambda: gain_moe[:, :].rearrange("p (k a) -> p k a", a=1).to_broadcast([P, DC, EB])
        wide_shift = lambda: mod_cols[:, 24:32].rearrange("p (k a) -> p k a", a=1).to_broadcast([P, DC, EB])

        s_gu = [sem(f"s_gu{i}") for i in range(2)]
        s_dn = [sem(f"s_dn{i}") for i in range(2)]
        s_xe = [sem(f"s_xe{i}") for i in range(2)]
        s_xt5 = sem("s_xt5")
        s_xt_ok = sem("s_xt_ok")
        s_gu_done = sem("s_gu_done")
        s_e5 = sem("s_e5")
        s_t5 = sem("s_t5")
        s_d5 = sem("s_d5")
        s_r5 = sem("s_r5")
        s_g5 = sem("s_g5")
        s_h5 = sem("s_h5")
        s_down = sem("s_down")
        s_oe_a = sem("s_oe_a")
        s_oe_v = sem("s_oe_v")
        s_out5 = [sem(f"s_out5{i}") for i in range(2)]

        def transposed_rows(pe, buf, o):
            for k in range(DC):
                mm = pe.transpose(o[:, k * EB:(k + 1) * EB], xe[buf][:, k * P:(k + 1) * P], ident[0:EB, 0:EB])
            return mm

        def gate_and_up(pe, buf, o):
            for i, w in enumerate((wg[buf], wu[buf])):
                for m in range(FC):
                    for k in range(DC):
                        mm = pe.matmul(o[:, (i * FC + m) * EB:(i * FC + m + 1) * EB], w[:, k, m * P:(m + 1) * P],
                                       xe_t[buf][:, k, :], start=(k == 0), stop=(k == DC - 1))
            return mm

        def down(pe, buf, o):
            for half in range(2):
                for m in range(FC):
                    mm = pe.matmul(o[0:EB, half, :], act_h[buf][:, m, :], wd[buf][:, m, half * 512:half * 512 + 512],
                                   start=(m == 0), stop=(m == FC - 1))
            return mm

        def modulate(dve, buf, o, s_mid, mid, s_done):
            rows = o[:, :].rearrange("p (k t) -> p k t", k=DC)
            dve.tensor_tensor(xe_mid[:, :, :], rows, wide_gain(), ALU.mult).then_inc(s_mid, 1)
            dve.wait_ge(s_mid, mid)
            dve.tensor_tensor(xe_t[buf][:, :, :], xe_mid[:, :, :], wide_shift(), ALU.add).then_inc(s_done, 1)

        def silu_times_up(dve, buf, o, sems, value, s_done):
            flat = act_e[buf][:, :, :].rearrange("p m t -> p (m t)")
            dve.tensor_scalar(flat, flat, 1.0, None, ALU.add).then_inc(sems[0], 1)
            dve.wait_ge(sems[0], value)
            dve.reciprocal(flat, flat).then_inc(sems[1], 1)
            dve.wait_ge(sems[1], value)
            dve.tensor_tensor(flat, flat, o[:, 0:FC * EB], ALU.mult).then_inc(sems[2], 1)
            dve.wait_ge(sems[2], value)
            dve.tensor_tensor(act_h[buf][:, :, :].rearrange("p m t -> p (m t)"), flat, o[:, FC * EB:2 * FC * EB],
                              ALU.mult).then_inc(s_done, 1)

        with nc.Block() as block:
            @block.sync
            def _(sp):
                with sp.Fori(0, NE // 2) as it:
                    for b in range(2):
                        n = it * 2 + b
                        sp.wait_ge(s_gu_done, n + 1)
                        sp.dma_start(wg[b][:, :, :], gate_v[ds(n, 1)].rearrange("a p k f -> p (a k) f")).then_inc(s_gu[b], 16)
                        sp.dma_start(wu[b][:, :, :], up_v[ds(n, 1)].rearrange("a p k f -> p (a k) f")).then_inc(s_gu[b], 16)
                        sp.wait_ge(s_down, n + 1)
                        sp.dma_start(wd[b][:, :, :], down_v[ds(n, 1)].rearrange("a p k d -> p (a k) d")).then_inc(s_dn[b], 16)

            @block.tensor
            def _(pe):
                pe.sem_inc(s_gu_done, 2)
                pe.sem_inc(s_down, 2)
                pe.sem_inc(s_xt5, 1)
                pe.wait_ge(s_xe[0], 16)
                transposed_rows(pe, 0, bank[:, 0, :]).then_inc(s_xt5, 1)
                with pe.Fori(0, NE // 2) as it:
                    for b in range(2):
                        n = it * 2 + b
                        pe.wait_ge(s_xe[1 - b], it * 16 + 16 + 16 * b)
                        pe.wait_ge(s_gu[b], it * 32 + 32)
                        pe.wait_ge(s_xt_ok, n + 1)
                        pe.wait_ge(s_h5, n + 1)
                        gate_and_up(pe, b, bank[:, 2 + b, :]).then_inc(s_gu_done, 1)
                        transposed_rows(pe, 1 - b, bank[:, 1 - b, :]).then_inc(s_xt5, 1)
                        pe.wait_ge(s_dn[b], it * 16 + 16)
                        pe.wait_ge(s_h5, n + 3)
                        pe.wait_ge(s_oe_a, n + 1)
                        pe.wait_ge(s_oe_v, n + 1)
                        down(pe, b, bank[:, 4 + 2 * b:6 + 2 * b, :]).then_inc(s_down, 1)

            @block.scalar
            def _(act):
                act.sem_inc(s_oe_a, 2)
                act.sem_inc(s_out5[0], 16)
                act.sem_inc(s_out5[1], 16)
                act.dma_start(xe[0][:, :], slots_in[0:EB, :]).then_inc(s_xe[0], 16)
                with act.Fori(0, NE // 2) as it:
                    for b in range(2):
                        n = it * 2 + b
                        act.wait_ge(s_xt5, n + 1)
                        act.dma_start(xe[1 - b][:, :], slots_in[ds((n + 1) * EB, EB), :]).then_inc(s_xe[1 - b], 16)
                        act.wait_ge(s_gu_done, n + 3)
                        act.activation(act_e[b][:, :, :].rearrange("p m t -> p (m t)"), bank[:, 2 + b, 0:FC * EB], ACT.Exp,
                                       scale=-1.0).then_inc(s_e5, 1)
                        act.wait_ge(s_down, n + 3)
                        act.wait_ge(s_out5[b], it * 16 + 16)
                        act.copy(oe[b][:, 0:512], bank[0:EB, 4 + 2 * b, :]).then_inc(s_oe_a, 1)
                        act.wait_ge(s_oe_a, n + 3)
                        act.wait_ge(s_oe_v, n + 3)
                        act.dma_start(slots_out[ds(n * EB, EB), :], oe[b][:, :]).then_inc(s_out5[b], 16)
                for b in range(2):
                    act.wait_ge(s_out5[b], 16 * (NE // 2 + 1))

            @block.vector
            def _(dve):
                dve.sem_inc(s_oe_v, 2)
                dve.sem_inc(s_h5, 2)
                dve.wait_ge(s_xt5, 2)
                modulate(dve, 0, bank[:, 0, :], s_t5, 1, s_xt_ok)
                with dve.Fori(0, NE // 2) as it:
                    for b in range(2):
                        n = it * 2 + b
                        dve.wait_ge(s_e5, n + 1)
                        dve.wait_ge(s_down, n + 1)
                        silu_times_up(dve, b, bank[:, 2 + b, :], (s_d5, s_r5, s_g5), n + 1, s_h5)
                        dve.wait_ge(s_xt5, n + 3)
                        modulate(dve, 1 - b, bank[:, 1 - b, :], s_t5, n + 2, s_xt_ok)
                        dve.wait_ge(s_down, n + 3)
                        dve.wait_ge(s_out5[b], it * 16 + 16)
                        dve.tensor_copy(oe[b][:, 512:1024], bank[0:EB, 5 + 2 * b, :]).then_inc(s_oe_v, 1)

        s_v_load = sem("s_v_load")
        s_v_t = sem("s_v_t")
        s_v_mid = sem("s_v_mid")
        s_v_x = sem("s_v_x")
        s_v_gu = sem("s_v_gu")
        s_v_e = sem("s_v_e")
        s_v_3 = [sem(f"s_v_3{i}") for i in range(3)]
        s_v_h = sem("s_v_h")
        s_v_dn = sem("s_v_dn")
        s_v_o = sem("s_v_o")
        s_v_st = sem("s_v_st")
        s_v_end = sem("s_v_end")
        with nc.Block() as block:
            def used_blocks(eng):
                count = eng.value_load(over[0:1, 32:33], min_val=0, max_val=NOV)
                return count

            @block.sync
            def _(sp):
                count = used_blocks(sp)
                sp.sem_inc(s_v_st, 16)
                with sp.Fori(0, NOV) as n:
                    with sp.If(n < count):
                        e = sp.value_load(over[0:1, ds(n, 1)], min_val=0, max_val=NE - 1)
                        sp.wait_ge(s_v_st, n * 16 + 16)
                        sp.dma_start(wg[0][:, :, :], gate_v[ds(e, 1)].rearrange("a p k f -> p (a k) f")).then_inc(s_v_load, 16)
                        sp.dma_start(wu[0][:, :, :], up_v[ds(e, 1)].rearrange("a p k f -> p (a k) f")).then_inc(s_v_load, 16)
                        sp.dma_start(wd[0][:, :, :], down_v[ds(e, 1)].rearrange("a p k d -> p (a k) d")).then_inc(s_v_load, 16)
                        sp.dma_start(xe[0][:, :], slots_in[ds(n * EB + NE * EB, EB), :]).then_inc(s_v_load, 16)
                        sp.wait_ge(s_v_o, n + 1)
                        sp.dma_start(slots_out[ds(n * EB + NE * EB, EB), :], oe[0][:, :]).then_inc(s_v_st, 16)

            @block.tensor
            def _(pe):
                count = used_blocks(pe)
                with pe.Fori(0, NOV) as n:
                    with pe.If(n < count):
                        pe.wait_ge(s_v_load, n * 64 + 64)
                        pe.matmul(bank[:, 1, 0:P], ident[:, :], ident[:, :], start=True, stop=True)
                        transposed_rows(pe, 0, bank[:, 0, :]).then_inc(s_v_t, 1)
                        pe.wait_ge(s_v_x, n + 1)
                        gate_and_up(pe, 0, bank[:, 2, :]).then_inc(s_v_gu, 1)
                        pe.wait_ge(s_v_h, n + 1)
                        down(pe, 0, bank[:, 4:6, :]).then_inc(s_v_dn, 1)

            @block.scalar
            def _(act):
                count = used_blocks(act)
                with act.Fori(0, NOV) as n:
                    with act.If(n < count):
                        act.wait_ge(s_v_gu, n + 1)
                        act.activation(act_e[0][:, :, :].rearrange("p m t -> p (m t)"), bank[:, 2, 0:FC * EB], ACT.Exp,
                                       scale=-1.0).then_inc(s_v_e, 1)
                act.wait_ge(s_v_st, count * 16 + 16)
                act.copy(act_e[1][:, 0, 0:1], ones[:, 0:1]).then_inc(s_v_end, 1)

            @block.vector
            def _(dve):
                count = used_blocks(dve)
                with dve.Fori(0, NOV) as n:
                    with dve.If(n < count):
                        dve.wait_ge(s_v_t, n + 1)
                        modulate(dve, 0, bank[:, 0, :], s_v_mid, n + 1, s_v_x)
                        dve.wait_ge(s_v_e, n + 1)
                        silu_times_up(dve, 0, bank[:, 2, :], s_v_3, n + 1, s_v_h)
                        dve.wait_ge(s_v_dn, n + 1)
                        dve.tensor_copy(oe[0][:, :], bank[0:EB, 4:6, :].rearrange("p a b -> p (a b)")).then_inc(s_v_o, 1)
        ex.close()

        RING = 3
        c_ = lambda name, shape, dt=F32: ctx.enter_context(nc.sbuf_tensor(name, shape, dt))
        x1 = c_("x1", [P, NT, D])
        row_a = c_("row_a", [P, RING, D])
        row_b = c_("row_b", [P, RING, D])
        sq6 = c_("sq6", [P, D])
        g_fin = c_("g_fin", [P, D])
        rs6 = c_("rs6", [P, 3, NT])
        s_x6 = sem("s_x6")
        s_g6 = sem("s_g6")
        s_rows = [sem(f"s_rows{i}") for i in range(RING)]
        s_ga = sem("s_ga")
        s_x2_done = sem("s_x2_done")
        s_sq6 = sem("s_sq6")
        s_sd6 = sem("s_sd6")
        s_fin = sem("s_fin")
        s_out = sem("s_out")
        out_v = out[0].rearrange("(t p) d -> p t d", p=P)
        with nc.Block() as block:
            @block.sync
            def _(sp):
                for t in range(NT):
                    sp.dma_start(x1[:, t, :], x1_v[:, t, :]).then_inc(s_x6, 16)
                sp.dma_start(g_fin[:, :], norm_final_g.rearrange("(a d) -> a d", a=1).to_broadcast([P, D])).then_inc(s_g6, 16)
                for t in range(NT):
                    sp.wait_ge(s_fin, t + 1)
                    sp.dma_start(out_v[:, t, :], x1[:, t, :]).then_inc(s_out, 16)
                sp.wait_ge(s_out, 16 * NT)

            @block.gpsimd
            def _(pool):
                for t in range(NT):
                    if t >= RING:
                        pool.wait_ge(s_x2_done, t - RING + 1)
                    for j, r in enumerate((row_a, row_b)):
                        pool.indirect_dma_start(
                            out=r[:, t % RING, :], out_offset=None, in_=slots_out,
                            in_offset=bass.IndirectOffsetOnAxis(ap=row_slot[:, t, j:j + 1].bitcast(U32), axis=0)).then_inc(s_rows[t % RING], 16)

            @block.scalar
            def _(act):
                def weigh(t):
                    act.wait_ge(s_rows[t % RING], 32 * (t // RING + 1))
                    act.activation(row_a[:, t % RING, :], row_a[:, t % RING, :], ACT.Copy, scale=row_gate[:, t, 0:1]).then_inc(s_ga, 1)

                weigh(0)
                for t in range(NT):
                    if t + 1 < NT:
                        weigh(t + 1)
                    act.wait_ge(s_x2_done, t + 1)
                    act.activation(sq6[:, :], x1[:, t, :], ACT.Square, accum_out=rs6[:, 0, t:t + 1]).then_inc(s_sq6, 1)
                    act.wait_ge(s_sq6, t + 1)
                    act.activation(rs6[:, 1, t:t + 1], rs6[:, 0, t:t + 1], ACT.Sqrt, bias=eps_col[:, :], scale=1.0 / D).then_inc(s_sd6, 1)

            @block.vector
            def _(dve):
                def finish(t):
                    dve.wait_ge(s_sd6, t + 1)
                    link(dve.reciprocal(rs6[:, 2, t:t + 1], rs6[:, 1, t:t + 1]))
                    dve.scalar_tensor_tensor(out=x1[:, t, :], in0=x1[:, t, :], scalar=rs6[:, 2, t:t + 1], in1=g_fin[:, :],
                                             op0=ALU.mult, op1=ALU.mult).then_inc(s_fin, 1)

                dve.wait_ge(s_x6, 16 * NT)
                dve.wait_ge(s_g6, 16)
                for t in range(NT):
                    a, b = row_a[:, t % RING, :], row_b[:, t % RING, :]
                    dve.wait_ge(s_ga, t + 1)
                    link(dve.scalar_tensor_tensor(out=b, in0=b, scalar=row_gate[:, t, 1:2], in1=a, op0=ALU.mult, op1=ALU.add))
                    link(dve.tensor_tensor(b, b, gate_moe[:, :], ALU.mult))
                    dve.tensor_tensor(x1[:, t, :], x1[:, t, :], b, ALU.add).then_inc(s_x2_done, 1)
                    if t >= 1:
                        finish(t - 1)
                finish(NT - 1)


class Mixer:

    def __init__(self, g, before):
        self.g, self.name, self.K, self.prev, self.rounds = g, g["name"], g["k"], g["prev"], g["rounds"]
        self.is_cmp, self.is_fox, self.is_swa, self.is_diff = (self.name == k for k in ("cmp", "fox", "swa", "diff"))
        self.rows = 64 if self.is_fox else self.K
        self.loads = 1 + (not self.is_cmp) + (not self.is_fox) + self.is_swa + 2 * self.is_fox
        self.steps = before.steps + 16 * before.rounds if before else 0
        self.jobs_biased = before.jobs_biased + 2 * before.rounds * (not before.is_fox) if before else 0
        self.load_sum = before.load_sum + 16 * before.loads * before.rounds if before else 0
        self.splits = before.splits + 8 * before.rounds * (before.prev >= 4) if before else 0
        self.factors = before.factors + before.rounds * before.factors_per_round if before else 0
        self.factors_per_round = 8 if self.is_diff else 16 if "gate" in g else 0

    def span(self, i):
        n = min(i, self.prev) + 1
        return i - n + 1, n

    def width(self, i):
        return NC if self.is_cmp else self.span(i)[1] * P

    def blocks(self, i):
        return 1 if self.is_cmp else self.span(i)[1]


def attend(nc, sem, have):
    bank, ident, qb, kb, neg_slope, sink, neg_sink, sink_exp, bias, probs, probs_t, low, total, factor, first_map, spare, nil, y, \
        v_tok, kc_t, vc, nsa_gate, neg_lam, row_seen, causal, qk_rows, cum_rows, neg_slopes, swa_sinks = (
            have[k] for k in ("bank ident qb kb neg_slope sink neg_sink sink_exp bias probs probs_t low total factor "
                              "first_map spare nil y v_tok kc_t vc nsa_gate neg_lam row_seen causal qk_rows cum_rows "
                              "neg_slopes swa_sinks").split())
    dists = {"diff": have["dist_full"], "sel": have["dist_full"], "win": have["dist_win"], "swa": have["dist_swa"],
             "cmp": have["dist_cmp"]}
    mixers = []
    for g in GROUPS:
        mixers.append(Mixer(g, mixers[-1] if mixers else None))

    s_load = [sem(f"s_load{i}") for i in range(2)]
    s_ones = sem("s_ones")
    s_nsink = sem("s_nsink")
    s_bias7 = sem("s_bias7")
    s_qk = sem("s_qk")
    s_max = sem("s_max")
    s_exp = sem("s_exp")
    s_sink = sem("s_sink")
    s_first = sem("s_first")
    s_tr7 = sem("s_tr7")
    s_cp0 = sem("s_cp0")
    s_cp1 = sem("s_cp1")
    s_pv = sem("s_pv")
    s_den = sem("s_den")
    s_spare = sem("s_spare")
    s_inv = sem("s_inv")
    s_fac = sem("s_fac")
    s_o = sem("s_o")

    with nc.Block() as block:
        def load_job(sp, m, it, b):
            q0, qi, qj = m.g["q"]
            sp.dma_start(qb[b][0:m.rows, :], qk_rows[ds(it * qi + (q0 + b * qj), m.rows), :]).then_inc(s_load[b], 16)
            if not m.is_cmp:
                k0, ki, kj = m.g["kk"]
                k_at = ds(it * ki + (k0 + b * kj), m.rows) if ki else slice(k0 + b * kj, k0 + b * kj + m.rows)
                sp.dma_start(kb[b][0:m.rows, :], qk_rows[k_at, :]).then_inc(s_load[b], 16)
            if not m.is_fox:
                sp.dma_start(neg_slope[:, b:b + 1], neg_slopes[ds(it * 2 + (m.g["job"] + b), 1), :].rearrange("a p -> p a"),
                             allow_slow_non_contiguous=True).then_inc(s_load[b], 16)
            if m.is_swa:
                sp.dma_start(sink[:, b:b + 1], swa_sinks[0:1, ds(it * 2 + b, 1)].to_broadcast([P, 1])).then_inc(s_load[b], 16)
            if m.is_fox:
                sp.dma_start(kb[b][64:65, :], cum_rows[0, ds(it * 2 + b, 1), :]).then_inc(s_load[b], 16)
                sp.dma_start(qb[b][65:66, :], cum_rows[1, ds(it * 2 + b, 1), :]).then_inc(s_load[b], 16)

        @block.sync
        def _(sp):
            for m in mixers:
                if m.is_fox:
                    sp.wait_ge(s_ones, 4)
                with sp.Fori(0, m.rounds) as it:
                    for b in range(2):
                        at = it * 16 + (m.steps + 8 * b + 8)
                        sp.wait_ge(s_qk, at)
                        sp.wait_ge(s_max, at)
                        if m.is_swa:
                            sp.wait_ge(s_sink, at)
                        load_job(sp, m, it, b)

        @block.gpsimd
        def _(pool):
            for n, t in enumerate((*qb, *kb)):
                pool.memset(t[64:66, :], 1.0).then_inc(s_ones, 1)
                pool.wait_ge(s_ones, n + 1)
            pool.memset(nil[:, :], 0.0).then_inc(s_ones, 1)
            pool.wait_ge(s_ones, 5)
            for m in mixers:
                if m.is_fox:
                    continue
                dist = dists[m.name]
                with pool.Fori(0, m.rounds) as it:
                    for b in range(2):
                        pool.wait_ge(s_load[b], it * (16 * m.loads) + (m.load_sum + 16 * m.loads))
                        pool.wait_ge(s_max, it * 16 + (m.steps + 8 * b + 8))
                        if m.is_swa:
                            pool.tensor_tensor(neg_sink[:, b:b + 1], nil[:, :], sink[:, b:b + 1], ALU.subtract).then_inc(s_nsink, 1)
                        pool.tensor_tensor(bias[:, b, 0:dist.shape[1]], dist[:, :],
                                           neg_slope[:, b:b + 1].to_broadcast([P, dist.shape[1]]), ALU.mult).then_inc(s_bias7, 1)

        @block.tensor
        def _(pe):
            pe.sem_inc(s_qk, 16)
            pe.sem_inc(s_tr7, 2)
            pe.sem_inc(s_pv, 2)

            def scores(m, it, k):
                b, i = k // 8, k % 8
                first, _ = m.span(i)
                if i == 0:
                    pe.wait_ge(s_load[b], it * (16 * m.loads) + (m.load_sum + 16 * m.loads))
                pe.wait_ge(s_max, it * 16 + (m.steps + k + 15))
                w = m.width(i)
                for at in range(0, w, 512):
                    keys = kc_t[:, :] if m.is_cmp else kb[b][0:m.K, first * P + at:first * P + min(w, at + 512)]
                    mm = pe.matmul(bank[:, 2 * (i % 2) + at // 512, 0:min(w - at, 512)], qb[b][0:m.K, i * P:(i + 1) * P],
                                   keys, start=True, stop=True)
                mm.then_inc(s_qk, 1)

            def turn(m, it, k):
                b, i = k // 8, k % 8
                pe.wait_ge(s_exp, it * 16 + (m.steps + k + 1))
                pe.wait_ge(s_cp0, it * 16 + (m.steps + k + 1))
                for j in range(m.blocks(i)):
                    if j == 4:
                        mm.then_inc(s_first, 1)
                        pe.wait_ge(s_cp1, it * 8 + (m.splits + 4 * b + i - 3))
                    mm = pe.transpose(bank[:, 4 + j // 4, j % 4 * P:(j % 4 + 1) * P], probs[:, i % 2, j * P:(j + 1) * P], ident[:, :])
                mm.then_inc(s_tr7, 1)

            def values(m, it, k):
                b, i = k // 8, k % 8
                first, nb = m.span(i)
                pe.wait_ge(s_cp0, it * 16 + (m.steps + k + 2))
                if m.blocks(i) > 4:
                    pe.wait_ge(s_cp1, it * 8 + (m.splits + 4 * b + i - 2))
                pe.wait_ge(s_o, it * 16 + (m.steps + k + 1))
                if m.is_cmp:
                    mm = pe.matmul(bank[:, 6 + i % 2, 0:HD], probs_t[0:NC, i % 2, 0, :], vc[:, :], start=True, stop=True)
                else:
                    v0, vi, vj = m.g["v"]
                    cols = ds(it * vi + (v0 + b * vj), HD) if vi else slice(v0 + b * vj, v0 + b * vj + HD)
                    for j in range(nb):
                        mm = pe.matmul(bank[:, 6 + i % 2, 0:HD], probs_t[:, i % 2, j, :], v_tok[:, first + j, cols],
                                       start=(j == 0), stop=(j == nb - 1))
                mm.then_inc(s_pv, 1)

            for m in mixers:
                with pe.Fori(0, m.rounds) as it:
                    for k in range(18):
                        if k < 16:
                            scores(m, it, k)
                        if 1 <= k < 17:
                            turn(m, it, k - 1)
                        if k >= 2:
                            values(m, it, k - 2)

        @block.scalar
        def _(act):
            act.sem_inc(s_cp0, 1)
            act.sem_inc(s_sink, 16 + next(m.steps for m in mixers if m.is_swa))

            def exponentials(m, it, k):
                i = k % 8
                p = probs[:, i % 2, 0:m.width(i)]
                act.wait_ge(s_max, it * 16 + (m.steps + k + 17))
                act.activation(p, p, ACT.Exp, bias=low[:, i:i + 1], scale=-1.0, accum_out=total[:, i:i + 1]).then_inc(s_exp, 1)
                if m.is_swa:
                    act.activation(sink_exp[:, i:i + 1], sink[:, k // 8:k // 8 + 1], ACT.Exp, bias=low[:, i:i + 1]).then_inc(s_sink, 1)

            def copy_first(m, it, k):
                b, i = k // 8, k % 8
                nb = m.blocks(i)
                if nb > 4:
                    act.wait_ge(s_first, it * 8 + (m.splits + 4 * b + i - 3))
                else:
                    act.wait_ge(s_tr7, it * 16 + (m.steps + k + 3))
                act.wait_ge(s_pv, it * 16 + (m.steps + k + 1))
                kw, w = (NC if m.is_cmp else P), min(nb, 4) * P
                act.copy(probs_t[0:kw, i % 2, 0:min(nb, 4), :].rearrange("p a b -> p (a b)"), bank[0:kw, 4, 0:w]).then_inc(s_cp0, 1)

            for m in mixers:
                with act.Fori(0, m.rounds) as it:
                    for k in range(17):
                        if k < 16:
                            exponentials(m, it, k)
                        if k >= 1:
                            copy_first(m, it, k - 1)

        @block.vector
        def _(dve):
            dve.memset(probs[:, :, :], 0.0).then_inc(s_max, 1)
            dve.wait_ge(s_max, 1)
            dve.sem_inc(s_max, 15)
            dve.sem_inc(s_cp1, 1)
            dve.sem_inc(s_o, 2)

            def reciprocal(m, it, k):
                i = k % 8
                t_, f = total[:, i:i + 1], factor[:, i:i + 1]
                dve.wait_ge(s_exp, it * 16 + (m.steps + k + 1))
                if m.is_swa:
                    dve.wait_ge(s_sink, it * 16 + (m.steps + k + 17))
                    dve.tensor_tensor(t_, t_, sink_exp[:, i:i + 1], ALU.add).then_inc(s_den, 1)
                    dve.wait_ge(s_den, it * 16 + (k + 1))
                dve.reciprocal(f, t_).then_inc(s_inv, 1)

            def maxima(m, it, k):
                b, i = k // 8, k % 8
                w = m.width(i)
                dve.wait_ge(s_qk, it * 16 + (m.steps + k + 17))
                if i == 0 and not m.is_fox:
                    dve.wait_ge(s_bias7, it * 2 + (m.jobs_biased + b + 1))
                dve.wait_ge(s_tr7, it * 16 + (m.steps + k + 1))
                if m.is_cmp:
                    add = bias[:, b, 56 - 8 * i:56 - 8 * i + NC]
                elif m.is_fox:
                    add = causal[:, T - w:T]
                else:
                    end = dists[m.name].shape[1]
                    add = bias[:, b, end - w:end]
                s = bank[:, 2 * (i % 2):2 * (i % 2) + 2, :].rearrange("p a b -> p (a b)")[:, 0:w]
                if k >= 2:
                    reciprocal(m, it, k - 2)
                else:
                    dve.memset(spare[:, k:k + 1], 0.0).then_inc(s_spare, 1)
                dve.tensor_tensor_reduce(out=probs[:, i % 2, 0:w], in0=s, in1=add, scale=-1.0,
                                         scalar=neg_sink[:, b:b + 1] if m.is_swa else HUGE, op0=ALU.add, op1=ALU.min,
                                         accum_out=low[:, i:i + 1]).then_inc(s_max, 1)

            def copy_second(m, it, k):
                i, nb = k % 8, m.blocks(k % 8)
                if nb > 4:
                    dve.wait_ge(s_tr7, it * 16 + (m.steps + k + 3))
                    dve.wait_ge(s_pv, it * 16 + (m.steps + k + 1))
                    dve.tensor_copy(probs_t[:, i % 2, 4:nb, :].rearrange("p a b -> p (a b)"), bank[:, 5, 0:(nb - 4) * P]).then_inc(s_cp1, 1)

            def output(m, it, k):
                b, i = k // 8, k % 8
                f = factor[:, i:i + 1]
                dve.wait_ge(s_inv, it * 16 + (m.steps + k + 1))
                if m.is_diff and b == 1:
                    dve.tensor_tensor(f, f, neg_lam[:, :], ALU.mult).then_inc(s_fac, 1)
                    dve.wait_ge(s_fac, it * 8 + (m.factors + i + 1))
                if "gate" in m.g:
                    gate = nsa_gate[:, i, ds(it * 6 + (3 * b + m.g["gate"]), 1)]
                    if m.is_cmp and i == 0:
                        dve.scalar_tensor_tensor(out=f, in0=f, scalar=gate, in1=row_seen[:, :], op0=ALU.mult, op1=ALU.mult).then_inc(s_fac, 1)
                    else:
                        dve.tensor_tensor(f, f, gate, ALU.mult).then_inc(s_fac, 1)
                    dve.wait_ge(s_fac, it * 16 + (m.factors + k + 1))
                dve.wait_ge(s_pv, it * 16 + (m.steps + k + 3))
                o = bank[:, 6 + i % 2, 0:HD]
                y0, yi, yj = m.g["y"]
                yo = y[:, i, ds(it * yi + (y0 + b * yj), HD)]
                if m.is_diff and b == 0:
                    dve.tensor_scalar(first_map[:, i, :], o, f, None, ALU.mult).then_inc(s_o, 1)
                elif m.is_diff:
                    dve.wait_ge(s_o, it * 16 + (m.steps + k - 5))
                    dve.scalar_tensor_tensor(out=yo, in0=o, scalar=f, in1=first_map[:, i, :], op0=ALU.mult, op1=ALU.add).then_inc(s_o, 1)
                elif m.name in ("sel", "win"):
                    dve.wait_ge(s_o, it * 16 + (m.steps + k - 29))
                    dve.scalar_tensor_tensor(out=yo, in0=o, scalar=f, in1=yo, op0=ALU.mult, op1=ALU.add).then_inc(s_o, 1)
                else:
                    dve.tensor_scalar(yo, o, f, None, ALU.mult).then_inc(s_o, 1)

            for m in mixers:
                with dve.Fori(0, m.rounds) as it:
                    for k in range(18):
                        if k < 16:
                            maxima(m, it, k)
                        if 1 <= k < 17:
                            copy_second(m, it, k - 1)
                        if k >= 16:
                            reciprocal(m, it, k - 2)
                        if k >= 2:
                            output(m, it, k - 2)


_INS = ['x', 'c', 'ada_w', 'ada_b', 'norm_attn_g', 'norm_moe_g', 'norm_final_g', 'w_in', 'w_out', 'diff_lam_q1',
        'diff_lam_k1', 'diff_lam_q2', 'diff_lam_k2', 'diff_subln_g', 'swa_sinks', 'fox_forget_b', 'nsa_cmp_pos',
        'nsa_cmp_w1', 'nsa_cmp_b1', 'nsa_cmp_w2', 'router_w', 'router_b', 'exp_w_gate', 'exp_w_up', 'exp_w_down']


def kernel(**inputs):
    import numpy as np
    import concourse.bacc as bacc
    from concourse.bass_utils import run_bass_kernel_spmd

    nc = bacc.Bacc("TRN2", target_bir_lowering=False, num_devices=1)
    arrays, args = {}, {}
    for name in _INS:
        a = np.ascontiguousarray(inputs[name])
        arrays[f"in_{name}"] = a
        args[name] = nc.dram_tensor(f"in_{name}", a.shape, F32, kind="ExternalInput").ap()
    arrays["in_neg_slopes"] = np.repeat(np.array(NEG_SLOPES, np.float32)[:, None], P, axis=1)
    args["neg_slopes"] = nc.dram_tensor("in_neg_slopes", (NJOBS, P), F32, kind="ExternalInput").ap()
    out = nc.dram_tensor("out", (1, T, D), F32, kind="ExternalOutput").ap()
    build(nc, **args, out=out)
    r = run_bass_kernel_spmd(nc, [arrays], core_ids=[0])
    return r.results[0]["out"]
```

```python
from contextlib import ExitStack

import concourse.bass as bass
from concourse import mybir

F32 = mybir.dt.float32
I32 = mybir.dt.int32
U32 = mybir.dt.uint32
F32R = mybir.dt.float32r
ALU = mybir.AluOpType
ACT = mybir.ActivationFunctionType
AX_X = mybir.AxisListType.X
ds = bass.ds

P = 128
T = 1024
NT = T // P
D = 1024
DC = D // P
HD = 64
NH = 4
EPS = 1e-6
BIG = 1e32
HUGE = 3e38

C_DQ, C_DK, C_DV = 0, 256, 512
C_SQ, C_SK, C_SV = 768, 1024, 1152
C_FQ, C_FK, C_FV, C_FF = 1280, 1536, 1792, 2048
C_NQ, C_KC, C_KS, C_KW, C_VS, C_VW, C_G = 2052, 2308, 2436, 2500, 2564, 2628, 2692
IN_COLS = 2704
ROW_TILES = (
    [(c, 32 ** -0.5) for c in (0, 128)] + [(c, 1.0) for c in (256, 384)]
    + [(c, 0.125) for c in (768, 896)] + [(1024, 1.0)]
    + [(c, 0.125) for c in (1280, 1408)] + [(c, 1.0) for c in (1536, 1664)]
    + [(c, 0.125) for c in (2052, 2180)] + [(C_KC, 1.0), (C_KS, 1.0)]
)
TOKEN_RUNS = [[(C_DV, 256), (C_SV, 128)], [(C_FV, 260), (C_VS, 64), (C_VW, 76)]]
VA = 384
VW = 784
V_D, V_S, V_F, V_FF, V_KS, V_KW, V_G = 0, 256, 384, 640, 644, 708, 772

SL = 256
N_SL = 6 * D // SL
ADA_RING = 2
NC = 63
NE = 64
EB = 128
IN_ROWS = 2 * T + EB
NOV_T = 16
NOV = (2 * T - 1) // (EB + 1)
OUT_ROWS = IN_ROWS + NOV * EB
DF = 512
FC = DF // P
LAM_INIT = 0.2


def slope(mixer, head):
    return 2.0 ** (-8.0 * (3 * head + mixer + 1) / (3 * NH))


GROUPS = [
    dict(name="diff", rounds=4, k=32, prev=7, q=(C_DQ, 64, 32), kk=(C_DK, 64, 32), v=(V_D, 64, 0), y=(0, 64, 0), job=0),
    dict(name="swa", rounds=2, k=64, prev=1, q=(C_SQ, 128, 64), kk=(C_SK, 64, 0), v=(V_S, 64, 0), y=(256, 128, 64), job=8),
    dict(name="fox", rounds=2, k=64, prev=7, q=(C_FQ, 128, 64), kk=(C_FK, 128, 64), v=(V_F, 128, 64), y=(512, 128, 64), job=12),
    dict(name="cmp", rounds=2, k=64, prev=0, q=(C_NQ, 128, 64), kk=None, v=None, y=(768, 128, 64), job=16, gate=0),
    dict(name="sel", rounds=2, k=64, prev=7, q=(C_NQ, 128, 64), kk=(C_KS, 0, 0), v=(V_KS, 0, 0), y=(768, 128, 64), job=20, gate=1),
    dict(name="win", rounds=2, k=64, prev=4, q=(C_NQ, 128, 64), kk=(C_KW, 0, 0), v=(V_KW, 0, 0), y=(768, 128, 64), job=24, gate=2),
]
NJOBS = 28
NEG_SLOPES = [-slope(0, j // 2) for j in range(8)] + [-slope(1, j) for j in range(4)] + [0.0] * 4 + [
    -slope(2, j % 4) for j in range(12)]


class Chain:

    def __init__(self, engine, semaphore):
        self.engine, self.semaphore, self.count = engine, semaphore, 0

    def __call__(self, ins):
        self.count += 1
        ins.then_inc(self.semaphore, 1)
        self.engine.wait_ge(self.semaphore, self.count)


def build(nc, x, c, ada_w, ada_b, norm_attn_g, norm_moe_g, norm_final_g, w_in, w_out,
          diff_lam_q1, diff_lam_k1, diff_lam_q2, diff_lam_k2, diff_subln_g,
          swa_sinks, fox_forget_b, nsa_cmp_pos, nsa_cmp_w1, nsa_cmp_b1, nsa_cmp_w2,
          router_w, router_b, exp_w_gate, exp_w_up, exp_w_down, neg_slopes, out):
    ctx = ExitStack()

    def dram(name, shape):
        return nc.dram_tensor(name, shape, F32).ap()

    qk_rows = dram("qk_rows", [2, IN_COLS, T])
    cum_rows = dram("cum_rows", [NH, 4, T])
    slots_in = dram("slots_in", [IN_ROWS, D])
    slots_out = dram("slots_out", [OUT_ROWS, D])

    with ctx:
        def sb(name, shape, dt=F32, to=None):
            return (to or ctx).enter_context(nc.sbuf_tensor(name, shape, dt))

        def sem(name):
            return ctx.enter_context(nc.semaphore(name))

        link = Chain(nc.vector, sem("s_chain"))
        then = Chain(nc.gpsimd, sem("s_pool"))
        bank = ctx.enter_context(nc.psum_tensor("bank", [P, 8, 512], F32))

        ident = sb("ident", [P, P])
        ones = sb("ones", [P, P])
        earlier = sb("earlier", [P, P])
        mod_cols = sb("mod_cols", [P, 48])
        gain_attn = sb("gain_attn", [P, 8])
        gain_moe = sb("gain_moe", [P, 8])
        param_cols = sb("param_cols", [P, 72])
        gate_attn = sb("gate_attn", [P, D])
        gate_moe = sb("gate_moe", [P, D])
        eps_col = sb("eps_col", [P, 1])
        row_gate = sb("row_gate", [P, NT, 2])
        row_slot = sb("row_slot", [P, NT, 2], I32)
        row_out = sb("row_out", [P, NT, 2], I32)
        starts = sb("starts", [1, NE], I32)

        proj = ExitStack()
        heads = ExitStack()
        kcvc = heads.enter_context(nc.sbuf_tensor("kcvc", [P, T], F32))
        v_tok = heads.enter_context(nc.sbuf_tensor("v_tok", [P, NT, VW], F32))

        pj = lambda name, shape, dt=F32: proj.enter_context(nc.sbuf_tensor(name, shape, dt))
        params = pj("params", [72, P])
        cond = pj("cond", [P, 8])
        cond_e = pj("cond_e", [P, 8])
        cond_wide = pj("cond_wide", [P, 8, P])
        xt = pj("xt", [P, 4, D])
        squares = pj("squares", [P, D])
        ss = pj("ss", [P, 3, NT])
        ht = pj("ht", [P, DC, T])
        win = pj("win", [P, DC, IN_COLS])
        ada = pj("ada", [P, ADA_RING, DC, SL])
        stage = pj("stage", [P, 4, 512])
        zeros = squares

        s_param = sem("s_param")
        s_param_t = sem("s_param_t")
        s_const = sem("s_const")
        s_eps = sem("s_eps")
        s_cond = sem("s_cond")
        s_cexp = sem("s_cexp")
        s_x = [sem(f"s_x{i}") for i in range(4)]
        s_ada = [sem(f"s_ada{i}") for i in range(ADA_RING)]
        s_ada_used = sem("s_ada_used")
        s_win = sem("s_win")
        s_sq = sem("s_sq")
        s_sd = sem("s_sd")
        s_xn = sem("s_xn")
        s_tr = sem("s_tr")
        s_ht_a = sem("s_ht_a")
        s_ht_v = sem("s_ht_v")
        s_mod = sem("s_mod")
        s_row_ev = sem("s_row_ev")
        s_rt = sem("s_rt")
        s_rt_a = sem("s_rt_a")
        s_rt_v = sem("s_rt_v")
        s_store = [sem(f"s_store{i}") for i in range(4)]
        s_tk = sem("s_tk")
        s_tk_v = sem("s_tk_v")
        s_bias = sem("s_bias")
        s_zero = sem("s_zero")
        s_zfill = sem("s_zfill")
        s_split = sem("s_split")

        ada_v = ada_w[0].rearrange("(k p) n -> p k n", p=P)
        win_v = w_in[0].rearrange("(k p) n -> p k n", p=P)
        x_v = x[0].rearrange("(t p) d -> p t d", p=P)
        N_RT = 2 * len(ROW_TILES)
        CMP_TILE = 13

        def stored_before(i):
            return sum(1 for j in range(i) if j // 2 != CMP_TILE)

        def uses_before(i):
            return sum(1 for j in range(i % 4, i, 4) if j // 2 != CMP_TILE)

        parts = lambda i: xt[:, i % 4, :].bitcast(F32R).rearrange("p (a n) -> p a n", a=2)

        def slice_section(s):
            return s * SL // D

        with nc.Block() as block:
            @block.sync
            def _(sp):
                sp.dma_start(params[0:48, :], ada_b[0].rearrange("(m p) -> m p", p=P)).then_inc(s_param, 16)
                sp.dma_start(params[48:56, :], norm_attn_g[0].rearrange("(m p) -> m p", p=P)).then_inc(s_param, 16)
                sp.dma_start(params[56:64, :], norm_moe_g[0].rearrange("(m p) -> m p", p=P)).then_inc(s_param, 16)
                sp.dma_start(params[64:72, :], c[0].rearrange("(m p) -> m p", p=P)).then_inc(s_param, 16)
                for s in range(N_SL):
                    if s < 4:
                        sp.dma_start(xt[:, s, :], x_v[:, s, :]).then_inc(s_x[s], 16)
                    if s >= ADA_RING:
                        sp.wait_ge(s_ada_used, s - ADA_RING + 1)
                    sp.dma_start(ada[:, s % ADA_RING, :, :], ada_v[:, :, s * SL:(s + 1) * SL]).then_inc(
                        s_ada[s % ADA_RING], 16)
                    if s == 8 + ADA_RING - 1:
                        for t in range(4, NT):
                            if t == 4:
                                sp.wait_ge(s_tr, 8)
                            sp.dma_start(xt[:, t - 4, :], x_v[:, t, :]).then_inc(s_x[t - 4], 16)

            @block.gpsimd
            def _(pool):
                for k in range(DC):
                    pool.dma_start(win[:, k, 0:C_KW], win_v[:, k, 0:C_KW]).then_inc(s_win, 16)
                for dst, src, w in ((C_KW, C_VS, 64), (C_VS, C_KW, 64), (C_VW, C_VW, IN_COLS - C_VW)):
                    pool.dma_start(win[:, :, dst:dst + w], win_v[:, :, src:src + w]).then_inc(s_win, 16)
                pool.dma_start(gate_attn[:, :], ada_b[0:1, 2 * D:3 * D].to_broadcast([P, D])).then_inc(s_bias, 16)
                pool.dma_start(gate_moe[:, :], ada_b[0:1, 5 * D:6 * D].to_broadcast([P, D])).then_inc(s_bias, 16)
                then(pool.memset(ident[:, :], 0.0))
                then(pool.affine_select(out=ident[:, :], in_=ident[:, :], compare_op=ALU.not_equal, fill=1.0,
                                        base=0, pattern=[[-1, P]], channel_multiplier=1))
                then(pool.memset(ones[:, :], 1.0))
                pool.sem_inc(s_const, 1)
                then(pool.affine_select(out=earlier[:, :], in_=ones[:, :], compare_op=ALU.is_gt, fill=0.0,
                                        base=0, pattern=[[1, P]], channel_multiplier=-1))
                for i in range(N_RT):
                    if i // 2 == CMP_TILE:
                        continue
                    m, half = i // 2, i % 2
                    c0 = ROW_TILES[m][0]
                    cols = slice(half * 512, half * 512 + 512)
                    pool.wait_ge(s_split, stored_before(i) + 1)
                    pool.dma_start(qk_rows[:, c0:c0 + P, cols].rearrange("a p n -> p a n"), parts(i).bitcast(F32)).then_inc(s_store[i % 4], 16)
                pool.wait_ge(s_zero, 1)
                pool.dma_start(slots_in[2 * T:IN_ROWS, :], zeros[:, :]).then_inc(s_zfill, 16)
                pool.dma_start(slots_out[2 * T:OUT_ROWS, :].rearrange("(p r) d -> p r d", p=P),
                               zeros[:, :].rearrange("p (a d) -> p a d", a=1).to_broadcast(
                                   [P, (OUT_ROWS - 2 * T) // P, D])).then_inc(s_zfill, 16)

            @block.tensor
            def _(pe):
                pe.wait_ge(s_param, 64)
                pe.wait_ge(s_const, 1)
                pe.transpose(bank[:, 0, 0:72], params[:, :], ident[0:72, 0:72]).then_inc(s_param_t, 1)
                rows_done = 0

                def ada_slice(s):
                    nonlocal rows_done
                    sec = slice_section(s)
                    pe.wait_ge(s_ada[s % ADA_RING], 16 * (s // ADA_RING + 1))
                    if sec in (2, 5):
                        if rows_done >= 2:
                            pe.wait_ge(s_row_ev, rows_done - 1)
                        o = bank[:, 2 + rows_done % 2, 0:SL]
                        for k in range(DC):
                            mm = pe.matmul(o, cond_wide[:, k, :], ada[:, s % ADA_RING, k, :],
                                           start=(k == 0), stop=(k == DC - 1))
                        rows_done += 1
                    else:
                        for m in range(SL // P):
                            col = sec * 8 + (s * SL % D) // P + m
                            o = bank[:, 1 if sec < 2 else 0, 128 + col:129 + col]
                            for k in range(DC):
                                mm = pe.matmul(o, ada[:, s % ADA_RING, k, m * P:(m + 1) * P], cond[:, k:k + 1],
                                               start=(k == 0), stop=(k == DC - 1))
                    return mm

                pe.wait_ge(s_cond, 2)
                for s in range(8):
                    ada_slice(s).then_inc(s_ada_used, 1)
                n = 0
                for g in range(2):
                    for k in range(DC):
                        for i in range(4):
                            t = 4 * g + i
                            if k == 0:
                                pe.wait_ge(s_xn, t + 1)
                            if i == 0 and n >= 2:
                                pe.wait_ge((s_ht_a, s_ht_v)[n % 2], n // 2)
                            mm = pe.transpose(bank[:, 2 + n % 2, i * P:(i + 1) * P], xt[:, i, k * P:(k + 1) * P], ident[:, :])
                        mm.then_inc(s_tr, 1)
                        n += 1
                pe.wait_ge(s_win, 16 * (DC + 3))
                pe.wait_ge(s_ht_a, 8)
                pe.wait_ge(s_ht_v, 8)
                for i in range(N_RT):
                    m, half = i // 2, i % 2
                    c0 = ROW_TILES[m][0]
                    if i >= 2:
                        pe.wait_ge((s_rt_a, s_rt_v)[i % 2], i // 2)
                    for k in range(DC):
                        mm = pe.matmul(bank[:, 4 + i % 2, :], win[:, k, c0:c0 + P], ht[:, k, half * 512:half * 512 + 512],
                                       start=(k == 0), stop=(k == DC - 1))
                    mm.then_inc(s_rt, 1)
                for i in range(2 * NT):
                    t, b = i // 2, i % 2
                    if i >= 2:
                        pe.wait_ge(s_tk_v, i - 1)
                    at = 0
                    for c0, w in TOKEN_RUNS[b]:
                        for k in range(DC):
                            mm = pe.matmul(bank[:, 6 + b, at:at + w], ht[:, k, t * P:(t + 1) * P], win[:, k, c0:c0 + w],
                                           start=(k == 0), stop=(k == DC - 1))
                        at += w
                    mm.then_inc(s_tk, 1)
                for s in range(8, N_SL):
                    ada_slice(s).then_inc(s_ada_used, 1)

            @block.scalar
            def _(act):
                act.wait_ge(s_cond, 1)
                act.activation(cond_e[:, :], param_cols[:, 64:72], ACT.Exp, scale=-1.0).then_inc(s_cexp, 1)
                act.wait_ge(s_eps, 1)
                n = 0
                for t in range(NT):
                    act.wait_ge(s_x[t % 4], 16 * (t // 4 + 1))
                    act.activation(squares[:, :], xt[:, t % 4, :], ACT.Square, accum_out=ss[:, 0, t:t + 1]).then_inc(s_sq, 1)
                    act.wait_ge(s_sq, t + 1)
                    act.activation(ss[:, 1, t:t + 1], ss[:, 0, t:t + 1], ACT.Sqrt, bias=eps_col[:, :], scale=1.0 / D).then_inc(s_sd, 1)
                    if t == 3:
                        act.wait_ge(s_mod, 1)
                        for k in range(0, DC, 2):
                            act.wait_ge(s_tr, k + 1)
                            act.activation(ht[:, k, 0:512], bank[:, 2, :], ACT.Identity, bias=mod_cols[:, k:k + 1],
                                           scale=gain_attn[:, k:k + 1]).then_inc(s_ht_a, 1)
                act.sem_inc(s_zero, 1)
                for k in range(0, DC, 2):
                    act.wait_ge(s_tr, 8 + k + 1)
                    act.activation(ht[:, k, 512:1024], bank[:, 2, :], ACT.Identity, bias=mod_cols[:, k:k + 1],
                                   scale=gain_attn[:, k:k + 1]).then_inc(s_ht_a, 1)
                for i in range(0, N_RT, 2):
                    m = i // 2
                    act.wait_ge(s_rt, i + 1)
                    if m == CMP_TILE:
                        act.copy(kcvc[:, 0:512], bank[:, 4, :]).then_inc(s_rt_a, 1)
                        continue
                    if i >= 4:
                        act.wait_ge(s_split, stored_before(i - 3))
                    act.mul(stage[:, i % 4, :], bank[:, 4, :], ROW_TILES[m][1]).then_inc(s_rt_a, 1)

            @block.vector
            def _(dve):
                dve.memset(eps_col[:, :], EPS).then_inc(s_eps, 1)
                dve.wait_ge(s_param_t, 1)
                link(dve.tensor_copy(param_cols[:, :], bank[:, 0, 0:72]))
                dve.sem_inc(s_cond, 1)
                dve.wait_ge(s_cexp, 1)
                link(dve.tensor_scalar(cond_e[:, :], cond_e[:, :], 1.0, None, ALU.add))
                link(dve.reciprocal(cond_e[:, :], cond_e[:, :]))
                link(dve.tensor_tensor(cond[:, :], param_cols[:, 64:72], cond_e[:, :], ALU.mult))
                dve.wait_ge(s_const, 1)
                for k in range(DC):
                    last = dve.tensor_scalar(cond_wide[:, k, :], ones[:, :], cond[:, k:k + 1], None, ALU.mult)
                last.then_inc(s_cond, 1)

                def normalise(t):
                    dve.wait_ge(s_sd, t + 1)
                    link(dve.reciprocal(ss[:, 2, t:t + 1], ss[:, 1, t:t + 1]))
                    dve.tensor_scalar(xt[:, t % 4, :], xt[:, t % 4, :], ss[:, 2, t:t + 1], None, ALU.mult).then_inc(s_xn, 1)

                for t in range(4):
                    normalise(t)
                dve.wait_ge(s_ada_used, 8)
                link(dve.tensor_tensor(mod_cols[:, 0:16], bank[:, 1, 128:144], param_cols[:, 0:16], ALU.add))
                link(dve.tensor_scalar(gain_attn[:, :], mod_cols[:, 8:16], 1.0, None, ALU.add))
                link(dve.tensor_tensor(gain_attn[:, :], gain_attn[:, :], param_cols[:, 48:56], ALU.mult))
                dve.sem_inc(s_mod, 1)
                for g in range(2):
                    for k in range(1, DC, 2):
                        dve.wait_ge(s_tr, 8 * g + k + 1)
                        dve.tensor_scalar(ht[:, k, g * 512:g * 512 + 512], bank[:, 3, :], gain_attn[:, k:k + 1],
                                          mod_cols[:, k:k + 1], ALU.mult, ALU.add).then_inc(s_ht_v, 1)
                    if g == 0:
                        for t in range(4, NT):
                            normalise(t)
                dve.wait_ge(s_zero, 1)
                dve.memset(zeros[:, :], 0.0).then_inc(s_zero, 1)
                for i in range(N_RT):
                    m = i // 2
                    if i % 2:
                        dve.wait_ge(s_rt, i + 1)
                        if m == CMP_TILE:
                            dve.tensor_copy(kcvc[:, 512:1024], bank[:, 5, :]).then_inc(s_rt_v, 1)
                            continue
                        dve.tensor_scalar(stage[:, i % 4, :], bank[:, 5, :], ROW_TILES[m][1], None, ALU.mult).then_inc(s_rt_v, 1)
                        dve.wait_ge(s_rt_v, i // 2 + 1)
                    elif m == CMP_TILE:
                        continue
                    else:
                        dve.wait_ge(s_rt_a, i // 2 + 1)
                    if uses_before(i):
                        dve.wait_ge(s_store[i % 4], 16 * uses_before(i))
                    link(dve.tensor_copy(parts(i)[:, 0, :], stage[:, i % 4, :]))
                    dve.tensor_tensor(parts(i)[:, 1, :], stage[:, i % 4, :], parts(i)[:, 0, :], ALU.subtract).then_inc(s_split, 1)
                for i in range(2 * NT):
                    t, b = i // 2, i % 2
                    w = (VA, VW - VA)[b]
                    dve.wait_ge(s_tk, i + 1)
                    dve.tensor_copy(v_tok[:, t, b * VA:b * VA + w], bank[:, 6 + b, 0:w]).then_inc(s_tk_v, 1)
                rows = 0
                dve.wait_ge(s_bias, 32)
                for s in range(8, N_SL):
                    if slice_section(s) in (2, 5):
                        o = (gate_attn if slice_section(s) == 2 else gate_moe)[:, s * SL % D:s * SL % D + SL]
                        dve.wait_ge(s_ada_used, s + 1)
                        dve.tensor_tensor(o, bank[:, 2 + rows % 2, 0:SL], o, ALU.add).then_inc(s_row_ev, 1)
                        rows += 1
                dve.wait_ge(s_ada_used, N_SL)
                link(dve.tensor_tensor(mod_cols[:, 24:40], bank[:, 0, 152:168], param_cols[:, 24:40], ALU.add))
                link(dve.tensor_scalar(gain_moe[:, :], mod_cols[:, 32:40], 1.0, None, ALU.add))
                link(dve.tensor_tensor(gain_moe[:, :], gain_moe[:, :], param_cols[:, 56:64], ALU.mult))
        proj.close()

        y = heads.enter_context(nc.sbuf_tensor("y", [P, NT, D], F32))
        kc_t = heads.enter_context(nc.sbuf_tensor("kc_t", [P, NC], F32))
        vc = heads.enter_context(nc.sbuf_tensor("vc", [NC, HD], F32))
        nsa_gate = heads.enter_context(nc.sbuf_tensor("nsa_gate", [P, NT, 3 * NH], F32))
        neg_lam = heads.enter_context(nc.sbuf_tensor("neg_lam", [P, 1], F32))
        dist_full = heads.enter_context(nc.sbuf_tensor("dist_full", [P, T], F32))
        dist_win = heads.enter_context(nc.sbuf_tensor("dist_win", [P, 640], F32))
        dist_swa = heads.enter_context(nc.sbuf_tensor("dist_swa", [P, 256], F32))
        dist_cmp = heads.enter_context(nc.sbuf_tensor("dist_cmp", [P, 119], F32))
        causal = heads.enter_context(nc.sbuf_tensor("causal", [P, T], F32))
        row_seen = heads.enter_context(nc.sbuf_tensor("row_seen", [P, 1], F32))
        comp = ExitStack()
        cp = lambda name, shape, dt=F32: comp.enter_context(nc.sbuf_tensor(name, shape, dt))
        w1 = cp("w1", [P, 32, P])
        pos_rows = cp("pos_rows", [64, HD])
        pos = cp("pos", [P, 32])
        b1 = cp("b1", [P, 2])
        w2 = cp("w2", [P, 3, HD])
        blocks_t = cp("blocks_t", [P, 32, NC])
        hid = cp("hid", [P, 2 * NC])
        hid_a = cp("hid_a", [P, 2 * NC])
        bf = cp("bf", [P, NH])
        fz = cp("fz", [P, 8, NT, NH])
        f_t = cp("f_t", [NH, 2, T])
        cum = cp("cum", [NH, T])
        cum_hl = cp("cum_hl", [NH, 4, T], F32R)
        lam_in = cp("lam_in", [P, 4, 32])
        lam = cp("lam", [P, 4])
        ge = cp("ge", [P, NT, 12])

        s_ld2 = sem("s_ld2")
        s_post = sem("s_post")
        s_pos = sem("s_pos")
        s_blk = sem("s_blk")
        s_hid = sem("s_hid")
        s_a2 = sem("s_a2")
        s_v2 = sem("s_v2")
        s_hid2 = sem("s_hid2")
        s_kc = sem("s_kc")
        s_ft = sem("s_ft")
        s_f = sem("s_f")
        s_cum = sem("s_cum")
        s_cumst = sem("s_cumst")

        with nc.Block() as block:
            @block.sync
            def _(sp):
                for h in range(2):
                    sp.dma_start(w1[64 * h:64 * h + 64, :, :], nsa_cmp_w1[0, h].rearrange("(j d) o -> d j o", d=HD)).then_inc(s_ld2, 16)
                sp.dma_start(pos_rows[:, :], nsa_cmp_pos[0].rearrange("h j d -> (h j) d")).then_inc(s_ld2, 16)
                sp.dma_start(b1[:, :], nsa_cmp_b1[0].rearrange("h o -> o h"), allow_slow_non_contiguous=True).then_inc(s_ld2, 16)
                sp.dma_start(w2[:, 1:3, :], nsa_cmp_w2[0].rearrange("h o d -> o h d")).then_inc(s_ld2, 16)
                sp.dma_start(w2[:, 0, :], nsa_cmp_w2[0, 0]).then_inc(s_ld2, 16)
                sp.dma_start(bf[:, :], fox_forget_b[0:1, :].to_broadcast([P, NH])).then_inc(s_ld2, 16)
                for i, v in enumerate((diff_lam_q1, diff_lam_k1, diff_lam_q2, diff_lam_k2)):
                    sp.dma_start(lam_in[:, i, :], v[0:1, :].to_broadcast([P, 32])).then_inc(s_ld2, 16)
                sp.wait_ge(s_cum, 1)
                sp.dma_start(cum_rows, cum_hl[:, :, :].bitcast(F32)).then_inc(s_cumst, 16)
                sp.wait_ge(s_cumst, 16)
                for i in range(4):
                    uses = sum(1 for j in range(i, N_RT, 4) if j // 2 != CMP_TILE)
                    sp.wait_ge(s_store[i], 16 * uses)
                sp.wait_ge(s_zfill, 32)

            @block.gpsimd
            def _(pool):
                then(pool.iota(dist_full[:, :], pattern=[[-1, T]], base=T - P, channel_multiplier=1,
                               allow_small_or_imprecise_dtypes=True))
                then(pool.affine_select(out=dist_full[:, :], in_=dist_full[:, :], compare_op=ALU.is_ge, fill=BIG,
                                        base=T - P, pattern=[[-1, T]], channel_multiplier=1))
                then(pool.affine_select(out=dist_win[:, :], in_=dist_full[:, T - 640:], compare_op=ALU.is_gt, fill=BIG,
                                        base=0, pattern=[[1, 640]], channel_multiplier=-1))
                then(pool.affine_select(out=dist_swa[:, :], in_=dist_full[:, T - 256:], compare_op=ALU.is_gt, fill=BIG,
                                        base=0, pattern=[[1, 256]], channel_multiplier=-1))
                then(pool.iota(dist_cmp[:, :], pattern=[[-16, 119]], base=16 * 56 - 31, channel_multiplier=1,
                               allow_small_or_imprecise_dtypes=True))
                then(pool.affine_select(out=dist_cmp[:, :], in_=dist_cmp[:, :], compare_op=ALU.is_ge, fill=BIG,
                                        base=16 * 56 - 31, pattern=[[-16, 119]], channel_multiplier=1))
                then(pool.memset(causal[:, :], 0.0))
                then(pool.affine_select(out=causal[:, :], in_=causal[:, :], compare_op=ALU.is_ge, fill=-1e30,
                                        base=T - P, pattern=[[-1, T]], channel_multiplier=1))
                then(pool.memset(row_seen[:, :], 1.0))
                then(pool.affine_select(out=row_seen[:, :], in_=row_seen[:, :], compare_op=ALU.is_ge, fill=0.0,
                                        base=-31, pattern=[[0, 1]], channel_multiplier=1))

            @block.tensor
            def _(pe):
                pe.wait_ge(s_ld2, 176)
                pe.transpose(bank[0:64, 0, 0:64], pos_rows[:, :], ident[0:64, 0:64]).then_inc(s_post, 1)
                pe.wait_ge(s_blk, 1)
                for h in range(2):
                    for j in range(32):
                        mm = pe.matmul(bank[:, 2 + h, 0:NC], w1[64 * h:64 * h + 64, j, :],
                                       blocks_t[64 * h:64 * h + 64, j, :], start=(j == 0), stop=(j == 31))
                mm.then_inc(s_hid, 1)
                pe.wait_ge(s_f, 1)
                for t in range(NT):
                    mm = pe.transpose(bank[0:NH, 4 + t // 4, t % 4 * P:t % 4 * P + P], fz[:, 7, t, :], ident[:, :])
                mm.then_inc(s_ft, 1)
                pe.wait_ge(s_hid2, 1)
                pe.matmul(bank[:, 6, 0:NC], w2[:, 0:2, :].rearrange("p a d -> p (a d)"), hid[:, 0:NC], start=True, stop=True)
                pe.matmul(bank[0:NC, 7, 0:HD], hid[:, NC:2 * NC], w2[:, 2, :], start=True, stop=True).then_inc(s_kc, 1)

            @block.scalar
            def _(act):
                act.activation(ge[:, :, :], v_tok[:, :, V_G:V_G + 12], ACT.Exp, scale=-1.0).then_inc(s_a2, 1)
                act.wait_ge(s_v2, 1)
                act.activation(fz[:, 2, :, :], fz[:, 1, :, :], ACT.Exp).then_inc(s_a2, 1)
                act.wait_ge(s_v2, 2)
                act.activation(lam[:, 0:2], lam[:, 0:2], ACT.Exp).then_inc(s_a2, 1)
                act.wait_ge(s_v2, 3)
                act.activation(hid_a[:, :], hid_a[:, :], ACT.Exp, scale=-2.0 * (2.0 / 3.141592653589793) ** 0.5).then_inc(s_a2, 1)
                act.wait_ge(s_v2, 4)
                act.activation(fz[:, 4, :, :], fz[:, 3, :, :], ACT.Ln).then_inc(s_a2, 1)

            @block.vector
            def _(dve):
                dve.wait_ge(s_ld2, 176)
                z = fz[:, 0, :, :]
                link(dve.tensor_tensor(z, v_tok[:, :, V_FF:V_FF + NH],
                                       bf[:, :].rearrange("p (a h) -> p a h", a=1).to_broadcast([P, NT, NH]), ALU.add))
                link(dve.tensor_scalar(fz[:, 1, :, :], z, -1.0, None, ALU.mult))
                link(dve.tensor_tensor(fz[:, 1, :, :], fz[:, 1, :, :], z, ALU.min))
                dve.sem_inc(s_v2, 1)
                link(dve.tensor_tensor(lam_in[:, 0, :], lam_in[:, 0, :], lam_in[:, 1, :], ALU.mult))
                link(dve.tensor_tensor(lam_in[:, 2, :], lam_in[:, 2, :], lam_in[:, 3, :], ALU.mult))
                link(dve.reduce_sum(lam[:, 0:1], lam_in[:, 0, :], AX_X))
                link(dve.reduce_sum(lam[:, 1:2], lam_in[:, 2, :], AX_X))
                dve.sem_inc(s_v2, 1)
                dve.wait_ge(s_post, 1)
                link(dve.tensor_copy(pos[0:64, :], bank[0:64, 0, 0:32]))
                link(dve.tensor_copy(pos[64:P, :], bank[0:64, 0, 32:64]))
                kv3 = kcvc[:, :].rearrange("p (n b) -> p b n", b=16)
                for a in range(2):
                    link(dve.tensor_tensor(blocks_t[:, 16 * a:16 * a + 16, :], kv3[:, :, a:a + NC],
                                           pos[:, 16 * a:16 * a + 16].rearrange("p (j a) -> p j a", a=1).to_broadcast([P, 16, NC]),
                                           ALU.add))
                dve.sem_inc(s_blk, 1)
                dve.wait_ge(s_a2, 2)
                link(dve.tensor_scalar(fz[:, 3, :, :], fz[:, 2, :, :], 1.0, None, ALU.add))
                dve.wait_ge(s_a2, 1)
                link(dve.tensor_scalar(ge[:, :, :], ge[:, :, :], 1.0, None, ALU.add))
                link(dve.reciprocal(nsa_gate[:, :, :], ge[:, :, :]))
                dve.wait_ge(s_a2, 3)
                link(dve.tensor_tensor(lam[:, 2:3], lam[:, 1:2], lam[:, 0:1], ALU.subtract))
                link(dve.tensor_scalar(neg_lam[:, :], lam[:, 2:3], -LAM_INIT, None, ALU.add))
                dve.wait_ge(s_hid, 1)
                for h in range(2):
                    link(dve.tensor_scalar(hid[:, h * NC:h * NC + NC], bank[:, 2 + h, 0:NC], b1[:, h:h + 1], None, ALU.add))
                link(dve.tensor_tensor(hid_a[:, :], hid[:, :], hid[:, :], ALU.mult))
                link(dve.tensor_scalar(hid_a[:, :], hid_a[:, :], 0.044715, 1.0, ALU.mult, ALU.add))
                link(dve.tensor_tensor(hid_a[:, :], hid_a[:, :], hid[:, :], ALU.mult))
                dve.sem_inc(s_v2, 1)
                dve.wait_ge(s_a2, 4)
                link(dve.tensor_scalar(hid_a[:, :], hid_a[:, :], 1.0, None, ALU.add))
                link(dve.reciprocal(hid_a[:, :], hid_a[:, :]))
                link(dve.tensor_tensor(hid[:, :], hid[:, :], hid_a[:, :], ALU.mult))
                dve.sem_inc(s_hid2, 1)
                dve.sem_inc(s_v2, 1)
                e, w, lw = fz[:, 2, :, :], fz[:, 3, :, :], fz[:, 4, :, :]
                is_one, den = fz[:, 5, :, :], fz[:, 6, :, :]
                dve.wait_ge(s_a2, 5)
                link(dve.tensor_scalar(den, w, -1.0, None, ALU.add))
                link(dve.tensor_scalar(is_one, den, 0.0, None, ALU.is_equal))
                link(dve.tensor_tensor(den, den, is_one, ALU.add))
                link(dve.tensor_tensor(lw, lw, is_one, ALU.add))
                link(dve.reciprocal(den, den))
                link(dve.tensor_tensor(lw, lw, e, ALU.mult))
                link(dve.tensor_tensor(lw, lw, den, ALU.mult))
                link(dve.tensor_scalar(z, z, 0.0, None, ALU.min))
                link(dve.tensor_tensor(fz[:, 7, :, :], z, lw, ALU.subtract))
                dve.sem_inc(s_f, 1)
                link(dve.memset(f_t[:, 1, :], 1.0))
                dve.wait_ge(s_ft, 1)
                link(dve.tensor_copy(f_t[:, 0, :], bank[0:NH, 4:6, :].rearrange("p a b -> p (a b)")))
                link(dve.tensor_tensor_scan(cum[:, :], f_t[:, 1, :], f_t[:, 0, :], 0.0, ALU.mult, ALU.add))
                link(dve.tensor_copy(cum_hl[:, 2, :], cum[:, :]))
                link(dve.tensor_tensor(cum_hl[:, 3, :], cum[:, :], cum_hl[:, 2, :], ALU.subtract))
                link(dve.tensor_scalar(cum_hl[:, 0:2, :], cum_hl[:, 2:4, :], -1.0, None, ALU.mult))
                dve.sem_inc(s_cum, 1)
                dve.wait_ge(s_kc, 1)
                link(dve.tensor_copy(kc_t[:, :], bank[:, 6, 0:NC]))
                link(dve.tensor_copy(vc[:, :], bank[0:NC, 7, 0:HD]))
        comp.close()

        att = ExitStack()
        at_ = lambda name, shape, dt=F32: att.enter_context(nc.sbuf_tensor(name, shape, dt))
        qb = [at_(f"qb{i}", [P, T], F32R) for i in range(2)]
        ka = [at_(f"ka{i}", [P, T], F32R) for i in range(2)]
        kb = [at_(f"kb{i}", [P, T], F32R) for i in range(2)]
        cq = [at_(f"cq{i}", [4, T], F32R) for i in range(2)]
        ck = [at_(f"ck{i}", [4, T], F32R) for i in range(2)]
        neg_slope = at_("neg_slope", [P, 2])
        sink = at_("sink", [P, 2])
        neg_sink = at_("neg_sink", [P, 2])
        sink_exp = at_("sink_exp", [P, 8])
        bias = at_("bias", [P, 2, T])
        probs = at_("probs", [P, 2, T])
        probs_t = at_("probs_t", [P, 2, 8, P])
        low = at_("low", [P, 8])
        total = at_("total", [P, 8])
        factor = at_("factor", [P, 8])
        spare = at_("spare", [P, 2])
        nil = at_("nil", [P, 1])
        first_map = at_("first_map", [P, NT, HD])

        attend(nc, sem, dict(
            bank=bank, ident=ident, qb=qb, ka=ka, kb=kb, cq=cq, ck=ck, neg_slope=neg_slope, sink=sink, neg_sink=neg_sink,
            sink_exp=sink_exp, bias=bias, probs=probs, probs_t=probs_t, low=low, total=total, factor=factor,
            first_map=first_map, spare=spare, nil=nil, y=y, v_tok=v_tok, kc_t=kc_t, vc=vc, nsa_gate=nsa_gate, neg_lam=neg_lam,
            row_seen=row_seen, causal=causal, dist_full=dist_full, dist_win=dist_win, dist_swa=dist_swa,
            dist_cmp=dist_cmp, qk_rows=qk_rows, cum_rows=cum_rows, neg_slopes=neg_slopes, swa_sinks=swa_sinks))
        att.close()

        po = ExitStack()
        tail = ExitStack()
        o_ = lambda name, shape, dt=F32: po.enter_context(nc.sbuf_tensor(name, shape, dt))
        wo = o_("wo", [P, DC, D])
        y_t = o_("y_t", [P, DC, T])
        sub = o_("sub", [P, NT, NH, HD])
        sub_s = o_("sub_s", [P, 3, NT * NH])
        sub_g = o_("sub_g", [P, HD])
        xr = o_("xr", [P, 4, D])
        x1_d = dram("x1_rows", [T, D])
        x1_v = x1_d.rearrange("(t p) d -> p t d", p=P)
        s_wo = sem("s_wo")
        s_sub = sem("s_sub")
        s_sqr = sem("s_sqr")
        s_yn = sem("s_yn")
        s_yt = sem("s_yt")
        s_yt_a = sem("s_yt_a")
        s_yt_v = sem("s_yt_v")
        s_wout = sem("s_wout")
        s_x1_done = sem("s_x1_done")
        s_xr = [sem(f"s_xr{i}") for i in range(4)]
        s_x1st = [sem(f"s_x1st{i}") for i in range(4)]
        with nc.Block() as block:
            @block.sync
            def _(sp):
                sp.dma_start(sub_g[:, :], diff_subln_g[0:1, :].to_broadcast([P, HD])).then_inc(s_sub, 16)
                for k in range(DC):
                    sp.dma_start(wo[:, k, :], w_out[0, k * P:(k + 1) * P, :]).then_inc(s_wo, 16)
                for t in range(NT):
                    if t >= 4:
                        sp.wait_ge(s_x1st[t % 4], 16 * (t // 4))
                    sp.dma_start(xr[:, t % 4, :], x_v[:, t, :]).then_inc(s_xr[t % 4], 16)

            @block.gpsimd
            def _(pool):
                for t in range(NT):
                    pool.wait_ge(s_x1_done, t + 1)
                    pool.dma_start(x1_v[:, t, :], xr[:, t % 4, :]).then_inc(s_x1st[t % 4], 16)
                for i in range(4):
                    pool.wait_ge(s_x1st[i], 32)

            @block.tensor
            def _(pe):
                n = 0
                for k in (2, 3, 4, 5, 6, 7, 0, 1):
                    if k == 0:
                        pe.wait_ge(s_yn, 1)
                    for g in range(2):
                        if n >= 2:
                            pe.wait_ge((s_yt_a, s_yt_v)[n % 2], n // 2)
                        for i in range(4):
                            mm = pe.transpose(bank[:, n % 2, i * P:(i + 1) * P], y[:, 4 * g + i, k * P:(k + 1) * P], ident[:, :])
                        mm.then_inc(s_yt, 1)
                        n += 1
                pe.wait_ge(s_yt_a, 8)
                pe.wait_ge(s_yt_v, 8)
                pe.wait_ge(s_wo, 16 * DC)
                for t in range(NT):
                    if t >= 2:
                        pe.wait_ge(s_x1_done, t - 1)
                    for half in range(2):
                        for k in range(DC):
                            mm = pe.matmul(bank[:, 2 + 2 * (t % 2) + half, :], y_t[:, k, t * P:(t + 1) * P],
                                           wo[:, k, half * 512:half * 512 + 512], start=(k == 0), stop=(k == DC - 1))
                    mm.then_inc(s_wout, 1)

            @block.scalar
            def _(act):
                act.wait_ge(s_sqr, 1)
                act.activation(sub_s[:, 1, :], sub_s[:, 0, :], ACT.Sqrt, bias=eps_col[:, :], scale=1.0 / HD).then_inc(s_sqr, 1)
                order = [(k, g) for k in (2, 3, 4, 5, 6, 7, 0, 1) for g in range(2)]
                for n in range(0, 16, 2):
                    k, g = order[n]
                    act.wait_ge(s_yt, n + 1)
                    act.copy(y_t[:, k, g * 512:g * 512 + 512], bank[:, 0, :]).then_inc(s_yt_a, 1)

            @block.vector
            def _(dve):
                yd = y[:, :, 0:NH * HD].rearrange("p t (h d) -> p t h d", h=NH)
                for t in range(NT):
                    link(dve.tensor_tensor(sub[:, t, :, :], yd[:, t, :, :], yd[:, t, :, :], ALU.mult))
                link(dve.reduce_sum(sub_s[:, 0, :], sub[:, :, :, :].rearrange("p t h d -> p (t h) d"), AX_X))
                dve.sem_inc(s_sqr, 1)
                dve.wait_ge(s_sub, 16)
                link(dve.tensor_scalar(sub_g[:, :], sub_g[:, :], 1.0 - LAM_INIT, None, ALU.mult))
                dve.wait_ge(s_sqr, 2)
                link(dve.reciprocal(sub_s[:, 2, :], sub_s[:, 1, :]))
                for t in range(NT):
                    r = sub_s[:, 2, t * NH:(t + 1) * NH].rearrange("p (h a) -> p h a", a=1).to_broadcast([P, NH, HD])
                    link(dve.tensor_tensor(yd[:, t, :, :], yd[:, t, :, :], r, ALU.mult))
                    link(dve.tensor_tensor(yd[:, t, :, :], yd[:, t, :, :],
                                           sub_g[:, :].rearrange("p (a d) -> p a d", a=1).to_broadcast([P, NH, HD]), ALU.mult))
                dve.sem_inc(s_yn, 1)
                order = [(k, g) for k in (2, 3, 4, 5, 6, 7, 0, 1) for g in range(2)]
                for m in range(1, 16, 2):
                    k, g = order[m]
                    dve.wait_ge(s_yt, m + 1)
                    dve.tensor_copy(y_t[:, k, g * 512:g * 512 + 512], bank[:, 1, :]).then_inc(s_yt_v, 1)
                for t in range(NT):
                    dve.wait_ge(s_wout, t + 1)
                    dve.wait_ge(s_xr[t % 4], 16 * (t // 4 + 1))
                    acc = bank[:, 2 + 2 * (t % 2):4 + 2 * (t % 2), :].rearrange("p a b -> p (a b)")
                    o = sub[:, 4 * (t % 2):4 * (t % 2) + 4, :, :].rearrange("p a b c -> p (a b c)")
                    link(dve.tensor_tensor(o, acc, gate_attn[:, :], ALU.mult))
                    dve.tensor_tensor(xr[:, t % 4, :], xr[:, t % 4, :], o, ALU.add).then_inc(s_x1_done, 1)
        po.close()
        heads.close()

        rt = ExitStack()
        over = ctx.enter_context(nc.sbuf_tensor("over", [1, 64], I32))
        r_ = lambda name, shape, dt=F32: rt.enter_context(nc.sbuf_tensor(name, shape, dt))
        xn = r_("xn", [P, NT, D])
        h2_t = r_("h2_t", [P, DC, T])
        sq2 = r_("sq2", [P, D])
        rs2 = r_("rs2", [P, 3, NT])
        rw = r_("rw", [P, DC, NE])
        rb = r_("rb", [P, NE])
        aff = r_("aff", [P, NT, NE])
        sel = r_("sel", [P, NT, NE])
        top = r_("top", [P, NT, 8, 8])
        gsum = r_("gsum", [P, NT, 8])
        gmax = r_("gmax", [P, NT, 8])
        gidx = r_("gidx", [P, NT, 8], U32)
        gidx_f = r_("gidx_f", [P, NT, 8])
        keep = r_("keep", [P, NT, NE])
        hot = r_("hot", [P, 2, NT, NE])
        both = r_("both", [P, NT, NE])
        before = r_("before", [P, NT, NE])
        tmp = r_("tmp", [P, NT, NE])
        iota_e = r_("iota_e", [P, NE])
        iota_g = r_("iota_g", [P, NE])
        steps = r_("steps", [P, 8])
        counts = r_("counts", [P, NE])
        cmp8 = r_("cmp8", [P, NE, 8])
        first = r_("first", [P, NE])
        ov_row = r_("ov_row", [P, NE])
        ovn = r_("ovn", [P, NE])
        ov_end = r_("ov_end", [P, NE])
        ov_base = r_("ov_base", [P, NE])
        ones_row = r_("ones_row", [P, NE])
        iota_b = r_("iota_b", [1, NOV_T])
        ended = r_("ended", [1, NOV_T, NE])
        begun = r_("begun", [1, NOV_T, NE])
        over_f = r_("over_f", [1, 2 * NOV_T + 1])
        rank = r_("rank", [P, NT, 8])
        slot_f = r_("slot_f", [P, NT, 2])
        s_ld4 = sem("s_ld4")
        s_x1r = [sem(f"s_x1r{i}") for i in range(NT)]
        s_iota = sem("s_iota")
        s_sq4 = sem("s_sq4")
        s_sd4 = sem("s_sd4")
        s_xn4 = sem("s_xn4")
        s_tr4 = sem("s_tr4")
        s_h_a = sem("s_h_a")
        s_h_v = sem("s_h_v")
        s_log = sem("s_log")
        s_sig = sem("s_sig")
        s_both = sem("s_both")
        s_pre = sem("s_pre")
        s_slot = sem("s_slot")
        s_starts = sem("s_starts")
        s_scat = sem("s_scat")
        with nc.Block() as block:
            @block.sync
            def _(sp):
                for t in range(NT):
                    sp.dma_start(xn[:, t, :], x1_v[:, t, :]).then_inc(s_x1r[t], 16)
                sp.dma_start(rw[:, :, :], router_w.rearrange("(k p) e -> p k e", p=P)).then_inc(s_ld4, 16)
                sp.dma_start(rb[:, :], router_b.rearrange("(a e) -> a e", a=1).to_broadcast([P, NE])).then_inc(s_ld4, 16)

            @block.gpsimd
            def _(pool):
                imp = dict(allow_small_or_imprecise_dtypes=True)
                pool.iota(iota_e[:, :], pattern=[[1, NE]], base=0, channel_multiplier=0, **imp).then_inc(s_iota, 1)
                pool.iota(iota_g[:, :], pattern=[[1, 8], [0, 8]], base=0, channel_multiplier=0, **imp).then_inc(s_iota, 1)
                pool.iota(steps[:, :], pattern=[[EB, 8]], base=EB, channel_multiplier=0, **imp).then_inc(s_iota, 1)
                pool.iota(iota_b[:, :], pattern=[[1, NOV_T]], base=0, channel_multiplier=0, **imp).then_inc(s_iota, 1)
                pool.memset(ones_row[:, :], 1.0).then_inc(s_iota, 1)
                pool.wait_ge(s_slot, 1)
                for t in range(NT):
                    for j in range(2):
                        pool.indirect_dma_start(
                            out=slots_in, out_offset=bass.IndirectOffsetOnAxis(ap=row_slot[:, t, j:j + 1].bitcast(U32), axis=0),
                            in_=xn[:, t, :], in_offset=None).then_inc(s_scat, 16)
                pool.wait_ge(s_scat, 16 * 2 * NT)

            @block.tensor
            def _(pe):
                n = 0
                for g in range(2):
                    for k in range(DC):
                        for i in range(4):
                            t = 4 * g + i
                            if k == 0:
                                pe.wait_ge(s_xn4, t + 1)
                            if i == 0 and n >= 2:
                                pe.wait_ge((s_h_a, s_h_v)[n % 2], n // 2)
                            mm = pe.transpose(bank[:, n % 2, i * P:(i + 1) * P], xn[:, t, k * P:(k + 1) * P], ident[:, :])
                        mm.then_inc(s_tr4, 1)
                        n += 1
                    pe.wait_ge(s_h_a, 4 * g + 4)
                    pe.wait_ge(s_h_v, 4 * g + 4)
                    pe.wait_ge(s_ld4, 32)
                    for i in range(4):
                        t = 4 * g + i
                        for k in range(DC):
                            mm = pe.matmul(bank[:, 2, t * NE:(t + 1) * NE], h2_t[:, k, t * P:(t + 1) * P], rw[:, k, :],
                                           start=(k == 0), stop=(k == DC - 1))
                mm.then_inc(s_log, 1)
                pe.wait_ge(s_both, 1)
                for t in range(NT):
                    for u in range(t):
                        pe.matmul(bank[:, 3, t * NE:(t + 1) * NE], ones[:, :], both[:, u, :], start=(u == 0), stop=False)
                    pe.matmul(bank[:, 3, t * NE:(t + 1) * NE], earlier[:, :], both[:, t, :], start=(t == 0), stop=True)
                for u in range(NT):
                    mm = pe.matmul(bank[:, 4, 0:NE], ones[:, :], both[:, u, :], start=(u == 0), stop=(u == NT - 1))
                mm.then_inc(s_pre, 1)

            @block.scalar
            def _(act):
                for t in range(NT):
                    act.wait_ge(s_x1r[t], 16)
                    act.activation(sq2[:, :], xn[:, t, :], ACT.Square, accum_out=rs2[:, 0, t:t + 1]).then_inc(s_sq4, 1)
                    act.wait_ge(s_sq4, t + 1)
                    act.activation(rs2[:, 1, t:t + 1], rs2[:, 0, t:t + 1], ACT.Sqrt, bias=eps_col[:, :], scale=1.0 / D).then_inc(s_sd4, 1)
                for n in range(0, 16, 2):
                    k, g = n % 8, n // 8
                    act.wait_ge(s_tr4, n + 1)
                    act.activation(h2_t[:, k, g * 512:g * 512 + 512], bank[:, 0, :], ACT.Identity, bias=mod_cols[:, 24 + k:25 + k],
                                   scale=gain_moe[:, k:k + 1]).then_inc(s_h_a, 1)
                act.wait_ge(s_log, 1)
                act.activation(aff[:, :, :].rearrange("p t e -> p (t e)"), bank[:, 2, :], ACT.Exp, scale=-1.0).then_inc(s_sig, 1)

            @block.vector
            def _(dve):
                def wide(ap, shape, spec, **kw):
                    return ap.rearrange(spec, **kw).to_broadcast(shape)

                def norm(t):
                    dve.wait_ge(s_sd4, t + 1)
                    link(dve.reciprocal(rs2[:, 2, t:t + 1], rs2[:, 1, t:t + 1]))
                    dve.tensor_scalar(xn[:, t, :], xn[:, t, :], rs2[:, 2, t:t + 1], None, ALU.mult).then_inc(s_xn4, 1)

                for t in range(NT):
                    norm(t)
                for m in range(1, 16, 2):
                    k, g = m % 8, m // 8
                    dve.wait_ge(s_tr4, m + 1)
                    dve.tensor_scalar(h2_t[:, k, g * 512:g * 512 + 512], bank[:, 1, :], gain_moe[:, k:k + 1],
                                      mod_cols[:, 24 + k:25 + k], ALU.mult, ALU.add).then_inc(s_h_v, 1)
                dve.wait_ge(s_sig, 1)
                dve.wait_ge(s_ld4, 32)
                link(dve.tensor_scalar(aff[:, :, :], aff[:, :, :], 1.0, None, ALU.add))
                link(dve.reciprocal(aff[:, :, :], aff[:, :, :]))
                link(dve.tensor_tensor(sel[:, :, :], aff[:, :, :], wide(rb[:, :], [P, NT, NE], "p (a e) -> p a e", a=1), ALU.add))
                for t in range(NT):
                    for g in range(8):
                        last = dve.max(out=top[:, t, g, :], in_=sel[:, t, 8 * g:8 * g + 8])
                link(last)
                link(dve.tensor_tensor(gsum[:, :, :], top[:, :, :, 0], top[:, :, :, 1], ALU.add))
                for t in range(NT):
                    last = dve.max(out=gmax[:, t, :], in_=gsum[:, t, :])
                link(last)
                for t in range(NT):
                    last = dve.max_index(out=gidx[:, t, :], in_max=gmax[:, t, :], in_values=gsum[:, t, :])
                link(last)
                link(dve.tensor_copy(gidx_f[:, :, :], gidx[:, :, :]))
                dve.wait_ge(s_iota, 5)
                link(dve.tensor_tensor(keep[:, :, :], wide(iota_g[:, :], [P, NT, NE], "p (a e) -> p a e", a=1),
                                       gidx_f[:, :, 0:1].to_broadcast([P, NT, NE]), ALU.is_equal))
                link(dve.tensor_tensor(sel[:, :, :], sel[:, :, :], keep[:, :, :], ALU.mult))
                link(dve.tensor_scalar(keep[:, :, :], keep[:, :, :], -1.0, 1e30, ALU.add, ALU.mult))
                link(dve.tensor_tensor(sel[:, :, :], sel[:, :, :], keep[:, :, :], ALU.add))
                for t in range(NT):
                    last = dve.max(out=gmax[:, t, :], in_=sel[:, t, :])
                link(last)
                for t in range(NT):
                    last = dve.max_index(out=gidx[:, t, :], in_max=gmax[:, t, :], in_values=sel[:, t, :])
                link(last)
                link(dve.tensor_copy(gidx_f[:, :, :], gidx[:, :, :]))
                for j in range(2):
                    link(dve.tensor_tensor(hot[:, j, :, :], wide(iota_e[:, :], [P, NT, NE], "p (a e) -> p a e", a=1),
                                           gidx_f[:, :, j:j + 1].to_broadcast([P, NT, NE]), ALU.is_equal))
                link(dve.tensor_tensor(both[:, :, :], hot[:, 0, :, :], hot[:, 1, :, :], ALU.add))
                dve.sem_inc(s_both, 1)

                def pick(o, table, j):
                    link(dve.tensor_tensor(tmp[:, :, :], hot[:, j, :, :], table, ALU.mult))
                    link(dve.reduce_sum(o, tmp[:, :, :], AX_X))

                for j in range(2):
                    pick(rank[:, :, j], aff[:, :, :], j)
                link(dve.tensor_tensor(rank[:, :, 2], rank[:, :, 0], rank[:, :, 1], ALU.add))
                link(dve.reciprocal(rank[:, :, 2], rank[:, :, 2]))
                for j in range(2):
                    link(dve.tensor_tensor(row_gate[:, :, j], rank[:, :, j], rank[:, :, 2], ALU.mult))
                dve.wait_ge(s_pre, 1)
                link(dve.tensor_copy(before[:, :, :].rearrange("p t e -> p (t e)"), bank[:, 3, :]))
                link(dve.tensor_copy(counts[:, :], bank[:, 4, 0:NE]))
                link(dve.tensor_tensor_scan(first[:, :], ones_row[:, :], counts[:, :], 0.0, ALU.mult, ALU.add))
                link(dve.tensor_tensor(first[:, :], first[:, :], counts[:, :], ALU.subtract))
                dve.tensor_copy(starts[:, :], first[0:1, :]).then_inc(s_starts, 1)
                wide_e = lambda ap: wide(ap, [P, NT, NE], "p (a e) -> p a e", a=1)

                def slots(o, table):
                    for j in range(2):
                        pick(o[:, :, j], table, j)

                link(dve.tensor_tensor(keep[:, :, :], before[:, :, :], wide_e(first[:, :]), ALU.add))
                slots(slot_f, keep[:, :, :])
                link(dve.tensor_copy(row_slot[:, :, :], slot_f[:, :, :]))
                dve.sem_inc(s_slot, 1)
                link(dve.tensor_tensor(cmp8[:, :, :], wide(counts[:, :], [P, NE, 8], "p (e a) -> p e a", a=1),
                                       wide(steps[:, :], [P, NE, 8], "p (a s) -> p a s", a=1), ALU.is_gt))
                link(dve.reduce_sum(ovn[:, :], cmp8[:, :, :], AX_X))
                link(dve.tensor_tensor_scan(ov_end[:, :], ones_row[:, :], ovn[:, :], 0.0, ALU.mult, ALU.add))
                link(dve.tensor_tensor(ov_base[:, :], ov_end[:, :], ovn[:, :], ALU.subtract))
                cmp_b = lambda ap: (wide(ap, [1, NOV_T, NE], "p (a e) -> p a e", a=1),
                                    wide(iota_b[:, :], [1, NOV_T, NE], "p (b a) -> p b a", a=1))
                link(dve.tensor_tensor(ended[:, :, :], *cmp_b(ov_end[0:1, :]), ALU.is_le))
                link(dve.reduce_sum(over_f[:, 0:NOV_T], ended[:, :, :], AX_X))
                link(dve.tensor_scalar(over_f[:, 0:NOV_T], over_f[:, 0:NOV_T], float(NE - 1), None, ALU.min))
                link(dve.tensor_scalar(ov_row[:, :], ov_base[:, :], float(EB), None, ALU.mult))
                link(dve.tensor_tensor(ov_row[:, :], first[:, :], ov_row[:, :], ALU.subtract))
                link(dve.tensor_tensor(begun[:, :, :], *cmp_b(ov_base[0:1, :]), ALU.is_le))
                link(dve.tensor_tensor(begun[:, :, :], begun[:, :, :], ended[:, :, :], ALU.subtract))
                link(dve.tensor_tensor(begun[:, :, :], begun[:, :, :], wide(ov_row[0:1, :], [1, NOV_T, NE], "p (a e) -> p a e", a=1), ALU.mult))
                link(dve.reduce_sum(over_f[:, NOV_T:2 * NOV_T], begun[:, :, :], AX_X))
                link(dve.tensor_scalar(iota_b[:, :], iota_b[:, :], float(EB), float(EB), ALU.mult, ALU.add))
                link(dve.tensor_tensor(over_f[:, NOV_T:2 * NOV_T], over_f[:, NOV_T:2 * NOV_T], iota_b[:, :], ALU.add))
                link(dve.tensor_copy(over_f[:, 2 * NOV_T:2 * NOV_T + 1], ov_end[0:1, NE - 1:NE]))
                link(dve.tensor_copy(over[:, 0:2 * NOV_T + 1], over_f[:, :]))
                link(dve.tensor_scalar(ov_row[:, :], ov_row[:, :], -1.0, float(IN_ROWS - EB), ALU.mult, ALU.add))
                link(dve.tensor_scalar(before[:, :, :], before[:, :, :], float(EB), None, ALU.is_ge))
                link(dve.tensor_tensor(before[:, :, :], before[:, :, :], wide_e(ov_row[:, :]), ALU.mult))
                link(dve.tensor_tensor(keep[:, :, :], keep[:, :, :], before[:, :, :], ALU.add))
                slots(slot_f, keep[:, :, :])
                link(dve.tensor_copy(row_out[:, :, :], slot_f[:, :, :]))
        rt.close()

        ex = ExitStack()
        e_ = lambda name, shape, dt=F32: ex.enter_context(nc.sbuf_tensor(name, shape, dt))
        wg = [e_(f"wg{i}", [P, DC, DF]) for i in range(2)]
        wu = [e_(f"wu{i}", [P, DC, DF]) for i in range(2)]
        wd = [e_(f"wd{i}", [P, FC, D]) for i in range(2)]
        xe = [e_(f"xe{i}", [EB, D]) for i in range(2)]
        xe_mid = e_("xe_mid", [P, DC, EB])
        xe_t = e_("xe_t", [P, DC, EB])
        act_h = [e_(f"act_h{i}", [EB, DF]) for i in range(2)]
        act_t = e_("act_t", [P, FC, EB])
        oe = e_("oe", [EB, D])
        gate_v = exp_w_gate[0].rearrange("e (k p) f -> e p k f", p=P)
        up_v = exp_w_up[0].rearrange("e (k p) f -> e p k f", p=P)
        down_v = exp_w_down[0].rearrange("e (k p) d -> e p k d", p=P)
        wide_gain = lambda: gain_moe[:, :].rearrange("p (k a) -> p k a", a=1).to_broadcast([P, DC, EB])
        wide_shift = lambda: mod_cols[:, 24:32].rearrange("p (k a) -> p k a", a=1).to_broadcast([P, DC, EB])

        s_gu = [sem(f"s_gu{i}") for i in range(2)]
        s_dn = [sem(f"s_dn{i}") for i in range(2)]
        s_xe = [sem(f"s_xe{i}") for i in range(2)]
        s_xt5 = sem("s_xt5")
        s_xt_ok = sem("s_xt_ok")
        s_gu_done = sem("s_gu_done")
        s_e5 = sem("s_e5")
        s_t5 = sem("s_t5")
        s_d5 = sem("s_d5")
        s_r5 = sem("s_r5")
        s_g5 = sem("s_g5")
        s_h5 = sem("s_h5")
        s_ht5 = sem("s_ht5")
        s_hc5 = sem("s_hc5")
        s_down = sem("s_down")
        s_oe_a = sem("s_oe_a")
        s_oe_v = sem("s_oe_v")
        s_out5 = sem("s_out5")
        gate_up = [bank[:, 2 * i:2 * i + 2, :] for i in range(2)]
        rows_t = bank[:, 4:6, :].rearrange("p a b -> p (a b)")
        DOWN, ACT_T = 6, 7

        def transposed_rows(pe, buf):
            for k in range(DC):
                mm = pe.transpose(rows_t[:, k * EB:(k + 1) * EB], xe[buf][:, k * P:(k + 1) * P], ident[:, :])
            return mm

        def gate_and_up(pe, buf):
            for i, w in enumerate((wg[buf], wu[buf])):
                for k in range(DC):
                    mm = pe.matmul(gate_up[buf][:, i, :], xe_t[:, k, :], w[:, k, :], start=(k == 0), stop=(k == DC - 1))
            return mm

        def transposed_act(pe, buf):
            for m in range(FC):
                mm = pe.transpose(bank[:, ACT_T, m * EB:(m + 1) * EB], act_h[buf][:, m * P:(m + 1) * P], ident[:, :])
            return mm

        def down(pe, buf):
            for half in range(2):
                for m in range(FC):
                    mm = pe.matmul(bank[:, DOWN + half, :], act_t[:, m, :], wd[buf][:, m, half * 512:half * 512 + 512],
                                   start=(m == 0), stop=(m == FC - 1))
            return mm

        def modulate(dve, s_mid, mid, s_done):
            rows = rows_t.rearrange("p (k t) -> p k t", k=DC)
            dve.tensor_tensor(xe_mid[:, :, :], rows, wide_gain(), ALU.mult).then_inc(s_mid, 1)
            dve.wait_ge(s_mid, mid)
            dve.tensor_tensor(xe_t[:, :, :], xe_mid[:, :, :], wide_shift(), ALU.add).then_inc(s_done, 1)

        def exp_gate(act, buf, s_done):
            act.activation(act_h[buf][:, :], gate_up[buf][:, 0, :], ACT.Exp, scale=-1.0).then_inc(s_done, 1)

        def silu_times_up(dve, buf, sems, value, s_done):
            h = act_h[buf][:, :]
            dve.tensor_scalar(h, h, 1.0, None, ALU.add).then_inc(sems[0], 1)
            dve.wait_ge(sems[0], value)
            dve.reciprocal(h, h).then_inc(sems[1], 1)
            dve.wait_ge(sems[1], value)
            dve.tensor_tensor(h, h, gate_up[buf][:, 0, :], ALU.mult).then_inc(sems[2], 1)
            dve.wait_ge(sems[2], value)
            dve.tensor_tensor(h, h, gate_up[buf][:, 1, :], ALU.mult).then_inc(s_done, 1)

        def row_start(eng, n):
            return eng.value_load(starts[0:1, ds(n, 1)], min_val=0, max_val=2 * T)

        with nc.Block() as block:
            @block.sync
            def _(sp):
                def load_gate_up(n, b):
                    sp.wait_ge(s_gu_done, n + 1)
                    sp.dma_start(wg[b][:, :, :], gate_v[ds(n, 1)].rearrange("a p k f -> p (a k) f")).then_inc(s_gu[b], 16)
                    sp.dma_start(wu[b][:, :, :], up_v[ds(n, 1)].rearrange("a p k f -> p (a k) f")).then_inc(s_gu[b], 16)

                def load_down(n, b):
                    sp.wait_ge(s_down, n + 1)
                    sp.dma_start(wd[b][:, :, :], down_v[ds(n, 1)].rearrange("a p k d -> p (a k) d")).then_inc(s_dn[b], 16)

                load_gate_up(0, 0)
                with sp.Fori(0, NE // 2 - 1) as it:
                    for b in range(2):
                        load_gate_up(it * 2 + b + 1, 1 - b)
                        load_down(it * 2 + b, b)
                load_gate_up(NE - 1, 1)
                load_down(NE - 2, 0)
                load_down(NE - 1, 1)

            @block.tensor
            def _(pe):
                pe.sem_inc(s_gu_done, 2)
                pe.sem_inc(s_down, 2)
                for n in range(2):
                    pe.wait_ge(s_xe[n], 16)
                    if n == 1:
                        pe.wait_ge(s_xt_ok, 1)
                        pe.wait_ge(s_gu[0], 32)
                        gate_and_up(pe, 0).then_inc(s_gu_done, 1)
                    transposed_rows(pe, n).then_inc(s_xt5, 1)

                def step(n, b, gu_loads, dn_loads, xe_loads):
                    pe.wait_ge(s_gu[b], gu_loads)
                    pe.wait_ge(s_xt_ok, n + 1)
                    pe.wait_ge(s_h5, n)
                    gate_and_up(pe, b).then_inc(s_gu_done, 1)
                    pe.wait_ge(s_h5, n + 1)
                    pe.wait_ge(s_oe_v, n)
                    pe.wait_ge(s_oe_a, n)
                    transposed_act(pe, 1 - b).then_inc(s_ht5, 1)
                    if xe_loads is not None:
                        pe.wait_ge(s_xe[1 - b], xe_loads)
                        transposed_rows(pe, 1 - b).then_inc(s_xt5, 1)
                    pe.wait_ge(s_dn[1 - b], dn_loads)
                    pe.wait_ge(s_hc5, n)
                    down(pe, 1 - b).then_inc(s_down, 1)

                with pe.Fori(0, NE // 2 - 1) as it:
                    step(it * 2 + 1, 1, it * 32 + 32, it * 16 + 16, it * 16 + 32)
                    step(it * 2 + 2, 0, it * 32 + 64, it * 16 + 16, it * 16 + 32)
                step(NE - 1, 1, 16 * NE, 8 * NE, None)
                pe.wait_ge(s_h5, NE + 1)
                pe.wait_ge(s_oe_v, NE)
                pe.wait_ge(s_oe_a, NE)
                transposed_act(pe, 1).then_inc(s_ht5, 1)
                pe.wait_ge(s_dn[1], 8 * NE)
                pe.wait_ge(s_hc5, NE)
                down(pe, 1).then_inc(s_down, 1)

            @block.scalar
            def _(act):
                act.sem_inc(s_oe_a, 1)
                act.sem_inc(s_out5, 16)
                for b in range(2):
                    act.dma_start(xe[b][:, :], slots_in[ds(row_start(act, b), EB), :]).then_inc(s_xe[b], 16)
                act.wait_ge(s_gu_done, 3)
                exp_gate(act, 0, s_e5)

                def rest(n):
                    act.wait_ge(s_ht5, n)
                    act.copy(act_t[:, :, :].rearrange("p m t -> p (m t)"), bank[:, ACT_T, :]).then_inc(s_hc5, 1)
                    act.wait_ge(s_down, n + 2)
                    act.wait_ge(s_out5, n * 16)
                    act.copy(oe[:, 0:512], bank[:, DOWN, :]).then_inc(s_oe_a, 1)
                    act.wait_ge(s_oe_a, n + 1)
                    act.wait_ge(s_oe_v, n + 1)
                    act.dma_start(slots_out[ds(row_start(act, n - 1), EB), :], oe[:, :]).then_inc(s_out5, 16)

                with act.Fori(0, NE // 2 - 1) as it:
                    for b in (1, 0):
                        n = it * 2 + 2 - b
                        act.wait_ge(s_xt5, n)
                        act.dma_start(xe[1 - b][:, :], slots_in[ds(row_start(act, n + 1), EB), :]).then_inc(s_xe[1 - b], 16)
                        act.wait_ge(s_gu_done, n + 3)
                        exp_gate(act, b, s_e5)
                        rest(n)
                act.wait_ge(s_gu_done, NE + 2)
                exp_gate(act, 1, s_e5)
                rest(NE - 1)
                rest(NE)
                act.wait_ge(s_out5, 16 * (NE + 1))

            @block.vector
            def _(dve):
                dve.sem_inc(s_oe_v, 1)
                dve.sem_inc(s_h5, 1)
                silu = (s_d5, s_r5, s_g5)
                dve.wait_ge(s_xt5, 1)
                modulate(dve, s_t5, 1, s_xt_ok)
                dve.wait_ge(s_xt5, 2)
                modulate(dve, s_t5, 2, s_xt_ok)
                dve.wait_ge(s_e5, 1)
                silu_times_up(dve, 0, silu, 1, s_h5)

                def copy_out(n):
                    dve.wait_ge(s_down, n + 2)
                    dve.wait_ge(s_out5, n * 16)
                    dve.tensor_copy(oe[:, 512:1024], bank[:, ACT_T, :]).then_inc(s_oe_v, 1)

                with dve.Fori(0, NE // 2 - 1) as it:
                    for b in (1, 0):
                        n = it * 2 + 2 - b
                        dve.wait_ge(s_xt5, n + 2)
                        modulate(dve, s_t5, n + 2, s_xt_ok)
                        dve.wait_ge(s_e5, n + 1)
                        silu_times_up(dve, b, silu, n + 1, s_h5)
                        copy_out(n)
                dve.wait_ge(s_e5, NE)
                silu_times_up(dve, 1, silu, NE, s_h5)
                copy_out(NE - 1)
                copy_out(NE)

        s_v_load = sem("s_v_load")
        s_v_t = sem("s_v_t")
        s_v_mid = sem("s_v_mid")
        s_v_x = sem("s_v_x")
        s_v_gu = sem("s_v_gu")
        s_v_e = sem("s_v_e")
        s_v_3 = [sem(f"s_v_3{i}") for i in range(3)]
        s_v_h = sem("s_v_h")
        s_v_ht = sem("s_v_ht")
        s_v_hc = sem("s_v_hc")
        s_v_dn = sem("s_v_dn")
        s_v_o = sem("s_v_o")
        s_v_st = sem("s_v_st")
        s_v_end = sem("s_v_end")
        with nc.Block() as block:
            def used_blocks(eng):
                count = eng.value_load(over[0:1, 2 * NOV_T:2 * NOV_T + 1], min_val=0, max_val=NOV)
                return count

            @block.sync
            def _(sp):
                count = used_blocks(sp)
                sp.sem_inc(s_v_st, 16)
                with sp.Fori(0, NOV) as n:
                    with sp.If(n < count):
                        e = sp.value_load(over[0:1, ds(n, 1)], min_val=0, max_val=NE - 1)
                        start = sp.value_load(over[0:1, ds(n + NOV_T, 1)], min_val=0, max_val=2 * T)
                        sp.wait_ge(s_v_st, n * 16 + 16)
                        sp.dma_start(wg[0][:, :, :], gate_v[ds(e, 1)].rearrange("a p k f -> p (a k) f")).then_inc(s_v_load, 16)
                        sp.dma_start(wu[0][:, :, :], up_v[ds(e, 1)].rearrange("a p k f -> p (a k) f")).then_inc(s_v_load, 16)
                        sp.dma_start(wd[0][:, :, :], down_v[ds(e, 1)].rearrange("a p k d -> p (a k) d")).then_inc(s_v_load, 16)
                        sp.dma_start(xe[0][:, :], slots_in[ds(start, EB), :]).then_inc(s_v_load, 16)
                        sp.wait_ge(s_v_o, n + 1)
                        sp.dma_start(slots_out[ds(n * EB + IN_ROWS, EB), :], oe[:, :]).then_inc(s_v_st, 16)

            @block.tensor
            def _(pe):
                count = used_blocks(pe)
                with pe.Fori(0, NOV) as n:
                    with pe.If(n < count):
                        pe.wait_ge(s_v_load, n * 64 + 64)
                        pe.matmul(bank[:, 7, 0:P], ident[:, :], ident[:, :], start=True, stop=True)
                        transposed_rows(pe, 0).then_inc(s_v_t, 1)
                        pe.wait_ge(s_v_x, n + 1)
                        gate_and_up(pe, 0).then_inc(s_v_gu, 1)
                        pe.wait_ge(s_v_h, n + 1)
                        transposed_act(pe, 0).then_inc(s_v_ht, 1)
                        pe.wait_ge(s_v_hc, n + 1)
                        down(pe, 0).then_inc(s_v_dn, 1)

            @block.scalar
            def _(act):
                count = used_blocks(act)
                with act.Fori(0, NOV) as n:
                    with act.If(n < count):
                        act.wait_ge(s_v_gu, n + 1)
                        exp_gate(act, 0, s_v_e)
                        act.wait_ge(s_v_ht, n + 1)
                        act.copy(act_t[:, :, :].rearrange("p m t -> p (m t)"), bank[:, ACT_T, :]).then_inc(s_v_hc, 1)
                act.wait_ge(s_v_st, count * 16 + 16)
                act.copy(act_h[1][:, 0:1], ones[:, 0:1]).then_inc(s_v_end, 1)

            @block.vector
            def _(dve):
                count = used_blocks(dve)
                with dve.Fori(0, NOV) as n:
                    with dve.If(n < count):
                        dve.wait_ge(s_v_t, n + 1)
                        modulate(dve, s_v_mid, n + 1, s_v_x)
                        dve.wait_ge(s_v_e, n + 1)
                        silu_times_up(dve, 0, s_v_3, n + 1, s_v_h)
                        dve.wait_ge(s_v_dn, n + 1)
                        dve.tensor_copy(oe[:, :], bank[:, 6:8, :].rearrange("p a b -> p (a b)")).then_inc(s_v_o, 1)
        ex.close()

        RING = 3
        c_ = lambda name, shape, dt=F32: ctx.enter_context(nc.sbuf_tensor(name, shape, dt))
        x1 = c_("x1", [P, NT, D])
        row_a = c_("row_a", [P, RING, D])
        row_b = c_("row_b", [P, RING, D])
        sq6 = c_("sq6", [P, D])
        g_fin = c_("g_fin", [P, D])
        rs6 = c_("rs6", [P, 3, NT])
        s_x6 = sem("s_x6")
        s_g6 = sem("s_g6")
        s_rows = [sem(f"s_rows{i}") for i in range(RING)]
        s_ga = sem("s_ga")
        s_x2_done = sem("s_x2_done")
        s_sq6 = sem("s_sq6")
        s_sd6 = sem("s_sd6")
        s_fin = sem("s_fin")
        s_out = sem("s_out")
        out_v = out[0].rearrange("(t p) d -> p t d", p=P)
        with nc.Block() as block:
            @block.sync
            def _(sp):
                for t in range(NT):
                    sp.dma_start(x1[:, t, :], x1_v[:, t, :]).then_inc(s_x6, 16)
                sp.dma_start(g_fin[:, :], norm_final_g.rearrange("(a d) -> a d", a=1).to_broadcast([P, D])).then_inc(s_g6, 16)
                for t in range(NT):
                    sp.wait_ge(s_fin, t + 1)
                    sp.dma_start(out_v[:, t, :], x1[:, t, :]).then_inc(s_out, 16)
                sp.wait_ge(s_out, 16 * NT)

            @block.gpsimd
            def _(pool):
                for t in range(NT):
                    if t >= RING:
                        pool.wait_ge(s_x2_done, t - RING + 1)
                    for j, r in enumerate((row_a, row_b)):
                        pool.indirect_dma_start(
                            out=r[:, t % RING, :], out_offset=None, in_=slots_out,
                            in_offset=bass.IndirectOffsetOnAxis(ap=row_out[:, t, j:j + 1].bitcast(U32), axis=0)).then_inc(s_rows[t % RING], 16)

            @block.scalar
            def _(act):
                def weigh(t):
                    act.wait_ge(s_rows[t % RING], 32 * (t // RING + 1))
                    act.activation(row_a[:, t % RING, :], row_a[:, t % RING, :], ACT.Copy, scale=row_gate[:, t, 0:1]).then_inc(s_ga, 1)

                weigh(0)
                for t in range(NT):
                    if t + 1 < NT:
                        weigh(t + 1)
                    act.wait_ge(s_x2_done, t + 1)
                    act.activation(sq6[:, :], x1[:, t, :], ACT.Square, accum_out=rs6[:, 0, t:t + 1]).then_inc(s_sq6, 1)
                    act.wait_ge(s_sq6, t + 1)
                    act.activation(rs6[:, 1, t:t + 1], rs6[:, 0, t:t + 1], ACT.Sqrt, bias=eps_col[:, :], scale=1.0 / D).then_inc(s_sd6, 1)

            @block.vector
            def _(dve):
                def finish(t):
                    dve.wait_ge(s_sd6, t + 1)
                    link(dve.reciprocal(rs6[:, 2, t:t + 1], rs6[:, 1, t:t + 1]))
                    dve.scalar_tensor_tensor(out=x1[:, t, :], in0=x1[:, t, :], scalar=rs6[:, 2, t:t + 1], in1=g_fin[:, :],
                                             op0=ALU.mult, op1=ALU.mult).then_inc(s_fin, 1)

                dve.wait_ge(s_x6, 16 * NT)
                dve.wait_ge(s_g6, 16)
                for t in range(NT):
                    a, b = row_a[:, t % RING, :], row_b[:, t % RING, :]
                    dve.wait_ge(s_ga, t + 1)
                    link(dve.scalar_tensor_tensor(out=b, in0=b, scalar=row_gate[:, t, 1:2], in1=a, op0=ALU.mult, op1=ALU.add))
                    link(dve.tensor_tensor(b, b, gate_moe[:, :], ALU.mult))
                    dve.tensor_tensor(x1[:, t, :], x1[:, t, :], b, ALU.add).then_inc(s_x2_done, 1)
                    if t >= 1:
                        finish(t - 1)
                finish(NT - 1)


class Mixer:

    def __init__(self, g, before):
        self.g, self.name, self.K, self.prev, self.rounds = g, g["name"], g["k"], g["prev"], g["rounds"]
        self.is_cmp, self.is_fox, self.is_swa, self.is_diff = (self.name == k for k in ("cmp", "fox", "swa", "diff"))
        self.copies = P // self.K
        self.loads = self.copies * (1 if self.is_cmp else 2 if self.is_diff else 3) + (
            not self.is_fox) + self.is_swa + 2 * self.is_fox
        self.steps = before.steps + 16 * before.rounds if before else 0
        self.jobs_biased = before.jobs_biased + 2 * before.rounds * (not before.is_fox) if before else 0
        self.load_sum = before.load_sum + 16 * before.loads * before.rounds if before else 0
        self.splits = before.splits + 8 * before.rounds * (before.prev >= 4) if before else 0
        self.factors = before.factors + before.rounds * before.factors_per_round if before else 0
        self.factors_per_round = 8 if self.is_diff else 16 if "gate" in g else 0

    def span(self, i):
        n = min(i, self.prev) + 1
        return i - n + 1, n

    def width(self, i):
        return NC if self.is_cmp else self.span(i)[1] * P

    def blocks(self, i):
        return 1 if self.is_cmp else self.span(i)[1]


def attend(nc, sem, have):
    bank, ident, qb, ka, kb, cq, ck, neg_slope, sink, neg_sink, sink_exp, bias, probs, probs_t, low, total, factor, first_map, spare, nil, y, \
        v_tok, kc_t, vc, nsa_gate, neg_lam, row_seen, causal, qk_rows, cum_rows, neg_slopes, swa_sinks = (
            have[k] for k in ("bank ident qb ka kb cq ck neg_slope sink neg_sink sink_exp bias probs probs_t low total factor "
                              "first_map spare nil y v_tok kc_t vc nsa_gate neg_lam row_seen causal qk_rows cum_rows "
                              "neg_slopes swa_sinks").split())
    dists = {"diff": have["dist_full"], "sel": have["dist_full"], "win": have["dist_win"], "swa": have["dist_swa"],
             "cmp": have["dist_cmp"]}
    mixers = []
    for g in GROUPS:
        mixers.append(Mixer(g, mixers[-1] if mixers else None))

    s_load = [sem(f"s_load{i}") for i in range(2)]
    s_ones = sem("s_ones")
    s_nsink = sem("s_nsink")
    s_bias7 = sem("s_bias7")
    s_qk = sem("s_qk")
    s_max = sem("s_max")
    s_exp = sem("s_exp")
    s_sink = sem("s_sink")
    s_first = sem("s_first")
    s_tr7 = sem("s_tr7")
    s_cp0 = sem("s_cp0")
    s_cp1 = sem("s_cp1")
    s_pv = sem("s_pv")
    s_den = sem("s_den")
    s_spare = sem("s_spare")
    s_inv = sem("s_inv")
    s_fac = sem("s_fac")
    s_o = sem("s_o")

    with nc.Block() as block:
        def load_job(sp, m, it, b):
            def rows(name, part):
                at, step, within = m.g[name]
                row = ds(it * step + (at + b * within), m.K) if step else slice(at + b * within, at + b * within + m.K)
                return qk_rows[part, row, :]

            for i in range(m.copies):
                to = slice(i * m.K, (i + 1) * m.K)
                sp.dma_start(qb[b][to, :].bitcast(F32), rows("q", i * 2 // m.copies)).then_inc(s_load[b], 16)
                if m.is_diff:
                    sp.dma_start(ka[b][to, :].bitcast(F32), rows("kk", i % 2)).then_inc(s_load[b], 16)
                elif not m.is_cmp:
                    sp.dma_start(ka[b][to, :].bitcast(F32), rows("kk", 0)).then_inc(s_load[b], 16)
                    sp.dma_start(kb[b][to, :].bitcast(F32), rows("kk", 1)).then_inc(s_load[b], 16)
            if not m.is_fox:
                sp.dma_start(neg_slope[:, b:b + 1], neg_slopes[ds(it * 2 + (m.g["job"] + b), 1), :].rearrange("a p -> p a"),
                             allow_slow_non_contiguous=True).then_inc(s_load[b], 16)
            if m.is_swa:
                sp.dma_start(sink[:, b:b + 1], swa_sinks[0:1, ds(it * 2 + b, 1)].to_broadcast([P, 1])).then_inc(s_load[b], 16)
            if m.is_fox:
                head = ds(it * 2 + b, 1)
                sp.dma_start(ck[b][0:2, :].bitcast(F32), cum_rows[head, 0:2, :].rearrange("a i t -> (a i) t")).then_inc(s_load[b], 16)
                sp.dma_start(cq[b][2:4, :].bitcast(F32), cum_rows[head, 2:4, :].rearrange("a i t -> (a i) t")).then_inc(s_load[b], 16)

        @block.sync
        def _(sp):
            for m in mixers:
                if m.is_fox:
                    sp.wait_ge(s_ones, 4)
                with sp.Fori(0, m.rounds) as it:
                    for b in range(2):
                        at = it * 16 + (m.steps + 8 * b + 8)
                        sp.wait_ge(s_qk, at)
                        sp.wait_ge(s_max, at)
                        if m.is_swa:
                            sp.wait_ge(s_sink, at)
                        load_job(sp, m, it, b)

        @block.gpsimd
        def _(pool):
            for n, t in enumerate((*cq, *ck)):
                pool.memset(t[:, :].bitcast(F32), 1.0).then_inc(s_ones, 1)
                pool.wait_ge(s_ones, n + 1)
            pool.memset(nil[:, :], 0.0).then_inc(s_ones, 1)
            pool.wait_ge(s_ones, 5)
            for m in mixers:
                if m.is_fox:
                    continue
                dist = dists[m.name]
                with pool.Fori(0, m.rounds) as it:
                    for b in range(2):
                        pool.wait_ge(s_load[b], it * (16 * m.loads) + (m.load_sum + 16 * m.loads))
                        pool.wait_ge(s_max, it * 16 + (m.steps + 8 * b + 8))
                        if m.is_swa:
                            pool.tensor_tensor(neg_sink[:, b:b + 1], nil[:, :], sink[:, b:b + 1], ALU.subtract).then_inc(s_nsink, 1)
                        pool.tensor_tensor(bias[:, b, 0:dist.shape[1]], dist[:, :],
                                           neg_slope[:, b:b + 1].to_broadcast([P, dist.shape[1]]), ALU.mult).then_inc(s_bias7, 1)

        @block.tensor
        def _(pe):
            pe.sem_inc(s_qk, 16)
            pe.sem_inc(s_tr7, 2)
            pe.sem_inc(s_pv, 2)

            def scores(m, it, k):
                b, i = k // 8, k % 8
                first, _ = m.span(i)
                if i == 0:
                    pe.wait_ge(s_load[b], it * (16 * m.loads) + (m.load_sum + 16 * m.loads))
                pe.wait_ge(s_max, it * 16 + (m.steps + k + 15))
                w = m.width(i)
                for at in range(0, w, 512):
                    keys = slice(first * P + at, first * P + min(w, at + 512))
                    queries = slice(i * P, (i + 1) * P)
                    o = bank[:, 2 * (i % 2) + at // 512, 0:min(w - at, 512)]
                    if m.is_cmp:
                        mm = pe.matmul(o, qb[b][:, queries].bitcast(F32), kc_t[:, :], start=True, stop=True)
                        continue
                    mm = pe.matmul(o, qb[b][:, queries], ka[b][:, keys], start=True, stop=m.is_diff)
                    if not m.is_diff:
                        mm = pe.matmul(o, qb[b][:, queries], kb[b][:, keys], start=False, stop=not m.is_fox)
                    if m.is_fox:
                        mm = pe.matmul(o, cq[b][:, queries], ck[b][:, keys], start=False, stop=True)
                mm.then_inc(s_qk, 1)

            def turn(m, it, k):
                b, i = k // 8, k % 8
                pe.wait_ge(s_exp, it * 16 + (m.steps + k + 1))
                pe.wait_ge(s_cp0, it * 16 + (m.steps + k + 1))
                for j in range(m.blocks(i)):
                    if j == 4:
                        mm.then_inc(s_first, 1)
                        pe.wait_ge(s_cp1, it * 8 + (m.splits + 4 * b + i - 3))
                    mm = pe.transpose(bank[:, 4 + j // 4, j % 4 * P:(j % 4 + 1) * P], probs[:, i % 2, j * P:(j + 1) * P], ident[:, :])
                mm.then_inc(s_tr7, 1)

            def values(m, it, k):
                b, i = k // 8, k % 8
                first, nb = m.span(i)
                pe.wait_ge(s_cp0, it * 16 + (m.steps + k + 2))
                if m.blocks(i) > 4:
                    pe.wait_ge(s_cp1, it * 8 + (m.splits + 4 * b + i - 2))
                pe.wait_ge(s_o, it * 16 + (m.steps + k + 1))
                if m.is_cmp:
                    mm = pe.matmul(bank[:, 6 + i % 2, 0:HD], probs_t[0:NC, i % 2, 0, :], vc[:, :], start=True, stop=True)
                else:
                    v0, vi, vj = m.g["v"]
                    cols = ds(it * vi + (v0 + b * vj), HD) if vi else slice(v0 + b * vj, v0 + b * vj + HD)
                    for j in range(nb):
                        mm = pe.matmul(bank[:, 6 + i % 2, 0:HD], probs_t[:, i % 2, j, :], v_tok[:, first + j, cols],
                                       start=(j == 0), stop=(j == nb - 1))
                mm.then_inc(s_pv, 1)

            for m in mixers:
                with pe.Fori(0, m.rounds) as it:
                    for k in range(18):
                        if k < 16:
                            scores(m, it, k)
                        if 1 <= k < 17:
                            turn(m, it, k - 1)
                        if k >= 2:
                            values(m, it, k - 2)

        @block.scalar
        def _(act):
            act.sem_inc(s_cp0, 1)
            act.sem_inc(s_sink, 16 + next(m.steps for m in mixers if m.is_swa))

            def exponentials(m, it, k):
                i = k % 8
                p = probs[:, i % 2, 0:m.width(i)]
                act.wait_ge(s_max, it * 16 + (m.steps + k + 17))
                act.activation(p, p, ACT.Exp, bias=low[:, i:i + 1], scale=-1.0, accum_out=total[:, i:i + 1]).then_inc(s_exp, 1)
                if m.is_swa:
                    act.activation(sink_exp[:, i:i + 1], sink[:, k // 8:k // 8 + 1], ACT.Exp, bias=low[:, i:i + 1]).then_inc(s_sink, 1)

            def copy_first(m, it, k):
                b, i = k // 8, k % 8
                nb = m.blocks(i)
                if nb > 4:
                    act.wait_ge(s_first, it * 8 + (m.splits + 4 * b + i - 3))
                else:
                    act.wait_ge(s_tr7, it * 16 + (m.steps + k + 3))
                act.wait_ge(s_pv, it * 16 + (m.steps + k + 1))
                kw, w = (NC if m.is_cmp else P), min(nb, 4) * P
                act.copy(probs_t[0:kw, i % 2, 0:min(nb, 4), :].rearrange("p a b -> p (a b)"), bank[0:kw, 4, 0:w]).then_inc(s_cp0, 1)

            for m in mixers:
                with act.Fori(0, m.rounds) as it:
                    for k in range(17):
                        if k < 16:
                            exponentials(m, it, k)
                        if k >= 1:
                            copy_first(m, it, k - 1)

        @block.vector
        def _(dve):
            dve.memset(probs[:, :, :], 0.0).then_inc(s_max, 1)
            dve.wait_ge(s_max, 1)
            dve.sem_inc(s_max, 15)
            dve.sem_inc(s_cp1, 1)
            dve.sem_inc(s_o, 2)

            def reciprocal(m, it, k):
                i = k % 8
                t_, f = total[:, i:i + 1], factor[:, i:i + 1]
                dve.wait_ge(s_exp, it * 16 + (m.steps + k + 1))
                if m.is_swa:
                    dve.wait_ge(s_sink, it * 16 + (m.steps + k + 17))
                    dve.tensor_tensor(t_, t_, sink_exp[:, i:i + 1], ALU.add).then_inc(s_den, 1)
                    dve.wait_ge(s_den, it * 16 + (k + 1))
                dve.reciprocal(f, t_).then_inc(s_inv, 1)

            def maxima(m, it, k):
                b, i = k // 8, k % 8
                w = m.width(i)
                dve.wait_ge(s_qk, it * 16 + (m.steps + k + 17))
                if i == 0 and not m.is_fox:
                    dve.wait_ge(s_bias7, it * 2 + (m.jobs_biased + b + 1))
                dve.wait_ge(s_tr7, it * 16 + (m.steps + k + 1))
                if m.is_cmp:
                    add = bias[:, b, 56 - 8 * i:56 - 8 * i + NC]
                elif m.is_fox:
                    add = causal[:, T - w:T]
                else:
                    end = dists[m.name].shape[1]
                    add = bias[:, b, end - w:end]
                s = bank[:, 2 * (i % 2):2 * (i % 2) + 2, :].rearrange("p a b -> p (a b)")[:, 0:w]
                if k >= 2:
                    reciprocal(m, it, k - 2)
                else:
                    dve.memset(spare[:, k:k + 1], 0.0).then_inc(s_spare, 1)
                dve.tensor_tensor_reduce(out=probs[:, i % 2, 0:w], in0=s, in1=add, scale=-1.0,
                                         scalar=neg_sink[:, b:b + 1] if m.is_swa else HUGE, op0=ALU.add, op1=ALU.min,
                                         accum_out=low[:, i:i + 1]).then_inc(s_max, 1)

            def copy_second(m, it, k):
                i, nb = k % 8, m.blocks(k % 8)
                if nb > 4:
                    dve.wait_ge(s_tr7, it * 16 + (m.steps + k + 3))
                    dve.wait_ge(s_pv, it * 16 + (m.steps + k + 1))
                    dve.tensor_copy(probs_t[:, i % 2, 4:nb, :].rearrange("p a b -> p (a b)"), bank[:, 5, 0:(nb - 4) * P]).then_inc(s_cp1, 1)

            def output(m, it, k):
                b, i = k // 8, k % 8
                f = factor[:, i:i + 1]
                dve.wait_ge(s_inv, it * 16 + (m.steps + k + 1))
                if m.is_diff and b == 1:
                    dve.tensor_tensor(f, f, neg_lam[:, :], ALU.mult).then_inc(s_fac, 1)
                    dve.wait_ge(s_fac, it * 8 + (m.factors + i + 1))
                if "gate" in m.g:
                    gate = nsa_gate[:, i, ds(it * 6 + (3 * b + m.g["gate"]), 1)]
                    if m.is_cmp and i == 0:
                        dve.scalar_tensor_tensor(out=f, in0=f, scalar=gate, in1=row_seen[:, :], op0=ALU.mult, op1=ALU.mult).then_inc(s_fac, 1)
                    else:
                        dve.tensor_tensor(f, f, gate, ALU.mult).then_inc(s_fac, 1)
                    dve.wait_ge(s_fac, it * 16 + (m.factors + k + 1))
                dve.wait_ge(s_pv, it * 16 + (m.steps + k + 3))
                o = bank[:, 6 + i % 2, 0:HD]
                y0, yi, yj = m.g["y"]
                yo = y[:, i, ds(it * yi + (y0 + b * yj), HD)]
                if m.is_diff and b == 0:
                    dve.tensor_scalar(first_map[:, i, :], o, f, None, ALU.mult).then_inc(s_o, 1)
                elif m.is_diff:
                    dve.wait_ge(s_o, it * 16 + (m.steps + k - 5))
                    dve.scalar_tensor_tensor(out=yo, in0=o, scalar=f, in1=first_map[:, i, :], op0=ALU.mult, op1=ALU.add).then_inc(s_o, 1)
                elif m.name in ("sel", "win"):
                    dve.wait_ge(s_o, it * 16 + (m.steps + k - 29))
                    dve.scalar_tensor_tensor(out=yo, in0=o, scalar=f, in1=yo, op0=ALU.mult, op1=ALU.add).then_inc(s_o, 1)
                else:
                    dve.tensor_scalar(yo, o, f, None, ALU.mult).then_inc(s_o, 1)

            for m in mixers:
                with dve.Fori(0, m.rounds) as it:
                    for k in range(18):
                        if k < 16:
                            maxima(m, it, k)
                        if 1 <= k < 17:
                            copy_second(m, it, k - 1)
                        if k >= 16:
                            reciprocal(m, it, k - 2)
                        if k >= 2:
                            output(m, it, k - 2)


_INS = ['x', 'c', 'ada_w', 'ada_b', 'norm_attn_g', 'norm_moe_g', 'norm_final_g', 'w_in', 'w_out', 'diff_lam_q1',
        'diff_lam_k1', 'diff_lam_q2', 'diff_lam_k2', 'diff_subln_g', 'swa_sinks', 'fox_forget_b', 'nsa_cmp_pos',
        'nsa_cmp_w1', 'nsa_cmp_b1', 'nsa_cmp_w2', 'router_w', 'router_b', 'exp_w_gate', 'exp_w_up', 'exp_w_down']


def kernel(**inputs):
    import numpy as np
    import concourse.bacc as bacc
    from concourse.bass_utils import run_bass_kernel_spmd

    nc = bacc.Bacc("TRN2", target_bir_lowering=False, num_devices=1)
    arrays, args = {}, {}
    for name in _INS:
        a = np.ascontiguousarray(inputs[name])
        arrays[f"in_{name}"] = a
        args[name] = nc.dram_tensor(f"in_{name}", a.shape, F32, kind="ExternalInput").ap()
    arrays["in_neg_slopes"] = np.repeat(np.array(NEG_SLOPES, np.float32)[:, None], P, axis=1)
    args["neg_slopes"] = nc.dram_tensor("in_neg_slopes", (NJOBS, P), F32, kind="ExternalInput").ap()
    out = nc.dram_tensor("out", (1, T, D), F32, kind="ExternalOutput").ap()
    build(nc, **args, out=out)
    r = run_bass_kernel_spmd(nc, [arrays], core_ids=[0])
    return r.results[0]["out"]
```

```python
from contextlib import ExitStack

import concourse.bass as bass
from concourse import mybir

F32 = mybir.dt.float32
I32 = mybir.dt.int32
U32 = mybir.dt.uint32
F32R = mybir.dt.float32r
ALU = mybir.AluOpType
ACT = mybir.ActivationFunctionType
AX_X = mybir.AxisListType.X
ds = bass.ds

P = 128
T = 1024
NT = T // P
D = 1024
DC = D // P
HD = 64
NH = 4
EPS = 1e-6
BIG = 1e32
HUGE = 3e38

C_DQ, C_DK, C_DV = 0, 256, 512
C_SQ, C_SK, C_SV = 768, 1024, 1152
C_FQ, C_FK, C_FV, C_FF = 1280, 1536, 1792, 2048
C_NQ, C_KC, C_KS, C_KW, C_VS, C_VW, C_G = 2052, 2308, 2436, 2500, 2564, 2628, 2692
IN_COLS = 2704
ROW_TILES = (
    [(c, 32 ** -0.5) for c in (0, 128)] + [(c, 1.0) for c in (256, 384)]
    + [(c, 0.125) for c in (768, 896)] + [(1024, 1.0)]
    + [(c, 0.125) for c in (1280, 1408)] + [(c, 1.0) for c in (1536, 1664)]
    + [(c, 0.125) for c in (2052, 2180)] + [(C_KC, 1.0), (C_KS, 1.0)]
)
TOKEN_RUNS = [[(C_DV, 256), (C_SV, 128)], [(C_FV, 260), (C_VS, 64), (C_VW, 76)]]
VA = 384
VW = 784
V_D, V_S, V_F, V_FF, V_KS, V_KW, V_G = 0, 256, 384, 640, 644, 708, 772

SL = 256
N_SL = 6 * D // SL
ADA_RING = 2
NC = 63
NE = 64
EB = 128
HB = EB // 2
IN_ROWS = 2 * T + EB
NOV_T = 16
NOV = (2 * T - 1) // (EB + 1)
OUT_ROWS = IN_ROWS + NOV * EB
DF = 512
FC = DF // P
LAM_INIT = 0.2


def slope(mixer, head):
    return 2.0 ** (-8.0 * (3 * head + mixer + 1) / (3 * NH))


GROUPS = [
    dict(name="diff", rounds=4, k=32, prev=7, q=(C_DQ, 64, 32), kk=(C_DK, 64, 32), v=(V_D, 64, 0), y=(0, 64, 0), job=0),
    dict(name="swa", rounds=2, k=64, prev=1, q=(C_SQ, 128, 64), kk=(C_SK, 64, 0), v=(V_S, 64, 0), y=(256, 128, 64), job=8),
    dict(name="fox", rounds=2, k=64, prev=7, q=(C_FQ, 128, 64), kk=(C_FK, 128, 64), v=(V_F, 128, 64), y=(512, 128, 64), job=12),
    dict(name="cmp", rounds=2, k=64, prev=0, q=(C_NQ, 128, 64), kk=None, v=None, y=(768, 128, 64), job=16, gate=0),
    dict(name="sel", rounds=2, k=64, prev=7, q=(C_NQ, 128, 64), kk=(C_KS, 0, 0), v=(V_KS, 0, 0), y=(768, 128, 64), job=20, gate=1),
    dict(name="win", rounds=2, k=64, prev=4, q=(C_NQ, 128, 64), kk=(C_KW, 0, 0), v=(V_KW, 0, 0), y=(768, 128, 64), job=24, gate=2),
]
NJOBS = 28
NEG_SLOPES = [-slope(0, j // 2) for j in range(8)] + [-slope(1, j) for j in range(4)] + [0.0] * 4 + [
    -slope(2, j % 4) for j in range(12)]


class Chain:

    def __init__(self, engine, semaphore):
        self.engine, self.semaphore, self.count = engine, semaphore, 0

    def __call__(self, ins):
        self.count += 1
        ins.then_inc(self.semaphore, 1)
        self.engine.wait_ge(self.semaphore, self.count)


def build(nc, x, c, ada_w, ada_b, norm_attn_g, norm_moe_g, norm_final_g, w_in, w_out,
          diff_lam_q1, diff_lam_k1, diff_lam_q2, diff_lam_k2, diff_subln_g,
          swa_sinks, fox_forget_b, nsa_cmp_pos, nsa_cmp_w1, nsa_cmp_b1, nsa_cmp_w2,
          router_w, router_b, exp_w_gate, exp_w_up, exp_w_down, neg_slopes, out):
    ctx = ExitStack()

    def dram(name, shape):
        return nc.dram_tensor(name, shape, F32).ap()

    qk_rows = dram("qk_rows", [2, IN_COLS, T])
    cum_rows = dram("cum_rows", [NH, 4, T])
    slots_in = dram("slots_in", [IN_ROWS, D])
    slots_out = dram("slots_out", [OUT_ROWS, D])

    with ctx:
        def sb(name, shape, dt=F32, to=None):
            return (to or ctx).enter_context(nc.sbuf_tensor(name, shape, dt))

        def sem(name):
            return ctx.enter_context(nc.semaphore(name))

        link = Chain(nc.vector, sem("s_chain"))
        then = Chain(nc.gpsimd, sem("s_pool"))
        bank = ctx.enter_context(nc.psum_tensor("bank", [P, 8, 512], F32))

        ident = sb("ident", [P, P])
        ones = sb("ones", [P, P])
        earlier = sb("earlier", [P, P])
        mod_cols = sb("mod_cols", [P, 48])
        gain_attn = sb("gain_attn", [P, 8])
        gain_moe = sb("gain_moe", [P, 8])
        param_cols = sb("param_cols", [P, 72])
        gate_attn = sb("gate_attn", [P, D])
        gate_moe = sb("gate_moe", [P, D])
        eps_col = sb("eps_col", [P, 1])
        row_gate = sb("row_gate", [P, NT, 2])
        row_slot = sb("row_slot", [P, NT, 2], I32)
        row_out = sb("row_out", [P, NT, 2], I32)
        starts = sb("starts", [1, NE], I32)
        sizes = sb("sizes", [1, NE], I32)

        x1 = sb("x1", [P, NT, D])
        rs_moe = sb("rs_moe", [P, 3, NT])

        proj = ExitStack()
        heads = ExitStack()
        kcvc = heads.enter_context(nc.sbuf_tensor("kcvc", [P, T], F32))
        v_tok = heads.enter_context(nc.sbuf_tensor("v_tok", [P, NT, VW], F32))

        pj = lambda name, shape, dt=F32: proj.enter_context(nc.sbuf_tensor(name, shape, dt))
        params = pj("params", [72, P])
        cond = pj("cond", [P, 8])
        cond_e = pj("cond_e", [P, 8])
        cond_wide = pj("cond_wide", [P, 8, P])
        xt = pj("xt", [P, 4, D])
        squares = pj("squares", [P, D])
        ss = pj("ss", [P, 3, NT])
        ht = x1
        win = pj("win", [P, DC, IN_COLS])
        ada = pj("ada", [P, ADA_RING, DC, SL])
        stage = pj("stage", [P, 4, 512])
        ada_row = pj("ada_row", [P, 2, P])
        zeros = squares

        s_param = sem("s_param")
        s_param_t = sem("s_param_t")
        s_const = sem("s_const")
        s_eps = sem("s_eps")
        s_cond = sem("s_cond")
        s_cexp = sem("s_cexp")
        s_x = [sem(f"s_x{i}") for i in range(4)]
        s_ada = [sem(f"s_ada{i}") for i in range(ADA_RING)]
        s_ada_used = sem("s_ada_used")
        s_win = [sem(f"s_win{i}") for i in range(5)]
        s_sq = sem("s_sq")
        s_sd = sem("s_sd")
        s_xn = sem("s_xn")
        s_tr = sem("s_tr")
        s_ht_a = sem("s_ht_a")
        s_ht_v = sem("s_ht_v")
        s_mod = sem("s_mod")
        s_row_ev = sem("s_row_ev")
        s_turned = sem("s_turned")
        s_col_ev = sem("s_col_ev")
        s_rt = sem("s_rt")
        s_rt_a = sem("s_rt_a")
        s_rt_v = sem("s_rt_v")
        s_store = [sem(f"s_store{i}") for i in range(4)]
        s_tk = sem("s_tk")
        s_tk_v = sem("s_tk_v")
        s_bias = sem("s_bias")
        s_zfill = sem("s_zfill")
        s_split = sem("s_split")

        ada_v = ada_w[0].rearrange("(k p) n -> p k n", p=P)
        win_v = w_in[0].rearrange("(k p) n -> p k n", p=P)
        x_v = x[0].rearrange("(t p) d -> p t d", p=P)
        HALVES = [(m, half) for half in range(2) for m in range(len(ROW_TILES))]
        N_RT = len(HALVES)
        CMP_TILE = 13
        TURN_X = 3
        ada_at = lambda i: i + 3 if 5 <= i < 5 + N_SL - 8 else None
        WIN_LOADS = [[(0, 0, 512)], [(C_SQ, C_SQ, 384)], [(C_FQ, C_FQ, 512)], [(C_NQ, C_NQ, 448), (C_KW, C_VS, 64)],
                     [(C_DV, C_DV, 256), (C_SV, C_SV, 128), (C_FV, C_FV, 260), (C_VS, C_KW, 64), (C_VW, C_VW, IN_COLS - C_VW)]]
        WIN_OF_TILE = [0] * 4 + [1] * 3 + [2] * 4 + [3] * 4

        def stored_before(i):
            return sum(1 for j in range(i) if HALVES[j][0] != CMP_TILE)

        def uses_before(i):
            return sum(1 for j in range(i % 4, i, 4) if HALVES[j][0] != CMP_TILE)

        parts = lambda i: xt[:, i % 4, :].bitcast(F32R).rearrange("p (a n) -> p a n", a=2)

        def slice_section(s):
            return s * SL // D

        def is_gate(s):
            return slice_section(s) in (2, 5)

        def columns_before(s):
            return sum(1 for r in range(s) if not is_gate(r))

        with nc.Block() as block:
            @block.sync
            def _(sp):
                sp.dma_start(params[0:48, :], ada_b[0].rearrange("(m p) -> m p", p=P)).then_inc(s_param, 16)
                sp.dma_start(params[48:56, :], norm_attn_g[0].rearrange("(m p) -> m p", p=P)).then_inc(s_param, 16)
                sp.dma_start(params[56:64, :], norm_moe_g[0].rearrange("(m p) -> m p", p=P)).then_inc(s_param, 16)
                sp.dma_start(params[64:72, :], c[0].rearrange("(m p) -> m p", p=P)).then_inc(s_param, 16)
                for t in range(4):
                    sp.dma_start(xt[:, t, :], x_v[:, t, :]).then_inc(s_x[t], 16)
                for s in range(N_SL):
                    if s == 8:
                        for t in range(4, NT):
                            if t == 4:
                                sp.wait_ge(s_tr, 8)
                            sp.dma_start(xt[:, t - 4, :], x_v[:, t, :]).then_inc(s_x[t - 4], 16)
                    if s >= ADA_RING:
                        sp.wait_ge(s_ada_used, s - ADA_RING + 1)
                    sp.dma_start(ada[:, s % ADA_RING, :, :], ada_v[:, :, s * SL:(s + 1) * SL]).then_inc(
                        s_ada[s % ADA_RING], 16)

            @block.gpsimd
            def _(pool):
                then(pool.memset(ident[:, :], 0.0))
                then(pool.affine_select(out=ident[:, :], in_=ident[:, :], compare_op=ALU.not_equal, fill=1.0,
                                        base=0, pattern=[[-1, P]], channel_multiplier=1))
                then(pool.memset(ones[:, :], 1.0))
                pool.sem_inc(s_const, 1)
                then(pool.affine_select(out=earlier[:, :], in_=ones[:, :], compare_op=ALU.is_gt, fill=0.0,
                                        base=0, pattern=[[1, P]], channel_multiplier=-1))
                for g, loads in enumerate(WIN_LOADS):
                    if g == 0:
                        pool.wait_ge(s_ada_used, 4)
                    elif g == 1:
                        pool.wait_ge(s_x[3], 32)
                    for dst, src, w in loads:
                        pool.dma_start(win[:, :, dst:dst + w], win_v[:, :, src:src + w]).then_inc(s_win[g], 16)
                pool.dma_start(gate_attn[:, :], ada_b[0:1, 2 * D:3 * D].to_broadcast([P, D])).then_inc(s_bias, 16)
                pool.dma_start(gate_moe[:, :], ada_b[0:1, 5 * D:6 * D].to_broadcast([P, D])).then_inc(s_bias, 16)
                for i, (m, half) in enumerate(HALVES):
                    if m == CMP_TILE:
                        continue
                    c0 = ROW_TILES[m][0]
                    cols = slice(half * 512, half * 512 + 512)
                    pool.wait_ge(s_split, stored_before(i) + 1)
                    pool.dma_start(qk_rows[:, c0:c0 + P, cols].rearrange("a p n -> p a n"), parts(i).bitcast(F32)).then_inc(s_store[i % 4], 16)

            @block.tensor
            def _(pe):
                pe.wait_ge(s_param, 64)
                pe.wait_ge(s_const, 1)
                pe.transpose(bank[:, 0, 0:72], params[:, :], ident[0:72, 0:72]).then_inc(s_param_t, 1)

                def ada_rows(s):
                    pe.wait_ge(s_ada[s % ADA_RING], 16 * (s // ADA_RING + 1))
                    if s >= 2:
                        pe.wait_ge(s_row_ev, s - 1)
                    at = (6 if s < 8 else 2) + s % 2
                    for k in range(DC):
                        ends = dict(start=(k == 0), stop=(k == DC - 1))
                        if is_gate(s):
                            mm = pe.matmul(bank[:, at, 0:SL], cond_wide[:, k, :], ada[:, s % ADA_RING, k, :], **ends)
                            continue
                        for h in range(2):
                            mm = pe.matmul(bank[h * 64:h * 64 + 64, at, 0:P], cond_wide[:, k, 0:64],
                                           ada[:, s % ADA_RING, k, h * P:(h + 1) * P], **ends)
                    mm.then_inc(s_ada_used, 1)

                def ada_turn(s):
                    if is_gate(s):
                        return
                    n = columns_before(s)
                    pe.wait_ge(s_row_ev, s + 1)
                    if n >= 2:
                        pe.wait_ge(s_col_ev, n - 1)
                    pe.transpose(bank[:, n % 2, 0:P], ada_row[:, n % 2, :], ident[:, :]).then_inc(s_turned, 1)

                def turn_x(g):
                    for k in range(DC):
                        n = 8 * g + k
                        for i in range(4):
                            t = 4 * g + i
                            if k == 0:
                                pe.wait_ge(s_xn, t + 1)
                            if i == 0 and n >= 2:
                                pe.wait_ge((s_ht_a, s_ht_v)[n % 2], n // 2)
                            mm = pe.transpose(bank[:, 2 + n % 2, i * P:(i + 1) * P], xt[:, i, k * P:(k + 1) * P], ident[:, :])
                        mm.then_inc(s_tr, 1)
                    pe.wait_ge(s_ht_a, 4 * g + 4)
                    pe.wait_ge(s_ht_v, 4 * g + 4)

                pe.wait_ge(s_cond, 2)
                for s in range(8):
                    ada_rows(s)
                    if s >= 1:
                        ada_turn(s - 1)
                ada_turn(7)
                turn_x(0)
                for i, (m, half) in enumerate(HALVES):
                    c0 = ROW_TILES[m][0]
                    if half == 0:
                        g = WIN_OF_TILE[m]
                        pe.wait_ge(s_win[g], 16 * len(WIN_LOADS[g]))
                    if i >= 2:
                        pe.wait_ge((s_rt_a, s_rt_v)[i % 2], i // 2)
                    for k in range(DC):
                        mm = pe.matmul(bank[:, 4 + i % 2, :], win[:, k, c0:c0 + P], ht[:, k, half * 512:half * 512 + 512],
                                       start=(k == 0), stop=(k == DC - 1))
                    mm.then_inc(s_rt, 1)
                    if i == TURN_X:
                        turn_x(1)
                    if ada_at(i):
                        ada_rows(ada_at(i))
                        if ada_at(i) > 8:
                            ada_turn(ada_at(i) - 1)
                pe.wait_ge(s_win[4], 16 * len(WIN_LOADS[4]))
                for i in range(2 * NT):
                    t, b = i // 2, i % 2
                    if i >= 2:
                        pe.wait_ge(s_tk_v, i - 1)
                    at = 0
                    for c0, w in TOKEN_RUNS[b]:
                        for k in range(DC):
                            mm = pe.matmul(bank[:, 6 + b, at:at + w], ht[:, k, t * P:(t + 1) * P], win[:, k, c0:c0 + w],
                                           start=(k == 0), stop=(k == DC - 1))
                        at += w
                    mm.then_inc(s_tk, 1)

            @block.scalar
            def _(act):
                act.wait_ge(s_cond, 1)
                act.activation(cond_e[:, :], param_cols[:, 64:72], ACT.Exp, scale=-1.0).then_inc(s_cexp, 1)
                act.wait_ge(s_eps, 1)

                def deviation(t):
                    act.wait_ge(s_x[t % 4], 16 * (t // 4 + 1))
                    act.activation(squares[:, :], xt[:, t % 4, :], ACT.Square, accum_out=ss[:, 0, t:t + 1]).then_inc(s_sq, 1)
                    act.wait_ge(s_sq, t + 1)
                    act.activation(ss[:, 1, t:t + 1], ss[:, 0, t:t + 1], ACT.Sqrt, bias=eps_col[:, :], scale=1.0 / D).then_inc(s_sd, 1)

                def modulate_x(g):
                    for k in range(0, DC, 2):
                        act.wait_ge(s_tr, 8 * g + k + 1)
                        act.activation(ht[:, k, g * 512:g * 512 + 512], bank[:, 2, :], ACT.Identity, bias=mod_cols[:, k:k + 1],
                                       scale=gain_attn[:, k:k + 1]).then_inc(s_ht_a, 1)

                for t in range(4):
                    deviation(t)
                act.wait_ge(s_mod, 1)
                modulate_x(0)
                for i, (m, half) in enumerate(HALVES):
                    if i % 2 == 0:
                        act.wait_ge(s_rt, i + 1)
                        if m == CMP_TILE:
                            act.copy(kcvc[:, half * 512:half * 512 + 512], bank[:, 4, :]).then_inc(s_rt_a, 1)
                        else:
                            if i >= 4:
                                act.wait_ge(s_split, stored_before(i - 3))
                            act.mul(stage[:, i % 4, :], bank[:, 4, :], ROW_TILES[m][1]).then_inc(s_rt_a, 1)
                    elif i <= TURN_X:
                        deviation(3 + i)
                        deviation(4 + i)
                    if i == TURN_X:
                        modulate_x(1)

            @block.vector
            def _(dve):
                dve.memset(eps_col[:, :], EPS).then_inc(s_eps, 1)
                dve.wait_ge(s_param_t, 1)
                link(dve.tensor_copy(param_cols[:, :], bank[:, 0, 0:72]))
                dve.sem_inc(s_cond, 1)
                dve.wait_ge(s_cexp, 1)
                link(dve.tensor_scalar(cond_e[:, :], cond_e[:, :], 1.0, None, ALU.add))
                link(dve.reciprocal(cond_e[:, :], cond_e[:, :]))
                link(dve.tensor_tensor(cond[:, :], param_cols[:, 64:72], cond_e[:, :], ALU.mult))
                dve.wait_ge(s_const, 1)
                for k in range(DC):
                    last = dve.tensor_scalar(cond_wide[:, k, :], ones[:, :], cond[:, k:k + 1], None, ALU.mult)
                last.then_inc(s_cond, 1)

                def normalise(t):
                    dve.wait_ge(s_sd, t + 1)
                    link(dve.reciprocal(ss[:, 2, t:t + 1], ss[:, 1, t:t + 1]))
                    dve.tensor_scalar(xt[:, t % 4, :], xt[:, t % 4, :], ss[:, 2, t:t + 1], None, ALU.mult).then_inc(s_xn, 1)

                for t in range(4):
                    normalise(t)

                def take_row(s):
                    dve.wait_ge(s_ada_used, s + 1)
                    row = bank[:, (6 if s < 8 else 2) + s % 2, 0:SL if is_gate(s) else P]
                    if is_gate(s):
                        o = (gate_attn if slice_section(s) == 2 else gate_moe)[:, s * SL % D:s * SL % D + SL]
                        dve.tensor_tensor(o, row, o, ALU.add).then_inc(s_row_ev, 1)
                        return
                    n = columns_before(s)
                    if n >= 2:
                        dve.wait_ge(s_turned, n - 1)
                    dve.tensor_copy(ada_row[:, n % 2, :], row).then_inc(s_row_ev, 1)

                def take_columns(s):
                    if is_gate(s):
                        return
                    n = columns_before(s)
                    c = s * SL // P
                    dve.wait_ge(s_turned, n + 1)
                    dve.tensor_tensor(mod_cols[:, c:c + SL // P], bank[:, n % 2, 0:P].rearrange("p (m n) -> p m n", n=64)[:, :, 0],
                                      param_cols[:, c:c + SL // P], ALU.add).then_inc(s_col_ev, 1)

                def modulate_x(g):
                    for k in range(1, DC, 2):
                        dve.wait_ge(s_tr, 8 * g + k + 1)
                        dve.tensor_scalar(ht[:, k, g * 512:g * 512 + 512], bank[:, 3, :], gain_attn[:, k:k + 1],
                                          mod_cols[:, k:k + 1], ALU.mult, ALU.add).then_inc(s_ht_v, 1)

                def split(i):
                    if uses_before(i):
                        dve.wait_ge(s_store[i % 4], 16 * uses_before(i))
                    link(dve.tensor_copy(parts(i)[:, 0, :], stage[:, i % 4, :]))
                    dve.tensor_tensor(parts(i)[:, 1, :], stage[:, i % 4, :], parts(i)[:, 0, :], ALU.subtract).then_inc(s_split, 1)

                for s in range(8):
                    take_row(s)
                    if s >= 1:
                        take_columns(s - 1)
                take_columns(7)
                dve.wait_ge(s_col_ev, 8)
                link(dve.tensor_scalar(gain_attn[:, :], mod_cols[:, 8:16], 1.0, None, ALU.add))
                link(dve.tensor_tensor(gain_attn[:, :], gain_attn[:, :], param_cols[:, 48:56], ALU.mult))
                dve.sem_inc(s_mod, 1)
                modulate_x(0)
                for i, (m, half) in enumerate(HALVES):
                    if i % 2:
                        dve.wait_ge(s_rt, i + 1)
                        if m == CMP_TILE:
                            dve.tensor_copy(kcvc[:, half * 512:half * 512 + 512], bank[:, 5, :]).then_inc(s_rt_v, 1)
                        else:
                            dve.tensor_scalar(stage[:, i % 4, :], bank[:, 5, :], ROW_TILES[m][1], None, ALU.mult).then_inc(s_rt_v, 1)
                            dve.wait_ge(s_rt_v, i // 2 + 1)
                    else:
                        dve.wait_ge(s_rt_a, i // 2 + 1)
                    if i > TURN_X and m != CMP_TILE:
                        split(i)
                    if i % 2 and i <= TURN_X:
                        normalise(3 + i)
                        normalise(4 + i)
                    if i == TURN_X:
                        modulate_x(1)
                        for j in range(i + 1):
                            split(j)
                    if ada_at(i):
                        if ada_at(i) == 8:
                            dve.wait_ge(s_bias, 32)
                        take_row(ada_at(i))
                        if ada_at(i) > 8:
                            take_columns(ada_at(i) - 1)
                for i in range(2 * NT):
                    t, b = i // 2, i % 2
                    w = (VA, VW - VA)[b]
                    dve.wait_ge(s_tk, i + 1)
                    dve.tensor_copy(v_tok[:, t, b * VA:b * VA + w], bank[:, 6 + b, 0:w]).then_inc(s_tk_v, 1)
                dve.wait_ge(s_col_ev, columns_before(N_SL))
                link(dve.tensor_scalar(gain_moe[:, :], mod_cols[:, 32:40], 1.0, None, ALU.add))
                link(dve.tensor_tensor(gain_moe[:, :], gain_moe[:, :], param_cols[:, 56:64], ALU.mult))
        proj.close()

        y = heads.enter_context(nc.sbuf_tensor("y", [P, NT, D], F32))
        kc_t = heads.enter_context(nc.sbuf_tensor("kc_t", [P, NC], F32))
        vc = heads.enter_context(nc.sbuf_tensor("vc", [NC, HD], F32))
        nsa_gate = heads.enter_context(nc.sbuf_tensor("nsa_gate", [P, NT, 3 * NH], F32))
        neg_lam = heads.enter_context(nc.sbuf_tensor("neg_lam", [P, 1], F32))
        dist_full = heads.enter_context(nc.sbuf_tensor("dist_full", [P, T], F32))
        dist_win = heads.enter_context(nc.sbuf_tensor("dist_win", [P, 640], F32))
        dist_swa = heads.enter_context(nc.sbuf_tensor("dist_swa", [P, 256], F32))
        dist_cmp = heads.enter_context(nc.sbuf_tensor("dist_cmp", [P, 119], F32))
        causal = heads.enter_context(nc.sbuf_tensor("causal", [P, T], F32))
        row_seen = heads.enter_context(nc.sbuf_tensor("row_seen", [P, 1], F32))
        comp = ExitStack()
        cp = lambda name, shape, dt=F32: comp.enter_context(nc.sbuf_tensor(name, shape, dt))
        w1 = cp("w1", [P, 32, P])
        pos_rows = cp("pos_rows", [64, HD])
        pos = cp("pos", [P, 32])
        b1 = cp("b1", [P, 2])
        w2 = cp("w2", [P, 3, HD])
        blocks_t = cp("blocks_t", [P, 32, NC])
        hid = cp("hid", [P, 2 * NC])
        hid_a = cp("hid_a", [P, 2 * NC])
        bf = cp("bf", [P, NH])
        fz = cp("fz", [P, 8, NT, NH])
        f_t = cp("f_t", [NH, 2, T])
        cum = cp("cum", [NH, T])
        cum_hl = cp("cum_hl", [NH, 4, T], F32R)
        lam_in = cp("lam_in", [P, 4, 32])
        lam = cp("lam", [P, 4])
        ge = cp("ge", [P, NT, 12])

        s_ld2 = sem("s_ld2")
        s_post = sem("s_post")
        s_pos = sem("s_pos")
        s_blk = sem("s_blk")
        s_hid = sem("s_hid")
        s_a2 = sem("s_a2")
        s_v2 = sem("s_v2")
        s_hid2 = sem("s_hid2")
        s_kc = sem("s_kc")
        s_ft = sem("s_ft")
        s_f = sem("s_f")
        s_cum = sem("s_cum")
        s_cumst = sem("s_cumst")

        with nc.Block() as block:
            @block.sync
            def _(sp):
                for h in range(2):
                    sp.dma_start(w1[64 * h:64 * h + 64, :, :], nsa_cmp_w1[0, h].rearrange("(j d) o -> d j o", d=HD)).then_inc(s_ld2, 16)
                sp.dma_start(pos_rows[:, :], nsa_cmp_pos[0].rearrange("h j d -> (h j) d")).then_inc(s_ld2, 16)
                sp.dma_start(b1[:, :], nsa_cmp_b1[0].rearrange("h o -> o h"), allow_slow_non_contiguous=True).then_inc(s_ld2, 16)
                sp.dma_start(w2[:, 1:3, :], nsa_cmp_w2[0].rearrange("h o d -> o h d")).then_inc(s_ld2, 16)
                sp.dma_start(w2[:, 0, :], nsa_cmp_w2[0, 0]).then_inc(s_ld2, 16)
                sp.dma_start(bf[:, :], fox_forget_b[0:1, :].to_broadcast([P, NH])).then_inc(s_ld2, 16)
                for i, v in enumerate((diff_lam_q1, diff_lam_k1, diff_lam_q2, diff_lam_k2)):
                    sp.dma_start(lam_in[:, i, :], v[0:1, :].to_broadcast([P, 32])).then_inc(s_ld2, 16)
                sp.wait_ge(s_cum, 1)
                sp.dma_start(cum_rows, cum_hl[:, :, :].bitcast(F32)).then_inc(s_cumst, 16)
                sp.wait_ge(s_cumst, 16)
                for i in range(4):
                    uses = sum(1 for j in range(i, N_RT, 4) if HALVES[j][0] != CMP_TILE)
                    sp.wait_ge(s_store[i], 16 * uses)

            @block.gpsimd
            def _(pool):
                then(pool.iota(dist_full[:, :], pattern=[[-1, T]], base=T - P, channel_multiplier=1,
                               allow_small_or_imprecise_dtypes=True))
                then(pool.affine_select(out=dist_full[:, :], in_=dist_full[:, :], compare_op=ALU.is_ge, fill=BIG,
                                        base=T - P, pattern=[[-1, T]], channel_multiplier=1))
                then(pool.affine_select(out=dist_win[:, :], in_=dist_full[:, T - 640:], compare_op=ALU.is_gt, fill=BIG,
                                        base=0, pattern=[[1, 640]], channel_multiplier=-1))
                then(pool.affine_select(out=dist_swa[:, :], in_=dist_full[:, T - 256:], compare_op=ALU.is_gt, fill=BIG,
                                        base=0, pattern=[[1, 256]], channel_multiplier=-1))
                then(pool.iota(dist_cmp[:, :], pattern=[[-16, 119]], base=16 * 56 - 31, channel_multiplier=1,
                               allow_small_or_imprecise_dtypes=True))
                then(pool.affine_select(out=dist_cmp[:, :], in_=dist_cmp[:, :], compare_op=ALU.is_ge, fill=BIG,
                                        base=16 * 56 - 31, pattern=[[-16, 119]], channel_multiplier=1))
                then(pool.memset(causal[:, :], 0.0))
                then(pool.affine_select(out=causal[:, :], in_=causal[:, :], compare_op=ALU.is_ge, fill=-1e30,
                                        base=T - P, pattern=[[-1, T]], channel_multiplier=1))
                then(pool.memset(row_seen[:, :], 1.0))
                then(pool.affine_select(out=row_seen[:, :], in_=row_seen[:, :], compare_op=ALU.is_ge, fill=0.0,
                                        base=-31, pattern=[[0, 1]], channel_multiplier=1))

            @block.tensor
            def _(pe):
                pe.wait_ge(s_ld2, 176)
                pe.transpose(bank[0:64, 0, 0:64], pos_rows[:, :], ident[0:64, 0:64]).then_inc(s_post, 1)
                pe.wait_ge(s_blk, 1)
                for j in range(32):
                    for h in range(2):
                        mm = pe.matmul(bank[:, 2 + h, 0:NC], w1[64 * h:64 * h + 64, j, :],
                                       blocks_t[64 * h:64 * h + 64, j, :], start=(j == 0), stop=(j == 31))
                    if j == 23:
                        pe.wait_ge(s_f, 1)
                        for t in range(NT):
                            turned = pe.transpose(bank[0:NH, 4 + t // 4, t % 4 * P:t % 4 * P + P], fz[:, 7, t, :], ident[:, :])
                        turned.then_inc(s_ft, 1)
                mm.then_inc(s_hid, 1)
                pe.wait_ge(s_hid2, 1)
                pe.matmul(bank[:, 6, 0:NC], w2[:, 0:2, :].rearrange("p a d -> p (a d)"), hid[:, 0:NC], start=True, stop=True)
                pe.matmul(bank[0:NC, 7, 0:HD], hid[:, NC:2 * NC], w2[:, 2, :], start=True, stop=True).then_inc(s_kc, 1)

            @block.scalar
            def _(act):
                act.activation(ge[:, :, :], v_tok[:, :, V_G:V_G + 12], ACT.Exp, scale=-1.0).then_inc(s_a2, 1)
                act.wait_ge(s_v2, 1)
                act.activation(fz[:, 2, :, :], fz[:, 1, :, :], ACT.Exp).then_inc(s_a2, 1)
                act.wait_ge(s_v2, 2)
                act.activation(lam[:, 0:2], lam[:, 0:2], ACT.Exp).then_inc(s_a2, 1)
                act.wait_ge(s_v2, 3)
                act.activation(fz[:, 4, :, :], fz[:, 3, :, :], ACT.Ln).then_inc(s_a2, 1)
                act.wait_ge(s_v2, 4)
                act.activation(hid_a[:, :], hid_a[:, :], ACT.Exp, scale=-2.0 * (2.0 / 3.141592653589793) ** 0.5).then_inc(s_a2, 1)

            @block.vector
            def _(dve):
                dve.wait_ge(s_ld2, 176)
                z = fz[:, 0, :, :]
                link(dve.tensor_tensor(z, v_tok[:, :, V_FF:V_FF + NH],
                                       bf[:, :].rearrange("p (a h) -> p a h", a=1).to_broadcast([P, NT, NH]), ALU.add))
                link(dve.tensor_scalar(fz[:, 1, :, :], z, -1.0, None, ALU.mult))
                link(dve.tensor_tensor(fz[:, 1, :, :], fz[:, 1, :, :], z, ALU.min))
                dve.sem_inc(s_v2, 1)
                link(dve.tensor_tensor(lam_in[:, 0, :], lam_in[:, 0, :], lam_in[:, 1, :], ALU.mult))
                link(dve.tensor_tensor(lam_in[:, 2, :], lam_in[:, 2, :], lam_in[:, 3, :], ALU.mult))
                link(dve.reduce_sum(lam[:, 0:1], lam_in[:, 0, :], AX_X))
                link(dve.reduce_sum(lam[:, 1:2], lam_in[:, 2, :], AX_X))
                dve.sem_inc(s_v2, 1)
                dve.wait_ge(s_post, 1)
                link(dve.tensor_copy(pos[0:64, :], bank[0:64, 0, 0:32]))
                link(dve.tensor_copy(pos[64:P, :], bank[0:64, 0, 32:64]))
                kv3 = kcvc[:, :].rearrange("p (n b) -> p b n", b=16)
                for a in range(2):
                    link(dve.tensor_tensor(blocks_t[:, 16 * a:16 * a + 16, :], kv3[:, :, a:a + NC],
                                           pos[:, 16 * a:16 * a + 16].rearrange("p (j a) -> p j a", a=1).to_broadcast([P, 16, NC]),
                                           ALU.add))
                dve.sem_inc(s_blk, 1)
                dve.wait_ge(s_a2, 2)
                link(dve.tensor_scalar(fz[:, 3, :, :], fz[:, 2, :, :], 1.0, None, ALU.add))
                dve.sem_inc(s_v2, 1)
                dve.wait_ge(s_a2, 1)
                link(dve.tensor_scalar(ge[:, :, :], ge[:, :, :], 1.0, None, ALU.add))
                link(dve.reciprocal(nsa_gate[:, :, :], ge[:, :, :]))
                dve.wait_ge(s_a2, 3)
                link(dve.tensor_tensor(lam[:, 2:3], lam[:, 1:2], lam[:, 0:1], ALU.subtract))
                link(dve.tensor_scalar(neg_lam[:, :], lam[:, 2:3], -LAM_INIT, None, ALU.add))
                e, w, lw = fz[:, 2, :, :], fz[:, 3, :, :], fz[:, 4, :, :]
                is_one, den = fz[:, 5, :, :], fz[:, 6, :, :]
                dve.wait_ge(s_a2, 4)
                link(dve.tensor_scalar(den, w, -1.0, None, ALU.add))
                link(dve.tensor_scalar(is_one, den, 0.0, None, ALU.is_equal))
                link(dve.tensor_tensor(den, den, is_one, ALU.add))
                link(dve.tensor_tensor(lw, lw, is_one, ALU.add))
                link(dve.reciprocal(den, den))
                link(dve.tensor_tensor(lw, lw, e, ALU.mult))
                link(dve.tensor_tensor(lw, lw, den, ALU.mult))
                link(dve.tensor_scalar(z, z, 0.0, None, ALU.min))
                link(dve.tensor_tensor(fz[:, 7, :, :], z, lw, ALU.subtract))
                dve.sem_inc(s_f, 1)
                link(dve.memset(f_t[:, 1, :], 1.0))
                dve.wait_ge(s_ft, 1)
                link(dve.tensor_copy(f_t[:, 0, :], bank[0:NH, 4:6, :].rearrange("p a b -> p (a b)")))
                link(dve.tensor_tensor_scan(cum[:, :], f_t[:, 1, :], f_t[:, 0, :], 0.0, ALU.mult, ALU.add))
                link(dve.tensor_copy(cum_hl[:, 2, :], cum[:, :]))
                link(dve.tensor_tensor(cum_hl[:, 3, :], cum[:, :], cum_hl[:, 2, :], ALU.subtract))
                link(dve.tensor_scalar(cum_hl[:, 0:2, :], cum_hl[:, 2:4, :], -1.0, None, ALU.mult))
                dve.sem_inc(s_cum, 1)
                dve.wait_ge(s_hid, 1)
                for h in range(2):
                    link(dve.tensor_scalar(hid[:, h * NC:h * NC + NC], bank[:, 2 + h, 0:NC], b1[:, h:h + 1], None, ALU.add))
                link(dve.tensor_tensor(hid_a[:, :], hid[:, :], hid[:, :], ALU.mult))
                link(dve.tensor_scalar(hid_a[:, :], hid_a[:, :], 0.044715, 1.0, ALU.mult, ALU.add))
                link(dve.tensor_tensor(hid_a[:, :], hid_a[:, :], hid[:, :], ALU.mult))
                dve.sem_inc(s_v2, 1)
                dve.wait_ge(s_a2, 5)
                link(dve.tensor_scalar(hid_a[:, :], hid_a[:, :], 1.0, None, ALU.add))
                link(dve.reciprocal(hid_a[:, :], hid_a[:, :]))
                link(dve.tensor_tensor(hid[:, :], hid[:, :], hid_a[:, :], ALU.mult))
                dve.sem_inc(s_hid2, 1)
                dve.wait_ge(s_kc, 1)
                link(dve.tensor_copy(kc_t[:, :], bank[:, 6, 0:NC]))
                link(dve.tensor_copy(vc[:, :], bank[0:NC, 7, 0:HD]))
        comp.close()

        att = ExitStack()
        at_ = lambda name, shape, dt=F32: att.enter_context(nc.sbuf_tensor(name, shape, dt))
        qb = [at_(f"qb{i}", [P, T], F32R) for i in range(2)]
        ka = [at_(f"ka{i}", [P, T], F32R) for i in range(2)]
        kb = [at_(f"kb{i}", [P, T], F32R) for i in range(2)]
        cq = [at_(f"cq{i}", [4, T], F32R) for i in range(2)]
        ck = [at_(f"ck{i}", [4, T], F32R) for i in range(2)]
        neg_slope = at_("neg_slope", [P, 2])
        sink = at_("sink", [P, 2])
        neg_sink = at_("neg_sink", [P, 2])
        sink_exp = at_("sink_exp", [P, 8])
        bias = at_("bias", [P, 2, T])
        probs = at_("probs", [P, 4, T])
        probs_t = at_("probs_t", [P, 2, 8, P])
        low = at_("low", [P, 8])
        total = at_("total", [P, 8])
        factor = at_("factor", [P, 8])
        spare = at_("spare", [P, 2])
        nil = at_("nil", [P, 1])
        pool_spare = at_("pool_spare", [P, 2])
        vb = [at_(f"vb{i}", [P, NT, HD]) for i in range(2)]
        first_map = at_("first_map", [P, NT, HD])
        zeros = at_("zeros", [P, D])

        attend(nc, sem, dict(
            bank=bank, ident=ident, qb=qb, ka=ka, kb=kb, cq=cq, ck=ck, vb=vb, neg_slope=neg_slope, sink=sink, neg_sink=neg_sink,
            sink_exp=sink_exp, bias=bias, probs=probs, probs_t=probs_t, low=low, total=total, factor=factor,
            first_map=first_map, spare=spare, pool_spare=pool_spare, nil=nil, zeros=zeros, slots_in=slots_in, slots_out=slots_out, s_zfill=s_zfill, y=y, v_tok=v_tok, kc_t=kc_t, vc=vc, nsa_gate=nsa_gate, neg_lam=neg_lam,
            row_seen=row_seen, causal=causal, dist_full=dist_full, dist_win=dist_win, dist_swa=dist_swa,
            dist_cmp=dist_cmp, qk_rows=qk_rows, cum_rows=cum_rows, neg_slopes=neg_slopes, swa_sinks=swa_sinks))
        att.close()

        po = ExitStack()
        tail = ExitStack()
        o_ = lambda name, shape, dt=F32: po.enter_context(nc.sbuf_tensor(name, shape, dt))
        wo = o_("wo", [P, DC, D])
        y_t = o_("y_t", [P, DC, T])
        sub = o_("sub", [P, NT, NH, HD])
        sub_s = o_("sub_s", [P, 3, NT * NH])
        sub_g = o_("sub_g", [P, HD])
        sq2 = o_("sq2", [P, D])
        s_wo = sem("s_wo")
        s_sub = sem("s_sub")
        s_sqr = sem("s_sqr")
        s_yn = sem("s_yn")
        s_yt = sem("s_yt")
        s_yt_a = sem("s_yt_a")
        s_yt_v = sem("s_yt_v")
        s_wout = sem("s_wout")
        s_x1_done = sem("s_x1_done")
        s_sq4 = sem("s_sq4")
        s_sd4 = sem("s_sd4")
        s_xr = [sem(f"s_xr{i}") for i in range(NT)]
        with nc.Block() as block:
            @block.sync
            def _(sp):
                sp.dma_start(sub_g[:, :], diff_subln_g[0:1, :].to_broadcast([P, HD])).then_inc(s_sub, 16)
                for k in range(DC):
                    sp.dma_start(wo[:, k, :], w_out[0, k * P:(k + 1) * P, :]).then_inc(s_wo, 16)
                for t in range(NT):
                    sp.dma_start(x1[:, t, :], x_v[:, t, :]).then_inc(s_xr[t], 16)

            @block.tensor
            def _(pe):
                def project(t, chunks):
                    for half in range(2):
                        for k in chunks:
                            mm = pe.matmul(bank[:, 2 + 2 * (t % 2) + half, :], y_t[:, k, t * P:(t + 1) * P],
                                           wo[:, k, half * 512:half * 512 + 512], start=(k == 2), stop=(k == 1))
                    return mm

                n = 0
                for k in (2, 3, 4, 5, 6, 7, 0, 1):
                    if k == 0:
                        pe.wait_ge(s_yt_a, 6)
                        pe.wait_ge(s_yt_v, 6)
                        pe.wait_ge(s_wo, 16 * DC)
                        project(0, range(2, 8))
                        pe.wait_ge(s_yn, 1)
                    for g in range(2):
                        if n >= 2:
                            pe.wait_ge((s_yt_a, s_yt_v)[n % 2], n // 2)
                        for i in range(4):
                            mm = pe.transpose(bank[:, n % 2, i * P:(i + 1) * P], y[:, 4 * g + i, k * P:(k + 1) * P], ident[:, :])
                        mm.then_inc(s_yt, 1)
                        n += 1
                pe.wait_ge(s_yt_a, 8)
                pe.wait_ge(s_yt_v, 8)
                for t in range(NT):
                    if t >= 2:
                        pe.wait_ge(s_x1_done, t - 1)
                    project(t, (0, 1) if t == 0 else (2, 3, 4, 5, 6, 7, 0, 1)).then_inc(s_wout, 1)

            @block.scalar
            def _(act):
                act.wait_ge(s_sqr, 1)
                act.activation(sub_s[:, 1, :], sub_s[:, 0, :], ACT.Sqrt, bias=eps_col[:, :], scale=1.0 / HD).then_inc(s_sqr, 1)
                order = [(k, g) for k in (2, 3, 4, 5, 6, 7, 0, 1) for g in range(2)]
                for n in range(0, 16, 2):
                    k, g = order[n]
                    act.wait_ge(s_yt, n + 1)
                    act.copy(y_t[:, k, g * 512:g * 512 + 512], bank[:, 0, :]).then_inc(s_yt_a, 1)
                for t in range(NT):
                    act.wait_ge(s_x1_done, t + 1)
                    act.activation(sq2[:, :], x1[:, t, :], ACT.Square, accum_out=rs_moe[:, 0, t:t + 1]).then_inc(s_sq4, 1)
                    act.wait_ge(s_sq4, t + 1)
                    act.activation(rs_moe[:, 1, t:t + 1], rs_moe[:, 0, t:t + 1], ACT.Sqrt, bias=eps_col[:, :], scale=1.0 / D).then_inc(s_sd4, 1)

            @block.vector
            def _(dve):
                yd = y[:, :, 0:NH * HD].rearrange("p t (h d) -> p t h d", h=NH)
                for t in range(NT):
                    link(dve.tensor_tensor(sub[:, t, :, :], yd[:, t, :, :], yd[:, t, :, :], ALU.mult))
                link(dve.reduce_sum(sub_s[:, 0, :], sub[:, :, :, :].rearrange("p t h d -> p (t h) d"), AX_X))
                dve.sem_inc(s_sqr, 1)
                dve.wait_ge(s_sub, 16)
                link(dve.tensor_scalar(sub_g[:, :], sub_g[:, :], 1.0 - LAM_INIT, None, ALU.mult))
                dve.wait_ge(s_sqr, 2)
                link(dve.reciprocal(sub_s[:, 2, :], sub_s[:, 1, :]))
                for t in range(NT):
                    r = sub_s[:, 2, t * NH:(t + 1) * NH].rearrange("p (h a) -> p h a", a=1).to_broadcast([P, NH, HD])
                    link(dve.tensor_tensor(yd[:, t, :, :], yd[:, t, :, :], r, ALU.mult))
                    link(dve.tensor_tensor(yd[:, t, :, :], yd[:, t, :, :],
                                           sub_g[:, :].rearrange("p (a d) -> p a d", a=1).to_broadcast([P, NH, HD]), ALU.mult))
                dve.sem_inc(s_yn, 1)
                order = [(k, g) for k in (2, 3, 4, 5, 6, 7, 0, 1) for g in range(2)]
                for m in range(1, 16, 2):
                    k, g = order[m]
                    dve.wait_ge(s_yt, m + 1)
                    dve.tensor_copy(y_t[:, k, g * 512:g * 512 + 512], bank[:, 1, :]).then_inc(s_yt_v, 1)
                for t in range(NT):
                    dve.wait_ge(s_wout, t + 1)
                    dve.wait_ge(s_xr[t], 16)
                    acc = bank[:, 2 + 2 * (t % 2):4 + 2 * (t % 2), :].rearrange("p a b -> p (a b)")
                    o = sub[:, 4 * (t % 2):4 * (t % 2) + 4, :, :].rearrange("p a b c -> p (a b c)")
                    link(dve.tensor_tensor(o, acc, gate_attn[:, :], ALU.mult))
                    dve.tensor_tensor(x1[:, t, :], x1[:, t, :], o, ALU.add).then_inc(s_x1_done, 1)
        po.close()
        heads.close()

        rt = ExitStack()
        over = ctx.enter_context(nc.sbuf_tensor("over", [1, 64], I32))
        g_fin = ctx.enter_context(nc.sbuf_tensor("g_fin", [P, D], F32))
        ex = ExitStack()
        e_ = lambda name, shape, dt=F32: ex.enter_context(nc.sbuf_tensor(name, shape, dt))
        wg = [e_(f"wg{i}", [P, DC, DF]) for i in range(2)]
        wu = [e_("wu0", [P, DC, DF])]
        wd = [e_("wd0", [P, FC, D])]
        gate_v = exp_w_gate[0].rearrange("e (k p) f -> e p k f", p=P)
        up_v = exp_w_up[0].rearrange("e (k p) f -> e p k f", p=P)
        down_v = exp_w_down[0].rearrange("e (k p) d -> e p k d", p=P)
        s_gu = [sem(f"s_gu{i}") for i in range(2)]
        s_dn = [sem(f"s_dn{i}") for i in range(2)]
        r_ = lambda name, shape, dt=F32: rt.enter_context(nc.sbuf_tensor(name, shape, dt))
        xn = r_("xn", [P, NT, D])
        h2_t = r_("h2_t", [P, DC, T])
        rw = r_("rw", [P, DC, NE])
        rb = r_("rb", [P, NE])
        aff = r_("aff", [P, NT, NE])
        sel = r_("sel", [P, NT, NE])
        top = r_("top", [P, NT, 8, 8])
        gsum = r_("gsum", [P, NT, 8])
        gmax = r_("gmax", [P, NT, 8])
        gidx = r_("gidx", [P, NT, 8], U32)
        gidx_f = r_("gidx_f", [P, NT, 8])
        keep = r_("keep", [P, NT, NE])
        hot = r_("hot", [P, 2, NT, NE])
        both = r_("both", [P, NT, NE])
        tiles_before = r_("tiles_before", [P, NT + 1, NE])
        before = r_("before", [P, NT, NE])
        tmp = r_("tmp", [P, NT, NE])
        iota_e = r_("iota_e", [P, NE])
        iota_g = r_("iota_g", [P, NE])
        steps = r_("steps", [P, 8])
        counts = r_("counts", [P, NE])
        cmp8 = r_("cmp8", [P, NE, 8])
        first = r_("first", [P, NE])
        ov_row = r_("ov_row", [P, NE])
        ovn = r_("ovn", [P, NE])
        ov_end = r_("ov_end", [P, NE])
        ov_base = r_("ov_base", [P, NE])
        ones_row = r_("ones_row", [P, NE])
        iota_b = r_("iota_b", [1, NOV_T])
        ended = r_("ended", [1, NOV_T, NE])
        begun = h2_t[0:1, 0, :].rearrange("p (b e) -> p b e", e=NE)
        over_f = r_("over_f", [1, 2 * NOV_T + 1])
        rank = r_("rank", [P, NT, 8])
        slot_f = r_("slot_f", [P, NT, 2])
        s_ld4 = sem("s_ld4")
        s_g6 = sem("s_g6")
        s_iota = sem("s_iota")
        s_xn4 = sem("s_xn4")
        s_tr4 = sem("s_tr4")
        s_h_a = sem("s_h_a")
        s_h_v = sem("s_h_v")
        s_log = sem("s_log")
        s_sig = sem("s_sig")
        s_both = sem("s_both")
        s_pre = sem("s_pre")
        s_slot = sem("s_slot")
        s_starts = sem("s_starts")
        s_scat = sem("s_scat")
        with nc.Block() as block:
            @block.sync
            def _(sp):
                sp.dma_start(rw[:, :, :], router_w.rearrange("(k p) e -> p k e", p=P)).then_inc(s_ld4, 16)
                sp.dma_start(rb[:, :], router_b.rearrange("(a e) -> a e", a=1).to_broadcast([P, NE])).then_inc(s_ld4, 16)
                sp.dma_start(g_fin[:, :], norm_final_g.rearrange("(a d) -> a d", a=1).to_broadcast([P, D])).then_inc(s_g6, 16)
                sp.dma_start(wg[0][:, :, :], gate_v[0]).then_inc(s_gu[0], 16)
                sp.dma_start(wu[0][:, :, :], up_v[0]).then_inc(s_gu[0], 16)
                sp.dma_start(wd[0][:, :, :], down_v[0]).then_inc(s_dn[0], 16)
                sp.dma_start(wg[1][:, :, :], gate_v[1]).then_inc(s_gu[1], 16)

            @block.gpsimd
            def _(pool):
                imp = dict(allow_small_or_imprecise_dtypes=True)
                pool.iota(iota_e[:, :], pattern=[[1, NE]], base=0, channel_multiplier=0, **imp).then_inc(s_iota, 1)
                pool.iota(iota_g[:, :], pattern=[[1, 8], [0, 8]], base=0, channel_multiplier=0, **imp).then_inc(s_iota, 1)
                pool.iota(steps[:, :], pattern=[[EB, 8]], base=EB, channel_multiplier=0, **imp).then_inc(s_iota, 1)
                pool.iota(iota_b[:, :], pattern=[[1, NOV_T]], base=0, channel_multiplier=0, **imp).then_inc(s_iota, 1)
                pool.memset(ones_row[:, :], 1.0).then_inc(s_iota, 1)
                pool.wait_ge(s_slot, 1)
                for t in range(NT):
                    for j in range(2):
                        pool.indirect_dma_start(
                            out=slots_in, out_offset=bass.IndirectOffsetOnAxis(ap=row_slot[:, t, j:j + 1].bitcast(U32), axis=0),
                            in_=xn[:, t, :], in_offset=None).then_inc(s_scat, 16)
                pool.wait_ge(s_scat, 16 * 2 * NT)

            @block.tensor
            def _(pe):
                n = 0
                for g in range(2):
                    for k in range(DC):
                        for i in range(4):
                            t = 4 * g + i
                            if k == 0:
                                pe.wait_ge(s_xn4, t + 1)
                            if i == 0 and n >= 2:
                                pe.wait_ge((s_h_a, s_h_v)[n % 2], n // 2)
                            mm = pe.transpose(bank[:, n % 2, i * P:(i + 1) * P], xn[:, t, k * P:(k + 1) * P], ident[:, :])
                        mm.then_inc(s_tr4, 1)
                        n += 1
                    pe.wait_ge(s_h_a, 4 * g + 4)
                    pe.wait_ge(s_h_v, 4 * g + 4)
                    pe.wait_ge(s_ld4, 32)
                    for i in range(4):
                        t = 4 * g + i
                        for k in range(DC):
                            mm = pe.matmul(bank[:, 2, t * NE:(t + 1) * NE], h2_t[:, k, t * P:(t + 1) * P], rw[:, k, :],
                                           start=(k == 0), stop=(k == DC - 1))
                mm.then_inc(s_log, 1)
                pe.wait_ge(s_both, 1)
                flat = lambda ap: ap.rearrange("p t e -> p (t e)")
                pe.matmul(bank[:, 3, :], ones[:, :], flat(tiles_before[:, 0:NT, :]), start=True, stop=False)
                pe.matmul(bank[:, 3, :], earlier[:, :], flat(both[:, :, :]), start=False, stop=True)
                mm = pe.matmul(bank[:, 4, 0:NE], ones[:, :], tiles_before[:, NT, :], start=True, stop=True)
                mm.then_inc(s_pre, 1)

            @block.scalar
            def _(act):
                for n in range(0, 16, 2):
                    k, g = n % 8, n // 8
                    act.wait_ge(s_tr4, n + 1)
                    act.activation(h2_t[:, k, g * 512:g * 512 + 512], bank[:, 0, :], ACT.Identity, bias=mod_cols[:, 24 + k:25 + k],
                                   scale=gain_moe[:, k:k + 1]).then_inc(s_h_a, 1)
                act.wait_ge(s_log, 1)
                act.activation(aff[:, :, :].rearrange("p t e -> p (t e)"), bank[:, 2, :], ACT.Exp, scale=-1.0).then_inc(s_sig, 1)

            @block.vector
            def _(dve):
                def wide(ap, shape, spec, **kw):
                    return ap.rearrange(spec, **kw).to_broadcast(shape)

                def norm(t):
                    dve.wait_ge(s_sd4, t + 1)
                    link(dve.reciprocal(rs_moe[:, 2, t:t + 1], rs_moe[:, 1, t:t + 1]))
                    dve.tensor_scalar(xn[:, t, :], x1[:, t, :], rs_moe[:, 2, t:t + 1], None, ALU.mult).then_inc(s_xn4, 1)

                for t in range(NT):
                    norm(t)
                for m in range(1, 16, 2):
                    k, g = m % 8, m // 8
                    dve.wait_ge(s_tr4, m + 1)
                    dve.tensor_scalar(h2_t[:, k, g * 512:g * 512 + 512], bank[:, 1, :], gain_moe[:, k:k + 1],
                                      mod_cols[:, 24 + k:25 + k], ALU.mult, ALU.add).then_inc(s_h_v, 1)
                dve.wait_ge(s_sig, 1)
                dve.wait_ge(s_ld4, 32)
                link(dve.tensor_scalar(aff[:, :, :], aff[:, :, :], 1.0, None, ALU.add))
                link(dve.reciprocal(aff[:, :, :], aff[:, :, :]))
                link(dve.tensor_tensor(sel[:, :, :], aff[:, :, :], wide(rb[:, :], [P, NT, NE], "p (a e) -> p a e", a=1), ALU.add))
                for t in range(NT):
                    for g in range(8):
                        last = dve.max(out=top[:, t, g, :], in_=sel[:, t, 8 * g:8 * g + 8])
                link(last)
                link(dve.tensor_tensor(gsum[:, :, :], top[:, :, :, 0], top[:, :, :, 1], ALU.add))
                for t in range(NT):
                    last = dve.max(out=gmax[:, t, :], in_=gsum[:, t, :])
                link(last)
                for t in range(NT):
                    last = dve.max_index(out=gidx[:, t, :], in_max=gmax[:, t, :], in_values=gsum[:, t, :])
                link(last)
                link(dve.tensor_copy(gidx_f[:, :, :], gidx[:, :, :]))
                dve.wait_ge(s_iota, 5)
                link(dve.tensor_tensor(keep[:, :, :], wide(iota_g[:, :], [P, NT, NE], "p (a e) -> p a e", a=1),
                                       gidx_f[:, :, 0:1].to_broadcast([P, NT, NE]), ALU.is_equal))
                link(dve.tensor_tensor(sel[:, :, :], sel[:, :, :], keep[:, :, :], ALU.mult))
                link(dve.tensor_scalar(keep[:, :, :], keep[:, :, :], -1.0, 1e30, ALU.add, ALU.mult))
                link(dve.tensor_tensor(sel[:, :, :], sel[:, :, :], keep[:, :, :], ALU.add))
                for t in range(NT):
                    last = dve.max(out=gmax[:, t, :], in_=sel[:, t, :])
                link(last)
                for t in range(NT):
                    last = dve.max_index(out=gidx[:, t, :], in_max=gmax[:, t, :], in_values=sel[:, t, :])
                link(last)
                link(dve.tensor_copy(gidx_f[:, :, :], gidx[:, :, :]))
                for j in range(2):
                    link(dve.tensor_tensor(hot[:, j, :, :], wide(iota_e[:, :], [P, NT, NE], "p (a e) -> p a e", a=1),
                                           gidx_f[:, :, j:j + 1].to_broadcast([P, NT, NE]), ALU.is_equal))
                link(dve.memset(tiles_before[:, 0, :], 0.0))
                link(dve.tensor_tensor(both[:, :, :], hot[:, 0, :, :], hot[:, 1, :, :], ALU.add))
                for t in range(NT):
                    link(dve.tensor_tensor(tiles_before[:, t + 1, :], tiles_before[:, t, :], both[:, t, :], ALU.add))
                dve.sem_inc(s_both, 1)

                def pick(o, table, j):
                    link(dve.tensor_tensor(tmp[:, :, :], hot[:, j, :, :], table, ALU.mult))
                    link(dve.reduce_sum(o, tmp[:, :, :], AX_X))

                for j in range(2):
                    pick(rank[:, :, j], aff[:, :, :], j)
                link(dve.tensor_tensor(rank[:, :, 2], rank[:, :, 0], rank[:, :, 1], ALU.add))
                link(dve.reciprocal(rank[:, :, 2], rank[:, :, 2]))
                for j in range(2):
                    link(dve.tensor_tensor(row_gate[:, :, j], rank[:, :, j], rank[:, :, 2], ALU.mult))
                dve.wait_ge(s_pre, 1)
                link(dve.tensor_copy(before[:, :, :].rearrange("p t e -> p (t e)"), bank[:, 3, :]))
                link(dve.tensor_copy(counts[:, :], bank[:, 4, 0:NE]))
                link(dve.tensor_tensor_scan(first[:, :], ones_row[:, :], counts[:, :], 0.0, ALU.mult, ALU.add))
                link(dve.tensor_tensor(first[:, :], first[:, :], counts[:, :], ALU.subtract))
                dve.tensor_copy(starts[:, :], first[0:1, :]).then_inc(s_starts, 1)
                dve.tensor_copy(sizes[:, :], counts[0:1, :]).then_inc(s_starts, 1)
                wide_e = lambda ap: wide(ap, [P, NT, NE], "p (a e) -> p a e", a=1)

                def slots(o, table):
                    for j in range(2):
                        pick(o[:, :, j], table, j)

                link(dve.tensor_tensor(keep[:, :, :], before[:, :, :], wide_e(first[:, :]), ALU.add))
                slots(slot_f, keep[:, :, :])
                link(dve.tensor_copy(row_slot[:, :, :], slot_f[:, :, :]))
                dve.sem_inc(s_slot, 1)
                link(dve.tensor_tensor(cmp8[:, :, :], wide(counts[:, :], [P, NE, 8], "p (e a) -> p e a", a=1),
                                       wide(steps[:, :], [P, NE, 8], "p (a s) -> p a s", a=1), ALU.is_gt))
                link(dve.reduce_sum(ovn[:, :], cmp8[:, :, :], AX_X))
                link(dve.tensor_tensor_scan(ov_end[:, :], ones_row[:, :], ovn[:, :], 0.0, ALU.mult, ALU.add))
                link(dve.tensor_tensor(ov_base[:, :], ov_end[:, :], ovn[:, :], ALU.subtract))
                cmp_b = lambda ap: (wide(ap, [1, NOV_T, NE], "p (a e) -> p a e", a=1),
                                    wide(iota_b[:, :], [1, NOV_T, NE], "p (b a) -> p b a", a=1))
                link(dve.tensor_tensor(ended[:, :, :], *cmp_b(ov_end[0:1, :]), ALU.is_le))
                link(dve.reduce_sum(over_f[:, 0:NOV_T], ended[:, :, :], AX_X))
                link(dve.tensor_scalar(over_f[:, 0:NOV_T], over_f[:, 0:NOV_T], float(NE - 1), None, ALU.min))
                link(dve.tensor_scalar(ov_row[:, :], ov_base[:, :], float(EB), None, ALU.mult))
                link(dve.tensor_tensor(ov_row[:, :], first[:, :], ov_row[:, :], ALU.subtract))
                link(dve.tensor_tensor(begun[:, :, :], *cmp_b(ov_base[0:1, :]), ALU.is_le))
                link(dve.tensor_tensor(begun[:, :, :], begun[:, :, :], ended[:, :, :], ALU.subtract))
                link(dve.tensor_tensor(begun[:, :, :], begun[:, :, :], wide(ov_row[0:1, :], [1, NOV_T, NE], "p (a e) -> p a e", a=1), ALU.mult))
                link(dve.reduce_sum(over_f[:, NOV_T:2 * NOV_T], begun[:, :, :], AX_X))
                link(dve.tensor_scalar(iota_b[:, :], iota_b[:, :], float(EB), float(EB), ALU.mult, ALU.add))
                link(dve.tensor_tensor(over_f[:, NOV_T:2 * NOV_T], over_f[:, NOV_T:2 * NOV_T], iota_b[:, :], ALU.add))
                link(dve.tensor_copy(over_f[:, 2 * NOV_T:2 * NOV_T + 1], ov_end[0:1, NE - 1:NE]))
                link(dve.tensor_copy(over[:, 0:2 * NOV_T + 1], over_f[:, :]))
                link(dve.tensor_scalar(ov_row[:, :], ov_row[:, :], -1.0, float(IN_ROWS - EB), ALU.mult, ALU.add))
                link(dve.tensor_scalar(before[:, :, :], before[:, :, :], float(EB), None, ALU.is_ge))
                link(dve.tensor_tensor(before[:, :, :], before[:, :, :], wide_e(ov_row[:, :]), ALU.mult))
                link(dve.tensor_tensor(keep[:, :, :], keep[:, :, :], before[:, :, :], ALU.add))
                slots(slot_f, keep[:, :, :])
                link(dve.tensor_copy(row_out[:, :, :], slot_f[:, :, :]))
        rt.close()

        wu.append(e_("wu1", [P, DC, DF]))
        wd.append(e_("wd1", [P, FC, D]))
        xe = [e_(f"xe{i}", [EB, D]) for i in range(2)]
        xe_mid = e_("xe_mid", [P, DC, EB])
        xe_t = e_("xe_t", [P, DC, EB])
        act_h = [e_(f"act_h{i}", [EB, DF]) for i in range(2)]
        act_t = e_("act_t", [P, FC, EB])
        oe = e_("oe", [EB, D])
        gain_half = e_("gain_half", [P, DC])
        shift_half = e_("shift_half", [P, DC])
        gate_half = e_("gate_half", [P, DF])

        s_xe = [sem(f"s_xe{i}") for i in range(2)]
        s_xt5 = sem("s_xt5")
        s_xt_ok = sem("s_xt_ok")
        s_gu_done = sem("s_gu_done")
        s_e5 = sem("s_e5")
        s_t5 = sem("s_t5")
        s_d5 = sem("s_d5")
        s_r5 = sem("s_r5")
        s_g5 = sem("s_g5")
        s_h5 = sem("s_h5")
        s_ht5 = sem("s_ht5")
        s_hc5 = sem("s_hc5")
        s_down = sem("s_down")
        s_oe_v = sem("s_oe_v")
        s_out5 = sem("s_out5")
        gate_up = [bank[:, 2 * i:2 * i + 2, :] for i in range(2)]
        rows_t = bank[:, 4:6, :].rearrange("p a b -> p (a b)")
        DOWN, ACT_T = 6, 7

        def transposed_rows(pe, buf, full):
            for k in range(DC if full else DC // 2):
                mm = pe.transpose(rows_t[:, k * P:(k + 1) * P], xe[buf][:, k * P:(k + 1) * P], ident[:, :])
            return mm

        def rows_of_chunk(k, full):
            x = xe_t[:, :, :].rearrange("p k t -> p (k t)")
            return x[:, k * EB:(k + 1) * EB] if full else x[:, (k % 4 * 2 + k // 4) * HB:(k % 4 * 2 + k // 4 + 1) * HB]

        def gate_and_up(pe, buf, full):
            for i, w in enumerate((wg[buf], wu[buf])):
                for k in range(DC):
                    ends = dict(start=(k == 0), stop=(k == DC - 1))
                    if full:
                        mm = pe.matmul(gate_up[buf][:, i, :], rows_of_chunk(k, full), w[:, k, :], **ends)
                        continue
                    for h in range(2):
                        mm = pe.matmul(gate_up[buf][h * HB:(h + 1) * HB, i, 0:DF // 2], rows_of_chunk(k, full),
                                       w[:, k, h * DF // 2:(h + 1) * DF // 2], **ends)
            return mm

        def transposed_act(pe, buf, full):
            for m in range(FC if full else FC // 2):
                mm = pe.transpose(bank[:, ACT_T, m * P:(m + 1) * P], act_h[buf][:, m * P:(m + 1) * P], ident[:, :])
            return mm

        def down(pe, buf, full):
            flat = act_t[:, :, :].rearrange("p m t -> p (m t)")
            for m in range(FC):
                ends = dict(start=(m == 0), stop=(m == FC - 1))
                at = m * EB if full else (m % 2 * 2 + m // 2) * HB
                for half in range(2):
                    w = wd[buf][:, m, half * 512:half * 512 + 512]
                    if full:
                        mm = pe.matmul(bank[:, DOWN + half, :], flat[:, at:at + EB], w, **ends)
                    else:
                        mm = pe.matmul(bank[half * HB:(half + 1) * HB, DOWN, :], flat[:, at:at + HB], w, **ends)
            return mm

        def modulate(dve, full, s_mid, mid, s_done):
            n = EB if full else HB
            as_rows = lambda ap: ap.rearrange("p (k t) -> p k t", k=DC)
            wide_t = lambda ap: ap.rearrange("p (k a) -> p k a", a=1).to_broadcast([P, DC, n])
            mid_rows = as_rows(xe_mid[:, :, :].rearrange("p k t -> p (k t)")[:, 0:DC * n])
            out_rows = as_rows(xe_t[:, :, :].rearrange("p k t -> p (k t)")[:, 0:DC * n])
            gain, shift = (gain_moe[:, :], mod_cols[:, 24:32]) if full else (gain_half[:, :], shift_half[:, :])
            dve.tensor_tensor(mid_rows, as_rows(rows_t[:, 0:DC * n]), wide_t(gain), ALU.mult).then_inc(s_mid, 1)
            dve.wait_ge(s_mid, mid)
            dve.tensor_tensor(out_rows, mid_rows, wide_t(shift), ALU.add).then_inc(s_done, 1)

        def exp_gate(act, buf, full, s_done):
            w = DF if full else DF // 2
            act.activation(act_h[buf][:, 0:w], gate_up[buf][:, 0, 0:w], ACT.Exp, scale=-1.0).then_inc(s_done, 1)

        def silu_times_up(dve, buf, full, sems, value, s_done):
            w = DF if full else DF // 2
            h = act_h[buf][:, 0:w]
            dve.tensor_scalar(h, h, 1.0, None, ALU.add).then_inc(sems[0], 1)
            dve.wait_ge(sems[0], value)
            dve.reciprocal(h, h).then_inc(sems[1], 1)
            dve.wait_ge(sems[1], value)
            dve.tensor_tensor(h, h, gate_up[buf][:, 0, 0:w], ALU.mult).then_inc(sems[2], 1)
            dve.wait_ge(sems[2], value)
            dve.tensor_tensor(h, h, gate_up[buf][:, 1, 0:w], ALU.mult).then_inc(s_done, 1)

        def copy_act(act, full, s_done):
            w = DF if full else DF // 2
            act.copy(act_t[:, :, :].rearrange("p m t -> p (m t)")[:, 0:w], bank[:, ACT_T, 0:w]).then_inc(s_done, 1)

        def gated_out(dve, full, s_done):
            if full:
                dve.tensor_tensor(oe[:, :], bank[:, 6:8, :].rearrange("p a b -> p (a b)"), gate_moe[:, :], ALU.mult).then_inc(s_done, 1)
            else:
                dve.tensor_tensor(oe[:, 0:512], bank[:, DOWN, :], gate_half[:, :], ALU.mult).then_inc(s_done, 1)

        def halves(table, row, full, tile):
            for h in range(2):
                part = tile[h * HB:(h + 1) * HB, :]
                if full:
                    yield table[ds(row + h * HB, HB), :], part
                else:
                    yield table[ds(row, HB), h * 512:h * 512 + 512], part[:, 0:512]

        def row_start(eng, n):
            return eng.value_load(starts[0:1, ds(n, 1)], min_val=0, max_val=2 * T)

        def by_size(eng, n, stage):
            rows = eng.value_load(sizes[0:1, ds(n, 1)], min_val=0, max_val=T)
            with eng.If(rows > HB):
                stage(True)
            with eng.If(rows < HB + 1):
                stage(False)

        with nc.Block() as block:
            @block.sync
            def _(sp):
                def load_gate_up(n, b):
                    sp.wait_ge(s_gu_done, n + 1)
                    sp.dma_start(wg[b][:, :, :], gate_v[ds(n, 1)].rearrange("a p k f -> p (a k) f")).then_inc(s_gu[b], 16)
                    sp.dma_start(wu[b][:, :, :], up_v[ds(n, 1)].rearrange("a p k f -> p (a k) f")).then_inc(s_gu[b], 16)

                def load_down(n, b):
                    sp.wait_ge(s_down, n + 1)
                    sp.dma_start(wd[b][:, :, :], down_v[ds(n, 1)].rearrange("a p k d -> p (a k) d")).then_inc(s_dn[b], 16)

                sp.wait_ge(s_xe[0], 32)
                sp.dma_start(wu[1][:, :, :], up_v[1]).then_inc(s_gu[1], 16)
                with sp.Fori(0, NE // 2 - 1) as it:
                    for b in (1, 0):
                        load_gate_up(it * 2 + 3 - b, 1 - b)
                        load_down(it * 2 + 2 - b, b)
                load_down(NE - 1, 1)

            @block.tensor
            def _(pe):
                pe.sem_inc(s_gu_done, 2)
                pe.sem_inc(s_down, 2)

                def take_rows(n, b, loads):
                    def stage(full):
                        pe.wait_ge(s_xe[b], loads)
                        transposed_rows(pe, b, full).then_inc(s_xt5, 1)
                    by_size(pe, n, stage)

                def first_products(n, b, loads):
                    def stage(full):
                        pe.wait_ge(s_gu[b], loads)
                        pe.wait_ge(s_xt_ok, n + 1)
                        pe.wait_ge(s_h5, n + 1)
                        gate_and_up(pe, b, full).then_inc(s_gu_done, 1)
                    by_size(pe, n, stage)

                def turn_act(n, b):
                    def stage(full):
                        pe.wait_ge(s_h5, n + 3)
                        pe.wait_ge(s_oe_v, n + 1)
                        transposed_act(pe, b, full).then_inc(s_ht5, 1)
                    by_size(pe, n, stage)

                def last_product(n, b, loads):
                    def stage(full):
                        pe.wait_ge(s_dn[b], loads)
                        pe.wait_ge(s_hc5, n + 1)
                        down(pe, b, full).then_inc(s_down, 1)
                    by_size(pe, n, stage)

                def step(n, b, gu_loads, dn_loads, xe_loads):
                    first_products(n, b, gu_loads)
                    turn_act(n - 1, 1 - b)
                    if xe_loads is not None:
                        take_rows(n + 1, 1 - b, xe_loads)
                    last_product(n - 1, 1 - b, dn_loads)

                take_rows(0, 0, 32)
                first_products(0, 0, 32)
                take_rows(1, 1, 32)
                with pe.Fori(0, NE // 2 - 1) as it:
                    step(it * 2 + 1, 1, it * 32 + 32, it * 16 + 16, it * 32 + 64)
                    step(it * 2 + 2, 0, it * 32 + 64, it * 16 + 16, it * 32 + 64)
                step(NE - 1, 1, 16 * NE, 8 * NE, None)
                turn_act(NE - 1, 1)
                last_product(NE - 1, 1, 8 * NE)

            @block.scalar
            def _(act):
                act.sem_inc(s_out5, 32)

                def load_rows(n, b):
                    start = row_start(act, n)

                    def stage(full):
                        if not (isinstance(n, int) and n < 2):
                            act.wait_ge(s_xt5, n - 1)
                        for rows, tile in halves(slots_in, start, full, xe[b]):
                            act.dma_start(tile, rows).then_inc(s_xe[b], 16)
                    by_size(act, n, stage)

                def exponentials(n, b):
                    def stage(full):
                        act.wait_ge(s_gu_done, n + 3)
                        exp_gate(act, b, full, s_e5)
                    by_size(act, n, stage)

                def rest(n):
                    start = row_start(act, n)

                    def stage(full):
                        act.wait_ge(s_ht5, n + 1)
                        copy_act(act, full, s_hc5)
                        act.wait_ge(s_out5, n * 32 + 32)
                        act.wait_ge(s_oe_v, n + 2)
                        for rows, tile in halves(slots_out, start, full, oe):
                            act.dma_start(rows, tile).then_inc(s_out5, 16)
                    by_size(act, n, stage)

                for b in range(2):
                    load_rows(b, b)
                exponentials(0, 0)
                with act.Fori(0, NE // 2 - 1) as it:
                    for b in (1, 0):
                        n = it * 2 + 2 - b
                        load_rows(n + 1, 1 - b)
                        exponentials(n, b)
                        rest(n - 1)
                exponentials(NE - 1, 1)
                rest(NE - 2)
                rest(NE - 1)
                act.wait_ge(s_out5, 32 * (NE + 1))

            @block.vector
            def _(dve):
                dve.sem_inc(s_oe_v, 1)
                dve.sem_inc(s_h5, 2)
                side_by_side = lambda ap: ap.rearrange("p (j h) -> p h j", h=2)
                apart = lambda ap: ap.rearrange("p (h j) -> p h j", h=2)
                link(dve.tensor_copy(side_by_side(gain_half[:, :]), apart(gain_moe[:, :])))
                link(dve.tensor_copy(side_by_side(shift_half[:, :]), apart(mod_cols[:, 24:32])))
                for h in range(2):
                    link(dve.tensor_copy(gate_half[h * HB:(h + 1) * HB, :], gate_moe[h * HB:(h + 1) * HB, h * 512:h * 512 + 512]))

                def take_rows(n):
                    def stage(full):
                        dve.wait_ge(s_xt5, n + 1)
                        modulate(dve, full, s_t5, n + 1, s_xt_ok)
                    by_size(dve, n, stage)

                def products(n, b):
                    def stage(full):
                        dve.wait_ge(s_e5, n + 1)
                        silu_times_up(dve, b, full, (s_d5, s_r5, s_g5), n + 1, s_h5)
                    by_size(dve, n, stage)

                def outputs(n):
                    def stage(full):
                        dve.wait_ge(s_down, n + 3)
                        dve.wait_ge(s_out5, n * 32 + 32)
                        gated_out(dve, full, s_oe_v)
                    by_size(dve, n, stage)

                take_rows(0)
                take_rows(1)
                products(0, 0)
                with dve.Fori(0, NE // 2 - 1) as it:
                    for b in (1, 0):
                        n = it * 2 + 2 - b
                        take_rows(n + 1)
                        products(n, b)
                        outputs(n - 1)
                products(NE - 1, 1)
                outputs(NE - 2)
                outputs(NE - 1)

        s_v_load = sem("s_v_load")
        s_v_t = sem("s_v_t")
        s_v_gu = sem("s_v_gu")
        s_v_e = sem("s_v_e")
        s_v_h = sem("s_v_h")
        s_v_ht = sem("s_v_ht")
        s_v_hc = sem("s_v_hc")
        s_v_dn = sem("s_v_dn")
        s_v_o = sem("s_v_o")
        s_v_st = sem("s_v_st")
        s_v_end = sem("s_v_end")
        with nc.Block() as block:
            def used_blocks(eng):
                count = eng.value_load(over[0:1, 2 * NOV_T:2 * NOV_T + 1], min_val=0, max_val=NOV)
                return count

            @block.sync
            def _(sp):
                count = used_blocks(sp)
                sp.sem_inc(s_v_st, 16)
                with sp.If(count > 0):
                    with sp.Fori(0, NOV) as n:
                        with sp.If(n < count):
                            e = sp.value_load(over[0:1, ds(n, 1)], min_val=0, max_val=NE - 1)
                            start = sp.value_load(over[0:1, ds(n + NOV_T, 1)], min_val=0, max_val=2 * T)
                            sp.wait_ge(s_v_st, n * 16 + 16)
                            sp.dma_start(wg[0][:, :, :], gate_v[ds(e, 1)].rearrange("a p k f -> p (a k) f")).then_inc(s_v_load, 16)
                            sp.dma_start(wu[0][:, :, :], up_v[ds(e, 1)].rearrange("a p k f -> p (a k) f")).then_inc(s_v_load, 16)
                            sp.dma_start(wd[0][:, :, :], down_v[ds(e, 1)].rearrange("a p k d -> p (a k) d")).then_inc(s_v_load, 16)
                            sp.dma_start(xe[0][:, :], slots_in[ds(start, EB), :]).then_inc(s_v_load, 16)
                            sp.wait_ge(s_v_o, n + 1)
                            sp.dma_start(slots_out[ds(n * EB + IN_ROWS, EB), :], oe[:, :]).then_inc(s_v_st, 16)

            @block.tensor
            def _(pe):
                count = used_blocks(pe)
                with pe.If(count > 0):
                    with pe.Fori(0, NOV) as n:
                        with pe.If(n < count):
                            pe.wait_ge(s_v_load, n * 64 + 64)
                            pe.matmul(bank[:, 7, 0:P], ident[:, :], ident[:, :], start=True, stop=True)
                            transposed_rows(pe, 0, True).then_inc(s_v_t, 1)
                            pe.wait_ge(s_xt_ok, n + (NE + 1))
                            gate_and_up(pe, 0, True).then_inc(s_v_gu, 1)
                            pe.wait_ge(s_v_h, n + 1)
                            transposed_act(pe, 0, True).then_inc(s_v_ht, 1)
                            pe.wait_ge(s_v_hc, n + 1)
                            down(pe, 0, True).then_inc(s_v_dn, 1)

            @block.scalar
            def _(act):
                count = used_blocks(act)
                with act.If(count > 0):
                    with act.Fori(0, NOV) as n:
                        with act.If(n < count):
                            act.wait_ge(s_v_gu, n + 1)
                            exp_gate(act, 0, True, s_v_e)
                            act.wait_ge(s_v_ht, n + 1)
                            copy_act(act, True, s_v_hc)
                act.wait_ge(s_v_st, count * 16 + 16)
                act.copy(act_h[1][:, 0:1], ones[:, 0:1]).then_inc(s_v_end, 1)

            @block.vector
            def _(dve):
                count = used_blocks(dve)
                with dve.If(count > 0):
                    with dve.Fori(0, NOV) as n:
                        with dve.If(n < count):
                            dve.wait_ge(s_v_t, n + 1)
                            modulate(dve, True, s_t5, n + (NE + 1), s_xt_ok)
                            dve.wait_ge(s_v_e, n + 1)
                            silu_times_up(dve, 0, True, (s_d5, s_r5, s_g5), n + (NE + 1), s_v_h)
                            dve.wait_ge(s_v_dn, n + 1)
                            gated_out(dve, True, s_v_o)
        ex.close()

        RING = 3
        c_ = lambda name, shape, dt=F32: ctx.enter_context(nc.sbuf_tensor(name, shape, dt))
        row_a = c_("row_a", [P, RING, D])
        row_b = c_("row_b", [P, RING, D])
        sq6 = c_("sq6", [P, D])
        rs6 = c_("rs6", [P, 3, NT])
        s_rows = [sem(f"s_rows{i}") for i in range(RING)]
        s_x2_done = sem("s_x2_done")
        s_sq6 = sem("s_sq6")
        s_sd6 = sem("s_sd6")
        s_fin = sem("s_fin")
        s_out = sem("s_out")
        out_v = out[0].rearrange("(t p) d -> p t d", p=P)
        with nc.Block() as block:
            @block.sync
            def _(sp):
                for t in range(NT):
                    sp.wait_ge(s_fin, t + 1)
                    sp.dma_start(out_v[:, t, :], x1[:, t, :]).then_inc(s_out, 16)
                sp.wait_ge(s_out, 16 * NT)

            @block.gpsimd
            def _(pool):
                for t in range(NT):
                    if t >= RING:
                        pool.wait_ge(s_x2_done, t - RING + 1)
                    for j, r in enumerate((row_a, row_b)):
                        pool.indirect_dma_start(
                            out=r[:, t % RING, :], out_offset=None, in_=slots_out,
                            in_offset=bass.IndirectOffsetOnAxis(ap=row_out[:, t, j:j + 1].bitcast(U32), axis=0)).then_inc(s_rows[t % RING], 16)

            @block.scalar
            def _(act):
                for t in range(NT):
                    act.wait_ge(s_x2_done, t + 1)
                    act.activation(sq6[:, :], x1[:, t, :], ACT.Square, accum_out=rs6[:, 0, t:t + 1]).then_inc(s_sq6, 1)
                    act.wait_ge(s_sq6, t + 1)
                    act.activation(rs6[:, 1, t:t + 1], rs6[:, 0, t:t + 1], ACT.Sqrt, bias=eps_col[:, :], scale=1.0 / D).then_inc(s_sd6, 1)

            @block.vector
            def _(dve):
                def finish(t):
                    dve.wait_ge(s_sd6, t + 1)
                    link(dve.reciprocal(rs6[:, 2, t:t + 1], rs6[:, 1, t:t + 1]))
                    dve.scalar_tensor_tensor(out=x1[:, t, :], in0=x1[:, t, :], scalar=rs6[:, 2, t:t + 1], in1=g_fin[:, :],
                                             op0=ALU.mult, op1=ALU.mult).then_inc(s_fin, 1)

                dve.wait_ge(s_g6, 16)
                for t in range(NT):
                    dve.wait_ge(s_rows[t % RING], 32 * (t // RING + 1))
                    for j, r in enumerate((row_a, row_b)):
                        last = dve.scalar_tensor_tensor(out=x1[:, t, :], in0=r[:, t % RING, :], scalar=row_gate[:, t, j:j + 1],
                                                        in1=x1[:, t, :], op0=ALU.mult, op1=ALU.add)
                        if j == 0:
                            link(last)
                    last.then_inc(s_x2_done, 1)
                    if t >= 1:
                        finish(t - 1)
                finish(NT - 1)


class Mixer:

    def __init__(self, g, before):
        self.g, self.name, self.K, self.prev, self.rounds = g, g["name"], g["k"], g["prev"], g["rounds"]
        self.is_cmp, self.is_fox, self.is_swa, self.is_diff = (self.name == k for k in ("cmp", "fox", "swa", "diff"))
        self.copies = P // self.K
        self.loads = self.copies * (1 if self.is_cmp else 2 if self.is_diff else 3) + (
            not self.is_fox) + self.is_swa + 2 * self.is_fox
        self.steps = before.steps + 16 * before.rounds if before else 0
        self.jobs_biased = before.jobs_biased + 2 * before.rounds * (not before.is_fox) if before else 0
        self.value_jobs = before.value_jobs + 2 * before.rounds * (not before.is_cmp) if before else 0
        self.load_sum = before.load_sum + 16 * before.loads * before.rounds if before else 0
        self.splits = before.splits + 8 * before.rounds * (before.prev >= 4) if before else 0
        self.factors = before.factors + before.rounds * before.factors_per_round if before else 0
        self.factors_per_round = 8 if self.is_diff else 16 if "gate" in g else 0

    def span(self, i):
        n = min(i, self.prev) + 1
        return i - n + 1, n

    def width(self, i):
        return NC if self.is_cmp else self.span(i)[1] * P

    def blocks(self, i):
        return 1 if self.is_cmp else self.span(i)[1]


def attend(nc, sem, have):
    bank, ident, qb, ka, kb, cq, ck, vb, neg_slope, sink, neg_sink, sink_exp, bias, probs, probs_t, low, total, factor, first_map, spare, pool_spare, nil, zeros, slots_in, slots_out, s_zfill, y, \
        v_tok, kc_t, vc, nsa_gate, neg_lam, row_seen, causal, qk_rows, cum_rows, neg_slopes, swa_sinks = (
            have[k] for k in ("bank ident qb ka kb cq ck vb neg_slope sink neg_sink sink_exp bias probs probs_t low total factor "
                              "first_map spare pool_spare nil zeros slots_in slots_out s_zfill y v_tok kc_t vc nsa_gate neg_lam row_seen causal qk_rows cum_rows "
                              "neg_slopes swa_sinks").split())
    dists = {"diff": have["dist_full"], "sel": have["dist_full"], "win": have["dist_win"], "swa": have["dist_swa"],
             "cmp": have["dist_cmp"]}
    mixers = []
    for g in GROUPS:
        mixers.append(Mixer(g, mixers[-1] if mixers else None))

    s_load = [sem(f"s_load{i}") for i in range(2)]
    s_ones = sem("s_ones")
    s_nsink = sem("s_nsink")
    s_bias7 = sem("s_bias7")
    s_qk = sem("s_qk")
    s_max = sem("s_max")
    s_exp = sem("s_exp")
    s_sink = sem("s_sink")
    s_first = sem("s_first")
    s_tr7 = sem("s_tr7")
    s_cp0 = sem("s_cp0")
    s_cp1 = sem("s_cp1")
    s_vb = sem("s_vb")
    s_pv = sem("s_pv")
    s_den = sem("s_den")
    s_spare = sem("s_spare")
    s_spare_p = sem("s_spare_p")
    s_inv = sem("s_inv")
    s_fac = sem("s_fac")
    s_o = sem("s_o")

    with nc.Block() as block:
        def load_job(sp, m, it, b):
            def rows(name, part):
                at, step, within = m.g[name]
                row = ds(it * step + (at + b * within), m.K) if step else slice(at + b * within, at + b * within + m.K)
                return qk_rows[part, row, :]

            for i in range(m.copies):
                to = slice(i * m.K, (i + 1) * m.K)
                sp.dma_start(qb[b][to, :].bitcast(F32), rows("q", i * 2 // m.copies)).then_inc(s_load[b], 16)
                if m.is_diff:
                    sp.dma_start(ka[b][to, :].bitcast(F32), rows("kk", i % 2)).then_inc(s_load[b], 16)
                elif not m.is_cmp:
                    sp.dma_start(ka[b][to, :].bitcast(F32), rows("kk", 0)).then_inc(s_load[b], 16)
                    sp.dma_start(kb[b][to, :].bitcast(F32), rows("kk", 1)).then_inc(s_load[b], 16)
            if not m.is_fox:
                sp.dma_start(neg_slope[:, b:b + 1], neg_slopes[ds(it * 2 + (m.g["job"] + b), 1), :].rearrange("a p -> p a"),
                             allow_slow_non_contiguous=True).then_inc(s_load[b], 16)
            if m.is_swa:
                sp.dma_start(sink[:, b:b + 1], swa_sinks[0:1, ds(it * 2 + b, 1)].to_broadcast([P, 1])).then_inc(s_load[b], 16)
            if m.is_fox:
                head = ds(it * 2 + b, 1)
                sp.dma_start(ck[b][0:2, :].bitcast(F32), cum_rows[head, 0:2, :].rearrange("a i t -> (a i) t")).then_inc(s_load[b], 16)
                sp.dma_start(cq[b][2:4, :].bitcast(F32), cum_rows[head, 2:4, :].rearrange("a i t -> (a i) t")).then_inc(s_load[b], 16)

        def positions(eng):
            def place(m, it, then, q):
                return (m, it, q) if 0 <= q < 16 else then + (q - 16,) if then and q >= 16 else None

            for k in range(-3, 0):
                yield lambda lead: place(mixers[0], 0, None, k + lead)
            for m, after in zip(mixers, mixers[1:] + [None]):
                with eng.Fori(0, m.rounds - 1) as it:
                    for k in range(16):
                        yield lambda lead: place(m, it, (m, it + 1), k + lead)
                for k in range(16):
                    yield lambda lead: place(m, m.rounds - 1, after and (after, 0), k + lead)

        @block.sync
        def _(sp):
            for m in mixers:
                if m.is_fox:
                    sp.wait_ge(s_ones, 5)
                with sp.Fori(0, m.rounds) as it:
                    for b in range(2):
                        at = it * 16 + (m.steps + 8 * b + 8)
                        sp.wait_ge(s_qk, at)
                        sp.wait_ge(s_max, at)
                        if m.is_swa:
                            sp.wait_ge(s_sink, at)
                        load_job(sp, m, it, b)

        @block.gpsimd
        def _(pool):
            pool.memset(nil[:, :], 0.0).then_inc(s_ones, 1)
            pool.wait_ge(s_ones, 1)
            filled = 0
            for m in mixers:
                if m.is_swa:
                    for n, t in enumerate((*cq, *ck)):
                        pool.memset(t[:, :].bitcast(F32), 1.0).then_inc(s_ones, 1)
                        pool.wait_ge(s_ones, n + 2)
                    pool.memset(zeros[:, :], 0.0).then_inc(s_ones, 1)
                    pool.wait_ge(s_ones, 6)
                    pool.dma_start(slots_in[2 * T:IN_ROWS, :], zeros[:, :]).then_inc(s_zfill, 16)
                if not m.is_diff:
                    for row in range(filled, min(filled + 7 * P, OUT_ROWS), P):
                        pool.dma_start(slots_out[row:row + P, :], zeros[:, :]).then_inc(s_zfill, 16)
                        filled += P
                with pool.Fori(0, m.rounds) as it:
                    for b in range(2):
                        if not m.is_cmp:
                            v0, vi, vj = m.g["v"]
                            cols = ds(it * vi + (v0 + b * vj), HD) if vi else slice(v0 + b * vj, v0 + b * vj + HD)
                            pool.wait_ge(s_pv, it * 16 + (m.steps + 8 * b + 8))
                            pool.tensor_tensor(pool_spare[:, b:b + 1], nil[:, :], nil[:, :], ALU.add).then_inc(s_spare_p, 1)
                            pool.tensor_tensor(vb[b][:, :, :], v_tok[:, :, cols],
                                               nil[:, :].rearrange("p (a d) -> p a d", a=1).to_broadcast([P, NT, HD]),
                                               ALU.add).then_inc(s_vb, 1)
                        if m.is_fox:
                            continue
                        dist = dists[m.name]
                        pool.wait_ge(s_load[b], it * (16 * m.loads) + (m.load_sum + 16 * m.loads))
                        pool.wait_ge(s_max, it * 16 + (m.steps + 8 * b + 8))
                        if m.is_swa:
                            pool.tensor_tensor(neg_sink[:, b:b + 1], nil[:, :], sink[:, b:b + 1], ALU.subtract).then_inc(s_nsink, 1)
                        pool.tensor_tensor(bias[:, b, 0:dist.shape[1]], dist[:, :],
                                           neg_slope[:, b:b + 1].to_broadcast([P, dist.shape[1]]), ALU.mult).then_inc(s_bias7, 1)
            assert filled == OUT_ROWS
            pool.wait_ge(s_zfill, 16 * (1 + filled // P))

        @block.tensor
        def _(pe):
            pe.sem_inc(s_qk, 16)
            pe.sem_inc(s_tr7, 4)
            pe.sem_inc(s_pv, 16)

            def scores(m, it, k):
                b, i = k // 8, k % 8
                first, _ = m.span(i)
                if i == 0:
                    pe.wait_ge(s_load[b], it * (16 * m.loads) + (m.load_sum + 16 * m.loads))
                pe.wait_ge(s_max, it * 16 + (m.steps + k + 15))
                w = m.width(i)
                for at in range(0, w, 512):
                    keys = slice(first * P + at, first * P + min(w, at + 512))
                    queries = slice(i * P, (i + 1) * P)
                    o = bank[:, 2 * (i % 2) + at // 512, 0:min(w - at, 512)]
                    if m.is_cmp:
                        mm = pe.matmul(o, qb[b][:, queries].bitcast(F32), kc_t[:, :], start=True, stop=True)
                        continue
                    mm = pe.matmul(o, qb[b][:, queries], ka[b][:, keys], start=True, stop=m.is_diff)
                    if not m.is_diff:
                        mm = pe.matmul(o, qb[b][:, queries], kb[b][:, keys], start=False, stop=not m.is_fox)
                    if m.is_fox:
                        mm = pe.matmul(o, cq[b][:, queries], ck[b][:, keys], start=False, stop=True)
                mm.then_inc(s_qk, 1)

            def turn(m, it, k):
                b, i = k // 8, k % 8
                pe.wait_ge(s_exp, it * 16 + (m.steps + k + 1))
                pe.wait_ge(s_cp0, it * 16 + (m.steps + k + 1))
                for j in range(m.blocks(i)):
                    if j == 4:
                        mm.then_inc(s_first, 1)
                        pe.wait_ge(s_cp1, it * 8 + (m.splits + 4 * b + i - 3))
                    mm = pe.transpose(bank[:, 4 + j // 4, j % 4 * P:(j % 4 + 1) * P], probs[:, k % 4, j * P:(j + 1) * P], ident[:, :])
                mm.then_inc(s_tr7, 1)

            def values(m, it, k):
                b, i = k // 8, k % 8
                first, nb = m.span(i)
                pe.wait_ge(s_cp0, it * 16 + (m.steps + k + 2))
                if m.blocks(i) > 4:
                    pe.wait_ge(s_cp1, it * 8 + (m.splits + 4 * b + i - 2))
                pe.wait_ge(s_o, it * 16 + (m.steps + k + 1))
                if m.is_cmp:
                    mm = pe.matmul(bank[:, 6 + i % 2, 0:HD], probs_t[0:NC, i % 2, 0, :], vc[:, :], start=True, stop=True)
                else:
                    if i == 0:
                        pe.wait_ge(s_vb, it * 2 + (m.value_jobs + b + 1))
                    for j in range(nb):
                        for h in range(2):
                            q = slice(h * 64, h * 64 + 64)
                            mm = pe.matmul(bank[q, 6 + i % 2, 0:HD], probs_t[:, i % 2, j, q], vb[b][:, first + j, :],
                                           start=(j == 0), stop=(j == nb - 1))
                mm.then_inc(s_pv, 1)

            for at in positions(pe):
                for stage, lead in ((scores, 3), (turn, 1), (values, 0)):
                    if at(lead):
                        stage(*at(lead))

        @block.scalar
        def _(act):
            act.sem_inc(s_cp0, 1)
            act.sem_inc(s_sink, 16 + next(m.steps for m in mixers if m.is_swa))

            def exponentials(m, it, k):
                i = k % 8
                p = probs[:, k % 4, 0:m.width(i)]
                act.wait_ge(s_max, it * 16 + (m.steps + k + 17))
                act.activation(p, p, ACT.Exp, bias=low[:, i:i + 1], scale=-1.0, accum_out=total[:, i:i + 1]).then_inc(s_exp, 1)
                if m.is_swa:
                    act.activation(sink_exp[:, i:i + 1], sink[:, k // 8:k // 8 + 1], ACT.Exp, bias=low[:, i:i + 1]).then_inc(s_sink, 1)

            def copy_first(m, it, k):
                b, i = k // 8, k % 8
                nb = m.blocks(i)
                if nb > 4:
                    act.wait_ge(s_first, it * 8 + (m.splits + 4 * b + i - 3))
                else:
                    act.wait_ge(s_tr7, it * 16 + (m.steps + k + 5))
                act.wait_ge(s_pv, it * 16 + (m.steps + k + 15))
                kw, w = (NC if m.is_cmp else P), min(nb, 4) * P
                act.copy(probs_t[0:kw, i % 2, 0:min(nb, 4), :].rearrange("p a b -> p (a b)"), bank[0:kw, 4, 0:w]).then_inc(s_cp0, 1)

            for at in positions(act):
                for stage, lead in ((exponentials, 2), (copy_first, 1)):
                    if at(lead):
                        stage(*at(lead))

        @block.vector
        def _(dve):
            dve.sem_inc(s_max, 16)
            dve.sem_inc(s_cp1, 1)
            dve.sem_inc(s_o, 2)

            def reciprocal(m, it, k):
                i = k % 8
                t_, f = total[:, i:i + 1], factor[:, i:i + 1]
                dve.wait_ge(s_exp, it * 16 + (m.steps + k + 1))
                if m.is_swa:
                    dve.wait_ge(s_sink, it * 16 + (m.steps + k + 17))
                    dve.tensor_tensor(t_, t_, sink_exp[:, i:i + 1], ALU.add).then_inc(s_den, 1)
                    dve.wait_ge(s_den, it * 16 + (k + 1))
                dve.reciprocal(f, t_).then_inc(s_inv, 1)

            def maxima(before, m, it, k):
                b, i = k // 8, k % 8
                w = m.width(i)
                dve.wait_ge(s_qk, it * 16 + (m.steps + k + 17))
                if i == 0 and not m.is_fox:
                    dve.wait_ge(s_bias7, it * 2 + (m.jobs_biased + b + 1))
                dve.wait_ge(s_tr7, it * 16 + (m.steps + k + 1))
                if m.is_cmp:
                    add = bias[:, b, 56 - 8 * i:56 - 8 * i + NC]
                elif m.is_fox:
                    add = causal[:, T - w:T]
                else:
                    end = dists[m.name].shape[1]
                    add = bias[:, b, end - w:end]
                s = bank[:, 2 * (i % 2):2 * (i % 2) + 2, :].rearrange("p a b -> p (a b)")[:, 0:w]
                if before:
                    reciprocal(*before)
                else:
                    dve.memset(spare[:, k:k + 1], 0.0).then_inc(s_spare, 1)
                dve.tensor_tensor_reduce(out=probs[:, k % 4, 0:w], in0=s, in1=add, scale=-1.0,
                                         scalar=neg_sink[:, b:b + 1] if m.is_swa else HUGE, op0=ALU.add, op1=ALU.min,
                                         accum_out=low[:, i:i + 1]).then_inc(s_max, 1)

            def copy_second(m, it, k):
                i, nb = k % 8, m.blocks(k % 8)
                if nb > 4:
                    dve.wait_ge(s_tr7, it * 16 + (m.steps + k + 5))
                    dve.wait_ge(s_pv, it * 16 + (m.steps + k + 15))
                    dve.tensor_copy(probs_t[:, i % 2, 4:nb, :].rearrange("p a b -> p (a b)"), bank[:, 5, 0:(nb - 4) * P]).then_inc(s_cp1, 1)

            def output(m, it, k):
                b, i = k // 8, k % 8
                f = factor[:, i:i + 1]
                dve.wait_ge(s_inv, it * 16 + (m.steps + k + 1))
                if m.is_diff and b == 1:
                    dve.tensor_tensor(f, f, neg_lam[:, :], ALU.mult).then_inc(s_fac, 1)
                    dve.wait_ge(s_fac, it * 8 + (m.factors + i + 1))
                if "gate" in m.g:
                    gate = nsa_gate[:, i, ds(it * 6 + (3 * b + m.g["gate"]), 1)]
                    if m.is_cmp and i == 0:
                        dve.scalar_tensor_tensor(out=f, in0=f, scalar=gate, in1=row_seen[:, :], op0=ALU.mult, op1=ALU.mult).then_inc(s_fac, 1)
                    else:
                        dve.tensor_tensor(f, f, gate, ALU.mult).then_inc(s_fac, 1)
                    dve.wait_ge(s_fac, it * 16 + (m.factors + k + 1))
                dve.wait_ge(s_pv, it * 16 + (m.steps + k + 17))
                o = bank[:, 6 + i % 2, 0:HD]
                y0, yi, yj = m.g["y"]
                yo = y[:, i, ds(it * yi + (y0 + b * yj), HD)]
                if m.is_diff and b == 0:
                    dve.tensor_scalar(first_map[:, i, :], o, f, None, ALU.mult).then_inc(s_o, 1)
                elif m.is_diff:
                    dve.wait_ge(s_o, it * 16 + (m.steps + k - 5))
                    dve.scalar_tensor_tensor(out=yo, in0=o, scalar=f, in1=first_map[:, i, :], op0=ALU.mult, op1=ALU.add).then_inc(s_o, 1)
                elif m.name in ("sel", "win"):
                    dve.wait_ge(s_o, it * 16 + (m.steps + k - 29))
                    dve.scalar_tensor_tensor(out=yo, in0=o, scalar=f, in1=yo, op0=ALU.mult, op1=ALU.add).then_inc(s_o, 1)
                else:
                    dve.tensor_scalar(yo, o, f, None, ALU.mult).then_inc(s_o, 1)

            for at in positions(dve):
                if at(3):
                    maxima(at(1), *at(3))
                elif at(1):
                    reciprocal(*at(1))
                for stage, lead in ((copy_second, 1), (output, 0)):
                    if at(lead):
                        stage(*at(lead))


_INS = ['x', 'c', 'ada_w', 'ada_b', 'norm_attn_g', 'norm_moe_g', 'norm_final_g', 'w_in', 'w_out', 'diff_lam_q1',
        'diff_lam_k1', 'diff_lam_q2', 'diff_lam_k2', 'diff_subln_g', 'swa_sinks', 'fox_forget_b', 'nsa_cmp_pos',
        'nsa_cmp_w1', 'nsa_cmp_b1', 'nsa_cmp_w2', 'router_w', 'router_b', 'exp_w_gate', 'exp_w_up', 'exp_w_down']


def kernel(**inputs):
    import numpy as np
    import concourse.bacc as bacc
    from concourse.bass_utils import run_bass_kernel_spmd

    nc = bacc.Bacc("TRN2", target_bir_lowering=False, num_devices=1)
    arrays, args = {}, {}
    for name in _INS:
        a = np.ascontiguousarray(inputs[name])
        arrays[f"in_{name}"] = a
        args[name] = nc.dram_tensor(f"in_{name}", a.shape, F32, kind="ExternalInput").ap()
    arrays["in_neg_slopes"] = np.repeat(np.array(NEG_SLOPES, np.float32)[:, None], P, axis=1)
    args["neg_slopes"] = nc.dram_tensor("in_neg_slopes", (NJOBS, P), F32, kind="ExternalInput").ap()
    out = nc.dram_tensor("out", (1, T, D), F32, kind="ExternalOutput").ap()
    build(nc, **args, out=out)
    r = run_bass_kernel_spmd(nc, [arrays], core_ids=[0])
    return r.results[0]["out"]
```
